# Optimizing a Trainium2 kernel written in Bass

```python
import jax
import jax.numpy as jnp
from jax import lax
import numpy as np
import jax, jax.numpy as jnp

D_MODEL = 1024
BATCH = 1
SEQ = 1024
DEPTH = 1

RW_HEAD_DIM = 64
RW_WIDTH = D_MODEL // 2
RW_HEADS = RW_WIDTH // RW_HEAD_DIM
RW_DECAY_RANK = 64
RW_ICLR_RANK = 64
RW_GATE_RANK = 128
RW_GN_EPS = 64e-5
RET_QK_DIM = 64
RET_QK_WIDTH = D_MODEL // 2
RET_HEADS = RET_QK_WIDTH // RET_QK_DIM
RET_V_DIM = 2 * RET_QK_DIM
RET_V_WIDTH = RET_HEADS * RET_V_DIM
RET_CHUNK = 128
ROPE_BASE = 10000.0
RET_GN_EPS = 1e-5
D_FF = 2816
CONV_WIDTH = 3
RMS_EPS = 1e-6

RW_SIZES = (RW_WIDTH, RW_WIDTH, RW_WIDTH, RW_DECAY_RANK, RW_ICLR_RANK, RW_GATE_RANK)
RET_SIZES = (RET_QK_WIDTH, RET_QK_WIDTH, RET_V_WIDTH, RET_V_WIDTH)
RW_COLS = sum(RW_SIZES)
RET_COLS = sum(RET_SIZES)
IN_SIZES = (RW_COLS, RET_COLS, D_MODEL, D_MODEL)
IN_COLS = sum(IN_SIZES)


def _split(z, sizes):
    return jnp.split(z, [int(s) for s in np.cumsum(sizes)[:-1]], axis=-1)

def rms_norm(x, g):
    xf = x.astype(jnp.float32)
    y = xf * lax.rsqrt(jnp.mean(xf * xf, axis=-1, keepdims=True) + RMS_EPS)
    return (y * g.astype(jnp.float32)).astype(x.dtype)

def group_norm_heads(z, eps):
    mu = jnp.mean(z, axis=-1, keepdims=True)
    var = jnp.mean(jnp.square(z - mu), axis=-1, keepdims=True)
    return (z - mu) * lax.rsqrt(var + eps)

def token_shift(p):
    return jnp.pad(p, ((0, 0), (1, 0), (0, 0)))[:, :-1]

def rwkv7_mixer(p, mu, w0, w2, a0, a2, g2, k_k, k_a, r_k, lnx_w, lnx_b):
    B, T, _ = p.shape
    H, N = RW_HEADS, RW_HEAD_DIM
    p = p.astype(jnp.float32)
    p = p + (token_shift(p) - p) * mu.astype(jnp.float32)
    r, k, v, wd, ad, gd = _split(p, RW_SIZES)
    w = -jax.nn.softplus(-(w0 + jnp.tanh(wd) @ w2)) - 0.5
    decay = jnp.exp(-jnp.exp(w))
    a = jax.nn.sigmoid(a0 + ad @ a2)
    g = jax.nn.sigmoid(gd) @ g2
    heads = lambda z: z.reshape(B, T, H, N).astype(jnp.float32)
    kk = heads(k * k_k)
    kk = kk / jnp.maximum(jnp.sqrt(jnp.sum(kk * kk, axis=-1, keepdims=True)), 1e-12)
    k = k * (1.0 + (a - 1.0) * k_a)
    r, k, v, decay, a = heads(r), heads(k), heads(v), heads(decay), heads(a)

    def step(S, inp):
        r_t, k_t, v_t, w_t, kk_t, a_t = inp
        sa = jnp.einsum('bhvk,bhk->bhv', S, -kk_t)
        S = (S * w_t[:, :, None, :]
             + sa[..., None] * (kk_t * a_t)[:, :, None, :]
             + v_t[..., None] * k_t[:, :, None, :])
        y = jnp.einsum('bhvk,bhk->bhv', S, r_t)
        return S, y

    xs = tuple(jnp.moveaxis(z, 1, 0) for z in (r, k, v, decay, kk, a))
    S0 = jnp.zeros((B, H, N, N), jnp.float32)
    _, y = lax.scan(step, S0, xs)
    y = jnp.moveaxis(y, 0, 1)
    y = group_norm_heads(y, RW_GN_EPS) * lnx_w.reshape(H, N) + lnx_b.reshape(H, N)
    bonus = jnp.sum(r * k * r_k.reshape(H, N), axis=-1, keepdims=True) * v
    return (y + bonus).reshape(B, T, RW_WIDTH) * g

def rotary(z, pos):
    half = z.shape[-1] // 2
    inv = ROPE_BASE ** (-jnp.arange(half, dtype=jnp.float32) / half)
    ang = pos.astype(jnp.float32)[..., None] * inv
    cos = jnp.cos(ang)[:, :, None, :]
    sin = jnp.sin(ang)[:, :, None, :]
    z1, z2 = z[..., :half], z[..., half:]
    return jnp.concatenate([z1 * cos - z2 * sin, z1 * sin + z2 * cos], axis=-1)

def retention_mixer(p, positions):
    B, T, _ = p.shape
    H, dk, dv, C = RET_HEADS, RET_QK_DIM, RET_V_DIM, RET_CHUNK
    q, k, v, g = _split(p.astype(jnp.float32), RET_SIZES)
    q = rotary(q.reshape(B, T, H, dk), positions)
    k = rotary(k.reshape(B, T, H, dk), positions) * (dk ** -0.5)
    v = v.reshape(B, T, H, dv)
    log_gamma = jnp.log1p(-jnp.exp2(-5.0 - jnp.arange(H, dtype=jnp.float32)))
    idx = jnp.arange(C, dtype=jnp.float32)
    rel = idx[:, None] - idx[None, :]
    decay_mask = jnp.where(rel[None] >= 0,
                           jnp.exp(jnp.maximum(rel, 0.0)[None] * log_gamma[:, None, None]), 0.0)
    q_decay = jnp.exp((idx + 1.0)[:, None] * log_gamma[None, :])[None, :, :, None]
    k_decay = jnp.exp((C - 1.0 - idx)[:, None] * log_gamma[None, :])[None, :, :, None]
    chunk_decay = jnp.exp(C * log_gamma)[None, :, None, None]
    n_chunks = T // C
    chunks = lambda z: jnp.moveaxis(z.reshape(B, n_chunks, C, H, z.shape[-1]), 1, 0)

    def step(R, inp):
        qc, kc, vc = inp
        s = jnp.einsum('bihd,bjhd->bhij', qc, kc) * decay_mask
        inner = jnp.einsum('bhij,bjhe->bihe', s, vc)
        cross = jnp.einsum('bihd,bhde->bihe', qc * q_decay, R)
        R = R * chunk_decay + jnp.einsum('bjhd,bjhe->bhde', kc * k_decay, vc)
        return R, inner + cross

    R0 = jnp.zeros((B, H, dk, dv), jnp.float32)
    _, o = lax.scan(step, R0, (chunks(q), chunks(k), chunks(v)))
    o = jnp.moveaxis(o, 0, 1).reshape(B, T, H, dv)
    o = group_norm_heads(o, RET_GN_EPS).reshape(B, T, RET_V_WIDTH)
    return jax.nn.silu(g) * o

def conv_ffn(h, w_up, conv_w, conv_b, w_down):
    u = h @ w_up
    T = u.shape[1]
    up = jnp.pad(u, ((0, 0), (CONV_WIDTH - 1, 0), (0, 0)))
    u = sum(up[:, i:i + T] * conv_w[i] for i in range(CONV_WIDTH)) + conv_b
    gate, val = jnp.split(u, 2, axis=-1)
    return (jax.nn.gelu(gate, approximate=True) * val) @ w_down

def first_inputs(seed: int = 0) -> dict:
    key = jax.random.key(seed)
    ks = jax.random.split(key, 26)
    f32 = jnp.float32
    L = DEPTH
    nrm = lambda k, shape, s: s * jax.random.normal(k, shape, f32)
    x = jax.random.normal(ks[0], (BATCH, SEQ, D_MODEL), f32)
    offsets = jax.random.randint(ks[1], (BATCH, 1), 0, 4096, dtype=jnp.int32)
    positions = offsets + jnp.arange(SEQ, dtype=jnp.int32)[None, :]
    return {
        "x": x,
        "positions": positions,
        "norm_mix_pre": 1.0 + nrm(ks[2], (L, D_MODEL), 0.1),
        "norm_mix_post": 1.0 + nrm(ks[3], (L, D_MODEL), 0.1),
        "norm_ffn_pre": 1.0 + nrm(ks[4], (L, D_MODEL), 0.1),
        "norm_ffn_post": 1.0 + nrm(ks[5], (L, D_MODEL), 0.1),
        "w_in": nrm(ks[6], (L, D_MODEL, IN_COLS), D_MODEL ** -0.5),
        "rw_mu": jax.random.uniform(ks[7], (L, RW_COLS), f32, 0.0, 1.0),
        "rw_w0": jax.random.uniform(ks[8], (L, RW_WIDTH), f32, -6.0, 1.0),
        "rw_w2": nrm(ks[9], (L, RW_DECAY_RANK, RW_WIDTH), 0.1 * RW_DECAY_RANK ** -0.5),
        "rw_a0": nrm(ks[10], (L, RW_WIDTH), 0.1),
        "rw_a2": nrm(ks[11], (L, RW_ICLR_RANK, RW_WIDTH), 0.5 * RW_ICLR_RANK ** -0.5),
        "rw_g2": nrm(ks[12], (L, RW_GATE_RANK, RW_WIDTH), RW_GATE_RANK ** -0.5),
        "rw_k_k": 0.85 + nrm(ks[13], (L, RW_WIDTH), 0.1),
        "rw_k_a": 1.0 + nrm(ks[14], (L, RW_WIDTH), 0.1),
        "rw_r_k": nrm(ks[15], (L, RW_WIDTH), 0.1),
        "rw_lnx_w": 1.0 + nrm(ks[16], (L, RW_WIDTH), 0.1),
        "rw_lnx_b": nrm(ks[17], (L, RW_WIDTH), 0.01),
        "w_branch_rw": nrm(ks[18], (L, RW_WIDTH, D_MODEL), RW_WIDTH ** -0.5),
        "w_branch_ret": nrm(ks[19], (L, RET_V_WIDTH, D_MODEL), RET_V_WIDTH ** -0.5),
        "w_out": nrm(ks[20], (L, D_MODEL, D_MODEL), D_MODEL ** -0.5),
        "ffn_w_up": nrm(ks[21], (L, D_MODEL, 2 * D_FF), D_MODEL ** -0.5),
        "ffn_conv_w": nrm(ks[22], (L, CONV_WIDTH, 2 * D_FF), CONV_WIDTH ** -0.5),
        "ffn_conv_b": nrm(ks[23], (L, 2 * D_FF), 0.01),
        "ffn_w_down": nrm(ks[24], (L, D_FF, D_MODEL), D_FF ** -0.5),
    }

def first_block(x, positions, norm_mix_pre, norm_mix_post, norm_ffn_pre, norm_ffn_post, w_in,
              rw_mu, rw_w0, rw_w2, rw_a0, rw_a2, rw_g2, rw_k_k, rw_k_a, rw_r_k, rw_lnx_w, rw_lnx_b,
              w_branch_rw, w_branch_ret, w_out, ffn_w_up, ffn_conv_w, ffn_conv_b, ffn_w_down):
    h = x
    for l in range(DEPTH):
        hn = rms_norm(h, norm_mix_pre[l])
        p = hn @ w_in[l]
        p_rw, p_ret, g_rw, g_ret = _split(p, IN_SIZES)
        y_rw = rwkv7_mixer(p_rw, rw_mu[l], rw_w0[l], rw_w2[l], rw_a0[l], rw_a2[l], rw_g2[l],
                           rw_k_k[l], rw_k_a[l], rw_r_k[l], rw_lnx_w[l], rw_lnx_b[l])
        y_ret = retention_mixer(p_ret, positions)
        merged = (jax.nn.sigmoid(g_rw.astype(jnp.float32)) * (y_rw @ w_branch_rw[l])
                  + jax.nn.sigmoid(g_ret.astype(jnp.float32)) * (y_ret @ w_branch_ret[l]))
        h = h + rms_norm(merged @ w_out[l], norm_mix_post[l])
        f = conv_ffn(rms_norm(h, norm_ffn_pre[l]), ffn_w_up[l], ffn_conv_w[l], ffn_conv_b[l], ffn_w_down[l])
        h = h + rms_norm(f, norm_ffn_post[l])
    return h.astype(x.dtype)


D_MIX = D_MODEL
D_POOL = D_MIX // 2
POOL_WINDOWS = (2, 4, 8, 16)
N_POOL_GROUPS = len(POOL_WINDOWS)
POOL_GROUP = D_POOL // N_POOL_GROUPS
HEAD_DIM = 64
D_ATTN = D_MIX - D_POOL
N_HEADS = D_ATTN // HEAD_DIM
N_KV_HEADS = 2
GQA_GROUP = N_HEADS // N_KV_HEADS
D_KV = N_KV_HEADS * HEAD_DIM
WINDOW = 128
BLOCK = 128
IN_WIDTHS = (D_POOL, D_POOL, D_ATTN, D_KV, D_KV, D_ATTN)
D_IN = sum(IN_WIDTHS)
EPS = 1e-6
NEG_INF = -1e30


def rmsnorm(x, gain):
    x32 = x.astype(jnp.float32)
    y = x32 * lax.rsqrt(jnp.mean(x32 * x32, axis=-1, keepdims=True) + EPS) * gain.astype(jnp.float32)
    return y.astype(x.dtype)

def alibi_slopes():
    return jnp.exp2(-8.0 * jnp.arange(1, N_HEADS + 1, dtype=jnp.float32) / N_HEADS)

def pool_mixer(u, w_grp, scale):
    B, S, _ = u.shape
    u32 = u.astype(jnp.float32).reshape(B, S, N_POOL_GROUPS, POOL_GROUP)
    csum = jnp.cumsum(u32, axis=1)
    csum = jnp.concatenate([jnp.zeros_like(csum[:, :1]), csum], axis=1)
    pos = jnp.arange(1, S + 1, dtype=jnp.float32)
    means = []
    for g, w in enumerate(POOL_WINDOWS):
        c = csum[:, :, g]
        lo = jnp.concatenate([jnp.zeros_like(c[:, :w - 1]), c[:, :S + 1 - w]], axis=1)
        count = jnp.minimum(pos, float(w))[None, :, None]
        means.append((c[:, 1:] - lo) / count)
    pooled = jnp.stack(means, axis=2) - u32
    mixed = jnp.einsum('bsgc,gcd->bsgd', pooled.astype(u.dtype), w_grp)
    return mixed.reshape(B, S, D_POOL) * scale

def swa_sink_attention(q, k, v, sinks):
    B, S, _ = q.shape
    NB = S // BLOCK
    q = q.reshape(B, NB, BLOCK, N_KV_HEADS, GQA_GROUP, HEAD_DIM)
    k = k.reshape(B, NB, BLOCK, N_KV_HEADS, HEAD_DIM)
    v = v.reshape(B, NB, BLOCK, N_KV_HEADS, HEAD_DIM)

    def with_prev(t):
        prev = jnp.concatenate([jnp.zeros_like(t[:, :1]), t[:, :-1]], axis=1)
        return jnp.concatenate([prev, t], axis=2)

    kb, vb = with_prev(k), with_prev(v)
    scores = jnp.einsum('bnqhgd,bnkhd->bnhgqk', q, kb).astype(jnp.float32) * (HEAD_DIM ** -0.5)
    qi = jnp.arange(BLOCK)[:, None]
    kj = jnp.arange(2 * BLOCK)[None, :]
    dist = qi + BLOCK - kj
    in_win = (dist >= 0) & (dist < WINDOW)
    key_exists = (jnp.arange(NB)[:, None, None] > 0) | (kj >= BLOCK)[None]
    valid = in_win[None] & key_exists
    slopes = alibi_slopes().reshape(N_KV_HEADS, GQA_GROUP)
    bias = -slopes[:, :, None, None] * dist.astype(jnp.float32)
    scores = jnp.where(valid[None, :, None, None], scores + bias, NEG_INF)
    sink = jnp.broadcast_to(sinks.astype(jnp.float32).reshape(N_KV_HEADS, GQA_GROUP, 1, 1),
                            scores.shape[:-1] + (1,))
    probs = jax.nn.softmax(jnp.concatenate([scores, sink], axis=-1), axis=-1)[..., :-1]
    out = jnp.einsum('bnhgqk,bnkhd->bnqhgd', probs.astype(v.dtype), vb)
    return out.reshape(B, S, D_ATTN)

def second_inputs(seed: int = 0) -> dict:
    key = jax.random.key(seed)
    ks = jax.random.split(key, 9)
    x = jax.random.normal(ks[0], (BATCH, SEQ, D_MODEL), jnp.float32)
    w_in = jax.random.normal(ks[1], (DEPTH, D_MODEL, D_IN), jnp.float32) * D_MODEL ** -0.5
    pool_w = jax.random.normal(ks[2], (DEPTH, N_POOL_GROUPS, POOL_GROUP, POOL_GROUP), jnp.float32) * POOL_GROUP ** -0.5
    pool_scale = 1.0 + 0.1 * jax.random.normal(ks[3], (DEPTH, D_POOL), jnp.float32)
    attn_sinks = 0.5 * jax.random.normal(ks[4], (DEPTH, N_HEADS), jnp.float32)
    w_out = jax.random.normal(ks[5], (DEPTH, D_MIX, D_MODEL), jnp.float32) * D_MIX ** -0.5
    norm_pre = 1.0 + 0.1 * jax.random.normal(ks[6], (DEPTH, D_MODEL), jnp.float32)
    norm_post = 1.0 + 0.1 * jax.random.normal(ks[7], (DEPTH, D_MODEL), jnp.float32)
    return {"x": x, "w_in": w_in, "pool_w": pool_w, "pool_scale": pool_scale,
            "attn_sinks": attn_sinks, "w_out": w_out, "norm_pre": norm_pre, "norm_post": norm_post}

def second_block(x, w_in, pool_w, pool_scale, attn_sinks, w_out, norm_pre, norm_post):
    splits = [int(s) for s in np.cumsum(IN_WIDTHS)[:-1]]
    for layer in range(DEPTH):
        h = rmsnorm(x, norm_pre[layer])
        proj = h @ w_in[layer]
        pool_u, pool_gate, q, k, v, attn_gate = jnp.split(proj, splits, axis=-1)
        pool_out = pool_mixer(pool_u, pool_w[layer], pool_scale[layer]) * jax.nn.silu(pool_gate)
        attn_out = swa_sink_attention(q, k, v, attn_sinks[layer]) * jax.nn.silu(attn_gate)
        y = jnp.concatenate([pool_out, attn_out], axis=-1) @ w_out[layer]
        x = x + rmsnorm(y, norm_post[layer])
    return x


def setup_inputs(seed=0):
    out = dict(first_inputs(seed))
    for name, value in second_inputs(seed + 1).items():
        if name != "x":
            out[name + "_2"] = value
    return out


def reference(
    x, positions, norm_mix_pre, norm_mix_post, norm_ffn_pre, norm_ffn_post, w_in, rw_mu, rw_w0,
    rw_w2, rw_a0, rw_a2, rw_g2, rw_k_k, rw_k_a, rw_r_k, rw_lnx_w, rw_lnx_b, w_branch_rw,
    w_branch_ret, w_out, ffn_w_up, ffn_conv_w, ffn_conv_b, ffn_w_down, w_in_2, pool_w_2,
    pool_scale_2, attn_sinks_2, w_out_2, norm_pre_2, norm_post_2,
):
    x = first_block(
        x, positions, norm_mix_pre, norm_mix_post, norm_ffn_pre, norm_ffn_post, w_in, rw_mu,
        rw_w0, rw_w2, rw_a0, rw_a2, rw_g2, rw_k_k, rw_k_a, rw_r_k, rw_lnx_w, rw_lnx_b,
        w_branch_rw, w_branch_ret, w_out, ffn_w_up, ffn_conv_w, ffn_conv_b, ffn_w_down,
    )
    return second_block(
        x, w_in_2, pool_w_2, pool_scale_2, attn_sinks_2, w_out_2, norm_pre_2, norm_post_2,
    )


_drawn_inputs = setup_inputs


def setup_inputs(seed=0):
    import zlib

    import numpy as np

    out = dict(_drawn_inputs(seed))
    spreads = {}
    factors = {'rw_w2': 8.0, 'rw_lnx_b': 8.0, 'ffn_conv_b': 6.138, 'attn_sinks_2': 8.0}
    for name, (base, spread) in spreads.items():
        noise = np.random.default_rng([zlib.crc32(name.encode()), seed]).standard_normal(out[name].shape)
        drawn = base * np.exp(spread * noise) if base else spread * noise
        out[name] = jnp.asarray(drawn.astype(out[name].dtype))
    for name, factor in factors.items():
        out[name] = (out[name] * factor).astype(out[name].dtype)
    return out
```

```python
from contextlib import ExitStack

import numpy as np

import concourse.bass as bass
from concourse import mybir

F32 = mybir.dt.float32
F32R = mybir.dt.float32r
I32 = mybir.dt.int32
ALU = mybir.AluOpType
ACT = mybir.ActivationFunctionType
AX_X = mybir.AxisListType.X

P = 128
T = 1024
HALF = 512
D = 1024
KT = D // P
FF = 2816
FT = FF // P
PAIRS = 4
CH = 64
GROUPS = 4
LEVELS = 6
NB = T // P
C0 = float(np.exp(-0.5))
TWO_PI_A = 6.28125
TWO_PI_B = float(np.float32(2 * np.pi - 6.28125))
TWO_PI_C = float(2 * np.pi - 6.28125 - np.float32(2 * np.pi - 6.28125))
MAGIC = float(1.5 * 2 ** 23)
NEG = -1e30

COLS = {}
_n = 0
for _name, _w in (("g_mix_pre", 8), ("g_mix_post", 8), ("g_ffn_pre", 8), ("g_ffn_post", 8), ("g2_pre", 8),
                  ("g2_post", 8), ("mu_low", 2), ("rw", 40), ("conv", 176), ("pscale", 4), ("sinks", 8),
                  ("cdecay", 4), ("invf", 1), ("sgn", 1), ("counts", 60)):
    COLS[_name] = _n
    _n += _w
NPAR = _n

NORM = {n: i for i, n in enumerate(("a", "out", "pre", "down", "h2", "fin"))}
SPLIT = {n: i for i, n in enumerate(("x", "pre", "h2"))}

M_ID, M_ONES, M_BLK, M_STRICT, M_INCL, M_LOW0T, M_LVL = 0, 1, 2, 3, 4, 5, 6
NMAT = M_LVL + LEVELS

B_LORA, T_LORA = 0, 0
B_RW, T_RW = 2, 2
B_BRW, T_BRW = B_RW + 4 * PAIRS, T_RW + 6 * PAIRS
B_RET, T_RET = B_BRW + 16, T_BRW + 16
B_MRG, T_MRG = B_RET + 6 * PAIRS, T_RET + 6 * PAIRS
B_OUT, T_OUT = B_MRG + 16, T_MRG + 16
B_UP, T_UP = B_OUT + 8, T_OUT + 8
B_DOWN = B_UP + 2 * FT
B_P2, T_P2 = B_DOWN + 2 * FT, T_UP + 2 * FT
B_O2, T_O2 = B_P2 + 18, T_P2 + 18
NBLK = B_O2 + 8
NSTORED = NBLK - FT


def build(nc, xt, pos, w, par, mats, ret_tab, att_bias, pool_w, out):
    mrw_d = nc.dram_tensor("mrw_scratch", [P, KT, T], F32).ap()
    h_d = nc.dram_tensor("h_scratch", [P, KT, T], F32).ap()

    with ExitStack() as ctx:
        base = [((nc.sbuf_base + 31) // 32) * 32]

        def at(name, offset, shape, dt=F32):
            return nc.alloc_sbuf_tensor_at(name, shape, dt, offset=offset)

        def sb(name, shape, dt=F32):
            size = 4 * int(np.prod(shape[1:]))
            t = at(name, base[0], shape, dt)
            base[0] += (size + 31) // 32 * 32
            return t

        wraw = sb("wraw", [P, 2, 1024])
        whi = sb("whi", [P, 2, 1024], F32R)
        wlo = sb("wlo", [P, 2, 1024], F32R)
        mat = sb("mat", [P, NMAT, P])
        prm = sb("prm", [P, NPAR])
        pp = sb("pp", [P, 14])
        cp = sb("cp", [P, 8])
        ec = sb("ec", [P, 16])
        id2 = sb("id2", [P, CH])
        sm = sb("sm", [P, 24])
        x_at = base[0]
        xhi = sb("xhi", [P, KT, T], F32R)
        xlo = sb("xlo", [P, KT, T], F32R)
        arena = base[0]
        assert arena + 28 * 4096 <= nc.sbuf_usable_end, (arena + 28 * 4096, nc.sbuf_usable_end)

        def tiles(name, i, shape, dt=F32):
            return at(name, arena + 4096 * i, shape, dt)

        def m(i):
            return mat[:, i, :]

        def many(i, n):
            return m(i).unsqueeze(1).broadcast_to([P, n, P])

        def par_col(name, j=0):
            c = COLS[name] + j
            return prm[:, c:c + 1]

        psg = [ctx.enter_context(nc.psum_tensor(f"psg{b}", [P, T], F32)) for b in range(2)]
        psa = ctx.enter_context(nc.psum_tensor("psa", [P, 2, HALF], F32))
        psb = ctx.enter_context(nc.psum_tensor("psb", [P, 2, HALF], F32))
        bank = [psa[:, 0, :], psa[:, 1, :], psb[:, 0, :], psb[:, 1, :]]

        def flat(ps):
            return ps[:].rearrange("p a b -> p (a b)")

        sems = {}

        def sem(name):
            if name not in sems:
                sems[name] = ctx.enter_context(nc.semaphore(name))
            return sems[name]

        w_landed = [sem("w_landed0"), sem("w_landed1")]
        w_ready = sem("w_ready")
        w_used = sem("w_used")
        g_full = sem("g_full")
        g_free = [sem("g_free0"), sem("g_free1")]
        go = sem("go")
        consts_in = sem("consts_in")
        x_in = sem("x_in")

        xres = tiles("xres", 0, [P, KT, T])
        pa_sq = tiles("pa_sq", 8, [P, 2, T])
        pa_acc = tiles("pa_acc", 10, [P, T])
        pa_rstd = tiles("pa_rstd", 11, [P, T])
        pa_tmp = tiles("pa_tmp", 12, [P, 2, T])

        yrw = tiles("yrw", 0, [P, PAIRS, T])
        ta_hi, ta_lo = tiles("ta_hi", 4, [P, T], F32R), tiles("ta_lo", 5, [P, T], F32R)
        sg_hi, sg_lo = tiles("sg_hi", 6, [P, T], F32R), tiles("sg_lo", 7, [P, T], F32R)
        R, K, V, KK, SG, A, CS, E1, EN, G, BON = (
            tiles(f"rw_{n}", 8 + i, [P, T]) for i, n in enumerate("R K V KK SG A CS E1 EN G BON".split()))
        KR = tiles("rw_KR", 19, [P, NB, 2, P])
        TM = tiles("rw_TM", 21, [P, T])
        SC = tiles("rw_SC", 22, [P, 4, 768])
        s_at = arena + 25 * 4096
        VT = at("rw_VT", s_at, [P, 4, CH])
        Z = at("rw_Z", s_at + 1024, [P, 4, P])
        GH = at("rw_GH", s_at + 3072, [P, 4, P])
        XM = at("rw_XM", s_at + 5120, [P, 4, P])
        M = at("rw_M", s_at + 7168, [P, 4, P])
        MT = at("rw_MT", s_at + 9216, [P, 4, P])
        e_at = arena + 15 * 4096
        RT = at("rw_RT", e_at, [P, 2, P])
        PT = at("rw_PT", e_at + 1024, [P, 2, P])
        ST = at("rw_ST", e_at + 2048, [P, 2, CH])
        YB = EN
        DG = R
        BE, KE = A, CS

        yrw_hi, yrw_lo = tiles("yrw_hi", 4, [P, PAIRS, T], F32R), tiles("yrw_lo", 8, [P, PAIRS, T], F32R)
        br_sig, br_out = tiles("br_sig", 12, [P, 2, T]), tiles("br_out", 14, [P, 2, T])

        yret = tiles("yret", 0, [P, KT, T])
        cos_t, sin_t = tiles("cos_t", 8, [P, T]), tiles("sin_t", 9, [P, T])
        rq_raw, rq_swp, rq_c = (tiles(n, 10 + i, [P, T]) for i, n in enumerate(("rq_raw", "rq_swp", "rq_c")))
        RQ, RK, RQD, RKD = (tiles(n, 13 + i, [P, T]) for i, n in enumerate(("RQ", "RK", "RQD", "RKD")))
        RV = tiles("RV", 17, [P, T])
        RVT = tiles("RVT", 18, [P, 2, NB, P])
        RKT = tiles("RKT", 20, [P, NB, P])
        RG = tiles("RG", 21, [P, 2, T])
        RS = tiles("RS", 23, [P, NB, P])
        RP = tiles("RP", 24, [P, NB, P])
        RD, RE = tiles("RD", 25, [P, T]), tiles("RE", 26, [P, T])
        RTAB = tiles("RTAB", 27, [P, 4, P])
        ang, kq = tiles("ang", 10, [P, T]), tiles("kq", 11, [P, T])
        posi = tiles("posi", 12, [P, T], I32)

        yret_hi, yret_lo = tiles("yret_hi", 8, [P, KT, T], F32R), tiles("yret_lo", 16, [P, KT, T], F32R)
        mg_in, mg_sig, mg_b = tiles("mg_in", 24, [P, 2, T]), tiles("mg_sig", 26, [P, T]), tiles("mg_b", 27, [P, T])
        merged = tiles("merged", 0, [P, KT, T])

        oy = tiles("oy", 8, [P, KT, T])
        osq = tiles("osq", 16, [P, 2, T])
        oacc, orstd = tiles("oacc", 18, [P, T]), tiles("orstd", 19, [P, T])
        oh = tiles("oh", 20, [P, KT, T])
        otmp = tiles("otmp", 0, [P, 2, T])

        ff = tiles("ff", 0, [P, FT, T])
        fg, fv = tiles("fg", 22, [P, 2, T]), tiles("fv", 24, [P, 2, T])
        dy = at("dy", x_at, [P, KT, T])
        dh = at("dh", x_at + 32768, [P, KT, T])
        fhi, flo = tiles("fhi", 22, [P, 2, HALF], F32R), tiles("flo", 23, [P, 2, HALF], F32R)
        dsq = tiles("dsq", 24, [P, 2, HALF])
        dacc, drstd = tiles("dacc", 25, [P, T]), tiles("drstd", 26, [P, T])
        h2 = tiles("h2", 0, [P, KT, T])
        dtmp = tiles("dtmp", 8, [P, 2, T])

        cat = tiles("cat", 8, [P, KT, T])
        pu, ps2 = tiles("pu", 16, [P, T]), tiles("ps2", 17, [P, T])
        ps4, pgt = tiles("ps4", 18, [P, T]), tiles("pgt", 19, [P, T])
        pw = tiles("pw", 20, [P, P])
        kd = tiles("kd", 16, [P, 2, T + P])
        vt2 = at("vt2", arena + 16 * 4096 + 9216, [P, NB + 1, P])
        ab = tiles("ab", 20, [P, 2, 2, 2 * P])
        aq, ag = tiles("aq", 21, [P, T]), tiles("ag", 22, [P, T])
        kv_f = tiles("kv_f", 21, [P, T])
        ap_ = tiles("ap_", 23, [P, 4, 2 * P])
        apt = tiles("apt", 24, [P, 4, 2, P])
        y2 = tiles("y2", 16, [P, KT, T])
        q2sq = tiles("q2sq", 24, [P, 2, T])
        q2acc, q2rstd = tiles("q2acc", 26, [P, T]), tiles("q2rstd", 27, [P, T])

        block = ctx.enter_context(nc.Block())

        @block.sync
        def _(sp):
            def stream(first, end, shift):
                with sp.Fori(first // 2, end // 2) as i:
                    for u in range(2):
                        sp.wait_ge(w_ready, 2 * i + u + 1)
                        sp.dma_start(wraw[:, u, :], w[bass.ds(2 * i + u - shift, 1)].rearrange("n p c -> p (n c)")
                                     ).then_inc(w_landed[u], 16)

            stream(0, B_DOWN + FT, 0)
            stream(B_DOWN + FT, NBLK, FT)

        @block.gpsimd
        def _(pool):
            pool.sem_inc(w_ready, 2)
            with pool.Fori(0, NBLK // 2) as i:
                for u in range(2):
                    pool.wait_ge(w_landed[u], 16 * i + 16)
                    pool.wait_ge(w_used, 2 * i + u + 1)
                    pool.sem_inc(go, 1)
                    pool.tensor_copy(whi[:, u, :], wraw[:, u, :])
                    pool.drain()
                    pool.tensor_tensor(wlo[:, u, :], wraw[:, u, :], whi[:, u, :].bitcast(F32),
                                       ALU.subtract).then_inc(w_ready, 1)

        @block.tensor
        def _(pe):
            pe.sem_inc(w_used, 1)

            def product(n, t, slot, b, use, rhs_hi, rhs_lo, kts=KT, col=0, first=True):
                pe.wait_ge(w_ready, n + 3)
                pe.wait_ge(g_free[b], use + 1)
                for half in range(2):
                    cols = slice(half * HALF, (half + 1) * HALF)
                    for k in range(kts):
                        w_cols = slice(col + k * P, col + (k + 1) * P)
                        mm = pe.matmul(psg[b][:, cols], whi[:, slot, w_cols], rhs_hi(k, cols),
                                       start=(k == 0), stop=False)
                        if first and half == 0 and k == 0:
                            mm.then_inc(w_used, 1)
                        pe.matmul(psg[b][:, cols], whi[:, slot, w_cols], rhs_lo(k, cols), start=False, stop=False)
                        mm = pe.matmul(psg[b][:, cols], wlo[:, slot, w_cols], rhs_hi(k, cols),
                                       start=False, stop=(k == kts - 1))
                mm.then_inc(g_full, 1)

            def x_h(k, cols):
                return xhi[:, k, cols]

            def x_l(k, cols):
                return xlo[:, k, cols]

            def sum_rows(ps, which, src):
                for half in range(2):
                    mm = pe.matmul(ps[:, half, :], m(which), src[:, half * HALF:(half + 1) * HALF],
                                   start=True, stop=True)
                return mm

            pe.wait_ge(consts_in, 32)
            pe.wait_ge(sem("a_added"), KT + 2)
            sum_rows(psa, M_ONES, pa_acc).then_inc(sem("norm_tot"), 1)
            pe.wait_ge(sem("norm_split"), KT)

            for u in range(2):
                product(B_LORA + u, T_LORA + u, u, u, 0, x_h, x_l)

            pe.wait_ge(sem("lora_split"), 2)
            with pe.Fori(0, PAIRS) as i:
                for j in range(3):
                    t = T_RW + j
                    product(B_RW + 4 * i + j, t, j % 2, t % 2, 3 * i + t // 2, x_h, x_l)
                for j in range(3):
                    t = T_RW + 3 + j
                    hi, lo = (ta_hi, ta_lo) if j < 2 else (sg_hi, sg_lo)
                    product(B_RW + 4 * i + 3, t, 1, t % 2, 3 * i + t // 2, lambda k, c, s=hi: s[:, c],
                            lambda k, c, s=lo: s[:, c], kts=1, col=j * P, first=(j == 0))
                pe.wait_ge(sem("kk_sq"), i + 1)
                sum_rows(psa, M_BLK, TM).then_inc(sem("kk_sum"), 1)
                pe.wait_ge(sem("rk_prod"), i + 1)
                sum_rows(psb, M_BLK, TM).then_inc(sem("bonus_sum"), 1)
                pe.wait_ge(sem("rw_prep"), i + 1)
                for g in range(GROUPS):
                    if g:
                        pe.wait_ge(sem("y_out"), 8 * i + 2 * g)
                        pe.wait_ge(sem("s_new"), 16 * i + 4 * g)
                        pe.wait_ge(sem("rt_pt"), 4 * i + g)
                        pe.sem_inc(go, 1)
                    for tt in range(2):
                        tl = 2 * g + tt
                        for h in range(2):
                            rows = slice(h * CH, h * CH + CH)
                            kr = KR[rows, tl, :, :].rearrange("p a b -> p (a b)")
                            pe.matmul(bank[2 * tt + h][:, 0:256], KK[rows, tl * P:tl * P + P], kr,
                                      start=True, stop=True)
                            pe.matmul(bank[2 * tt + h][:, 256:512], K[rows, tl * P:tl * P + P], kr,
                                      start=True, stop=True).then_inc(sem("scores"), 1)
                    for tt in range(2):
                        tl = 2 * g + tt
                        pe.wait_ge(sem("sc_out"), 16 * i + 4 * g + tt + 1)
                        for j, src in enumerate((BE[:, tl * P:tl * P + P], KE[:, tl * P:tl * P + P],
                                                 V[:, tl * P:tl * P + P], KR[:, tl, 0, :])):
                            mm = pe.transpose(bank[tt][:, j * P:j * P + P], src, m(M_ID))
                        mm.then_inc(sem("tr_full"), 1)
                    pe.wait_ge(sem("sc_out"), 16 * i + 4 * g + 4)
                    for q in range(4):
                        mm = pe.matmul(bank[2][:, q * P:q * P + P], SC[:, q, 0:P], m(M_ID), start=True, stop=True)
                    mm.then_inc(sem("x_full"), 1)
                    pe.wait_ge(sem("tr_act"), 8 * i + 2 * g + 2)
                    pe.wait_ge(sem("tr_dve"), 8 * i + 2 * g + 2)
                    for q in range(4):
                        mm = pe.matmul(bank[1][:, q * CH:q * CH + CH], SC[:, q, 384:512], VT[:, q, :],
                                       start=True, stop=True)
                    mm.then_inc(sem("dv_full"), 1)
                    for lv in range(1, LEVELS):
                        pe.wait_ge(sem("m_ready"), 24 * i + 6 * g + lv)
                        for q in range(4):
                            mm = pe.matmul(bank[2][:, q * P:q * P + P], SC[:, q, 0:P], M[:, q, :],
                                           start=True, stop=True)
                        mm.then_inc(sem("x_full"), 1)
                        pe.wait_ge(sem("x_out"), 20 * i + 5 * g + lv)
                        if lv < LEVELS - 1:
                            for q in range(4):
                                pe.matmul(bank[3][:, q * P:q * P + P], MT[:, q, :], XM[:, q, :],
                                          start=True, stop=True)
                        for q in range(4):
                            mm = pe.matmul(bank[0][:, q * P:q * P + P], XM[:, q, :], MT[:, q, :],
                                           start=True, stop=True)
                        mm.then_inc(sem("mx_full"), 1)
                    pe.wait_ge(sem("m_ready"), 24 * i + 6 * g + LEVELS)
                    pe.wait_ge(sem("z_ready"), 4 * i + g + 1)
                    for q in range(4):
                        mm = pe.matmul(bank[2][:, q * P:q * P + P], MT[:, q, :], Z[:, q, :], start=True, stop=True)
                    mm.then_inc(sem("gh_full"), 1)
                    pe.wait_ge(sem("gh_ready"), 4 * i + g + 1)
                    for q in range(4):
                        h = q % 2
                        mm = pe.matmul(bank[3][h * CH:h * CH + CH, (q // 2) * 256:(q // 2) * 256 + 256],
                                       GH[:, q, 0:CH], SC[:, q, P:P + 256], start=True, stop=True)
                    mm.then_inc(sem("rp_full"), 1)
                    pe.wait_ge(sem("rt_pt"), 4 * i + g + 1)
                    for tt in range(2):
                        psy = bank[0] if tt == 0 else bank[3]
                        for h in range(2):
                            q, rows = 2 * tt + h, slice(h * CH, h * CH + CH)
                            pe.matmul(psy[rows, 0:P], GH[:, q, CH:P], SC[:, q, P:2 * P], start=True, stop=False)
                            pe.matmul(psy[rows, 0:P], VT[:, q, :], SC[:, q, 512:640], start=False, stop=False)
                        for c in range(2):
                            step = 4 * g + 2 * tt + c
                            pss = bank[1 + c]
                            if step >= 2:
                                pe.wait_ge(sem("s_new"), 16 * i + step - 1)
                                pe.sem_inc(go, 1)
                            for h in range(2):
                                q, rows = 2 * tt + h, slice(h * CH, h * CH + CH)
                                pe.matmul(pss[rows, 0:CH], SC[:, q, 256 + c * CH:256 + c * CH + CH],
                                          GH[:, q, CH:P], start=True, stop=False)
                                pe.matmul(pss[rows, 0:CH], SC[:, q, 640 + c * CH:640 + c * CH + CH],
                                          VT[:, q, :], start=False, stop=False)
                            if step >= 1:
                                pe.wait_ge(sem("s_new"), 16 * i + step)
                                pe.sem_inc(go, 1)
                            for h in range(2):
                                rows = slice(h * CH, h * CH + CH)
                                mm = pe.matmul(pss[rows, 0:CH], PT[rows, tt, c * CH:c * CH + CH],
                                               ST[rows, step % 2, :], start=False, stop=True)
                            mm.then_inc(sem("s_full"), 1)
                            for h in range(2):
                                rows = slice(h * CH, h * CH + CH)
                                mm = pe.matmul(psy[rows, c * CH:c * CH + CH], ST[rows, step % 2, :],
                                               RT[rows, tt, c * CH:c * CH + CH], start=False, stop=(c == 1))
                        mm.then_inc(sem("y_full"), 1)
                pe.wait_ge(sem("y_out"), 8 * i + 8)
                pe.wait_ge(sem("s_new"), 16 * i + 16)
                sum_rows(psa, M_BLK, YB).then_inc(sem("gn_mean"), 1)
                pe.wait_ge(sem("gn_sq"), i + 1)
                sum_rows(psb, M_BLK, TM).then_inc(sem("gn_var"), 1)

            pe.wait_ge(sem("yrw_split"), PAIRS)
            with pe.Fori(0, KT) as i:
                product(B_BRW + 2 * i, T_BRW, 0, 0, T_BRW // 2 + i, x_h, x_l)
                product(B_BRW + 2 * i + 1, T_BRW + 1, 1, 1, T_BRW // 2 + i,
                        lambda k, c: yrw_hi[:, k, c], lambda k, c: yrw_lo[:, k, c], kts=PAIRS)

            with pe.Fori(0, PAIRS) as i:
                for j in range(6):
                    t = T_RET + j
                    product(B_RET + 6 * i + j, t, j % 2, t % 2, 3 * i + t // 2, x_h, x_l)
                    if j in (2, 3):
                        if j == 2:
                            pe.wait_ge(sem("ret_free"), i + 1)
                        else:
                            pe.wait_ge(sem("rv_tm"), 2 * i + 1)
                        pe.wait_ge(g_free[t % 2], 3 * i + t // 2 + 2)
                        for c in range(NB):
                            mm = pe.transpose(psb[:, c // 4, (c % 4) * P:(c % 4 + 1) * P], RV[:, c * P:c * P + P],
                                              m(M_ID))
                        mm.then_inc(sem("rv_tr"), 1)
                pe.wait_ge(sem("rkd"), i + 1)
                for c in range(NB):
                    mm = pe.transpose(psa[:, c // 4, (c % 4) * P:(c % 4 + 1) * P], RKD[:, c * P:c * P + P], m(M_ID))
                mm.then_inc(sem("rk_tr"), 1)
                pe.wait_ge(sem("rv_tm"), 2 * i + 2)
                pe.wait_ge(sem("rk_tm"), i + 1)
                for c in range(NB):
                    for h in range(2):
                        mm = pe.matmul(psb[h * CH:h * CH + CH, c // 4, (c % 4) * P:(c % 4 + 1) * P],
                                       RKT[:, c, h * CH:h * CH + CH], RVT[:, h, c, :], start=True, stop=True)
                mm.then_inc(sem("kv_full"), 1)
                pe.wait_ge(sem("r_states"), i + 1)
                for h in range(2):
                    rows = slice(h * CH, h * CH + CH)
                    for c in range(NB):
                        mm = pe.matmul(psa[:, c // 4, (c % 4) * P:(c % 4 + 1) * P], RK[rows, c * P:c * P + P],
                                       RQ[rows, c * P:c * P + P], start=True, stop=True)
                    mm.then_inc(sem("rs_full"), 1)
                    pe.wait_ge(sem("rs_ready"), 2 * i + h + 1)
                    for c in range(NB):
                        o = psb[:, c // 4, (c % 4) * P:(c % 4 + 1) * P]
                        mm = pe.matmul(o, RVT[:, h, c, :], RP[:, c, :], start=True, stop=(c == 0))
                        if c:
                            mm = pe.matmul(o, RS[rows, c, :], RQD[rows, c * P:c * P + P], start=False, stop=True)
                    mm.then_inc(sem("ro_full"), 1)
                    pe.wait_ge(sem("rd_raw"), 2 * i + h + 1)
                    sum_rows(psa, M_ONES, RD).then_inc(sem("rgn_mean"), 1)
                    pe.wait_ge(sem("rgn_sq"), 2 * i + h + 1)
                    sum_rows(psb, M_ONES, RE).then_inc(sem("rgn_var"), 1)

            pe.wait_ge(sem("yret_split"), KT)
            with pe.Fori(0, KT) as i:
                product(B_MRG + 2 * i, T_MRG, 0, 0, T_MRG // 2 + i, x_h, x_l)
                product(B_MRG + 2 * i + 1, T_MRG + 1, 1, 1, T_MRG // 2 + i,
                        lambda k, c: yret_hi[:, k, c], lambda k, c: yret_lo[:, k, c])

            def plain(b0, t0, pairs):
                with pe.Fori(0, pairs) as i:
                    for u in range(2):
                        product(b0 + 2 * i + u, t0 + u, u, u, t0 // 2 + i, x_h, x_l)

            def norm_sum(acc, name, adds=KT):
                pe.wait_ge(sem(name + "_added"), adds + 2)
                sum_rows(psa, M_ONES, acc).then_inc(sem("norm_tot"), 1)

            pe.wait_ge(sem("merged_split"), KT)
            plain(B_OUT, T_OUT, KT // 2)
            norm_sum(oacc, "out")
            norm_sum(oacc, "pre")
            pe.wait_ge(sem("norm_split"), 2 * KT)
            plain(B_UP, T_UP, FT)
            banks = [psg[0][:, 0:HALF], psg[0][:, HALF:T], psg[1][:, 0:HALF], psg[1][:, HALF:T]] + bank

            def down(n, done, u, start, stop):
                pe.wait_ge(w_ready, n + 3)
                pe.wait_ge(sem("f_split"), done + 1)
                for j in range(KT):
                    w_cols = slice(j * P, j * P + P)
                    mm = pe.matmul(banks[j], whi[:, u, w_cols], fhi[:, u, :], start=start, stop=False)
                    if j == 0:
                        mm.then_inc(w_used, 1)
                    pe.matmul(banks[j], whi[:, u, w_cols], flo[:, u, :], start=False, stop=False)
                    mm = pe.matmul(banks[j], wlo[:, u, w_cols], fhi[:, u, :], start=False, stop=stop)
                mm.then_inc(sem("f_used"), 1)

            pe.wait_ge(g_free[0], T_P2 // 2 + 1)
            pe.wait_ge(g_free[1], T_P2 // 2 + 1)
            for half in range(2):
                if half:
                    pe.wait_ge(sem("down_sq"), KT)
                n0, k0 = B_DOWN + half * FT, half * FT
                down(n0, k0, 0, True, False)
                down(n0 + 1, k0 + 1, 1, False, False)
                with pe.Fori(1, FT // 2 - 1) as i:
                    for u in range(2):
                        down(n0 + 2 * i + u, k0 + 2 * i + u, u, False, False)
                down(n0 + FT - 2, k0 + FT - 2, 0, False, False)
                down(n0 + FT - 1, k0 + FT - 1, 1, False, True)
            pe.wait_ge(sem("down_sq"), 2 * KT)
            norm_sum(dacc, "down", 2 * KT)
            norm_sum(dacc, "h2")
            pe.wait_ge(sem("norm_split"), 3 * KT)

            for g in range(4):
                for u in range(2):
                    product(B_P2 + 2 * g + u, T_P2 + 2 * g + u, u, u, T_P2 // 2 + g, x_h, x_l)
                pe.wait_ge(sem("pw_in"), 16 * g + 16)
                pe.wait_ge(sem("pooled"), g + 1)
                for half in range(2):
                    mm = pe.matmul(psa[:, half, :], pw[:, :], pu[:, half * HALF:(half + 1) * HALF],
                                   start=True, stop=True)
                mm.then_inc(sem("mixed"), 1)
            for u in range(2):
                product(B_P2 + 8 + u, T_P2 + 8 + u, u, u, T_P2 // 2 + 4, x_h, x_l)
            pe.wait_ge(g_free[1], T_P2 // 2 + 6)
            for c in range(NB):
                mm = pe.transpose(psb[:, c // 4, (c % 4) * P:(c % 4 + 1) * P], kv_f[:, c * P:c * P + P], m(M_ID))
            mm.then_inc(sem("v2_tr"), 1)
            pe.wait_ge(sem("v2_ready"), 1)
            for kv in range(2):
                with pe.Fori(0, 2) as ii:
                    for u in range(2):
                        product(B_P2 + 10 + 4 * kv + 2 * ii + u, T_P2 + 10 + u, u, u, T_P2 // 2 + 5 + 2 * kv + ii,
                                x_h, x_l)
                    pe.wait_ge(g_free[0], T_P2 // 2 + 7 + 2 * kv + ii)
                    pe.sem_inc(go, 1)
                    for s in range(4):
                        n = 8 * kv + 4 * ii + s
                        for h in range(2):
                            rows = slice(h * CH, h * CH + CH)
                            for b in range(2):
                                nb = 2 * s + b
                                mm = pe.matmul(psa[:, h, b * 256:b * 256 + 256], aq[rows, nb * P:nb * P + P],
                                               kd[rows, kv, nb * P:nb * P + 256], start=True, stop=True)
                        mm.then_inc(sem("as_full"), 1)
                        pe.wait_ge(sem("ap_ready"), n + 1)
                        pe.wait_ge(sem("ao_out"), n + 1)
                        for q in range(4):
                            for kb in range(2):
                                mm = pe.transpose(psb[:, q // 2, (q % 2) * 256 + kb * P:(q % 2) * 256 + kb * P + P],
                                                  ap_[:, q, kb * P:kb * P + P], m(M_ID))
                        mm.then_inc(sem("apt_full"), 1)
                        pe.wait_ge(sem("apt_ready"), n + 1)
                        for h in range(2):
                            for b in range(2):
                                for kb in range(2):
                                    mm = pe.matmul(psb[h * CH:h * CH + CH, 0, b * P:b * P + P],
                                                   vt2[:, 2 * s + b + kb, kv * CH:kv * CH + CH],
                                                   apt[:, 2 * h + b, kb, :], start=(kb == 0), stop=(kb == 1))
                        mm.then_inc(sem("ao_full"), 1)

            pe.wait_ge(sem("cat_split"), KT)
            plain(B_O2, T_O2, KT // 2)
            norm_sum(q2acc, "fin")

        @block.vector
        def _(v):
            tt, ts, stt = v.tensor_tensor, v.tensor_scalar, v.scalar_tensor_tensor
            MUL, ADD, SUB = ALU.mult, ALU.add, ALU.subtract
            v.sem_inc(g_free[0], 1)
            v.sem_inc(g_free[1], 1)

            def start_sum(name, acc):
                v.memset(acc[:, :], 0.0)
                v.sem_inc(sem(name + "_added"), 2)

            def add_square(name, acc, sq, j):
                v.drain()
                v.wait_ge(sem(name + "_sq"), j + 1)
                tt(acc[:, :], acc[:, :], sq, ADD).then_inc(sem(name + "_added"), 1)

            def root(name, rstd):
                v.wait_ge(sem("norm_tot"), NORM[name] + 1)
                ts(rstd[:, :], flat(psa), 1.0 / D, 1e-6, MUL, ADD).then_inc(sem("norm_ms"), 1)
                v.wait_ge(sem("norm_sd"), NORM[name] + 1)
                v.reciprocal(rstd[:, :], rstd[:, :])
                v.drain()

            def split_normed(name, src, gain, rstd, tmp):
                for j in range(KT + 1):
                    if j < KT:
                        stt(tmp[:, j % 2, :], src[:, j, :], par_col(gain, j), rstd[:, :], MUL, MUL
                            ).then_inc(sem("normed"), 1)
                    if j:
                        v.wait_ge(sem("norm_high"), KT * SPLIT[name] + j)
                        tt(xlo[:, j - 1, :], tmp[:, (j - 1) % 2, :], xhi[:, j - 1, :].bitcast(F32), SUB
                           ).then_inc(sem("norm_split"), 1)
                    v.drain()

            def split_low(name, src, hi, lo, n):
                for j in range(n):
                    v.wait_ge(sem(name + "_h"), j + 1)
                    tt(lo[:, j, :], src[:, j, :], hi[:, j, :].bitcast(F32), SUB).then_inc(sem(name + "_split"), 1)

            start_sum("a", pa_acc)
            for j in range(KT):
                add_square("a", pa_acc, pa_sq[:, j % 2, :], j)
            v.wait_ge(consts_in, 32)
            root("a", pa_rstd)
            split_normed("x", xres, "g_mix_pre", pa_rstd, pa_tmp)
            tt(id2[:, :], m(M_ID)[:, 0:CH], m(M_ID)[:, CH:P], ADD)
            v.memset(SC[:, :, :], 0.0)

            ts(pp[:, 10:12], prm[:, COLS["mu_low"]:COLS["mu_low"] + 2], -1.0, 1.0, MUL, ADD
               ).then_inc(sem("low_par"), 1)
            for u, buf in enumerate((R, K)):
                v.wait_ge(sem("low_a"), u + 1)
                stt(buf[:, 1:T], psg[u][:, 0:T - 1], par_col("mu_low", u), buf[:, 1:T], MUL, ADD
                    ).then_inc(g_free[u], 1)
            v.wait_ge(sem("low_hi"), 1)
            tt(ta_lo[:, :], R[:, :], ta_hi[:, :].bitcast(F32), SUB).then_inc(sem("lora_split"), 1)
            v.wait_ge(sem("low_hi"), 2)
            tt(sg_lo[:, :], K[:, :], sg_hi[:, :].bitcast(F32), SUB).then_inc(sem("lora_split"), 1)

            with v.Fori(0, PAIRS) as i:
                v.drain()
                v.tensor_copy(pp[:, 0:10], prm[:, bass.ds(COLS["rw"] + 10 * i, 10)])
                v.drain()
                ts(pp[:, 10:13], pp[:, 0:3], -1.0, 1.0, MUL, ADD)
                ts(pp[:, 13:14], pp[:, 6:7], -1.0, 1.0, MUL, ADD).then_inc(sem("pp_ready"), 1)
                for j, buf in enumerate((R, K, V)):
                    v.wait_ge(sem("sh_a"), 3 * i + j + 1)
                    stt(buf[:, 1:T], psg[j % 2][:, 0:T - 1], pp[:, j:j + 1], buf[:, 1:T], MUL, ADD
                        ).then_inc(g_free[j % 2], 1)
                v.drain()
                ts(KK[:, :], K[:, :], pp[:, 5:6], None, MUL).then_inc(sem("kk_ready"), 1)
                v.memset(E1[:, :], 1.0)
                v.drain()
                v.memset(E1[:, 0:T:CH], 0.0)
                v.drain()
                v.wait_ge(g_free[1], 3 * i + 4)
                v.tensor_tensor_scan(CS[:, :], E1[:, :], SG[:, :], 0.0, MUL, ADD)
                v.drain()
                tt(SG[:, :], CS[:, :], SG[:, :], SUB)
                v.wait_ge(g_free[0], 3 * i + 5)
                ts(BON[:, :], A[:, :], pp[:, 6:7], pp[:, 13:14], MUL, ADD)
                v.drain()
                tt(K[:, :], K[:, :], BON[:, :], MUL)
                v.wait_ge(sem("kk_sum"), i + 1)
                ts(TM[:, :], flat(psa), 1e-24, None, ALU.max).then_inc(sem("kk_max"), 1)
                v.wait_ge(sem("kk_root"), i + 1)
                v.reciprocal(TM[:, :], TM[:, :])
                v.drain()
                tt(KK[:, :], KK[:, :], TM[:, :], MUL)
                v.drain()
                stt(TM[:, :], R[:, :], pp[:, 7:8], K[:, :], MUL, MUL).then_inc(sem("rk_prod"), 1)
                v.wait_ge(sem("exp_ready"), i + 1)
                tt(KR[:, :, 0, :], KK[:, :].rearrange("p (n c) -> p n c", c=P),
                   SG[:, :].rearrange("p (n c) -> p n c", c=P), MUL)
                tt(KR[:, :, 1, :], R[:, :].rearrange("p (n c) -> p n c", c=P),
                   E1[:, :].rearrange("p (n c) -> p n c", c=P), MUL)
                tt(A[:, :], KK[:, :], A[:, :], MUL)
                v.tensor_copy(ec[:, :], E1[:, CH - 1:T:CH])
                tt(K[:, :], K[:, :], EN[:, :], MUL)
                v.drain()
                tt(KK[:, :], A[:, :], EN[:, :], MUL)
                v.drain()

                def by_chunk(t):
                    return t[:, :].rearrange("p (n c) -> p n c", c=CH)

                ecb = ec[:, :].unsqueeze(2).broadcast_to([P, 16, CH])
                tt(by_chunk(BE), by_chunk(KK), ecb, MUL)
                tt(by_chunk(KE), by_chunk(K), ecb, MUL)
                tt(by_chunk(DG), id2[:, :].unsqueeze(1).broadcast_to([P, 16, CH]), ecb, MUL)
                v.memset(ST[:, 0, :], 0.0)
                v.wait_ge(sem("bonus_sum"), i + 1)
                tt(BON[:, :], flat(psb), V[:, :], MUL).then_inc(sem("rw_prep"), 1)
                for g in range(GROUPS):
                    msk = mat[:, M_STRICT:M_STRICT + 2, :].rearrange("p a b -> p (a b)").unsqueeze(1
                                                                                    ).broadcast_to([P, 2, 256])
                    for q in range(4):
                        v.wait_ge(sem("scores"), 16 * i + 4 * g + q + 1)
                        tt(SC[:, q, :].rearrange("p (a x) -> p a x", a=2)[:, :, 0:256],
                           bank[q].rearrange("p (a x) -> p a x", a=2), msk, MUL).then_inc(sem("sc_out"), 1)
                    for t2 in range(2):
                        v.wait_ge(sem("tr_full"), 8 * i + 2 * g + t2 + 1)
                        for c in range(2):
                            rows = slice(c * CH, c * CH + CH)
                            mm = v.tensor_copy(
                                SC[rows, 2 * t2:2 * t2 + 2, :].rearrange("p h (k x) -> p h k x", k=2)[
                                    :, :, :, 256 + c * CH:256 + c * CH + CH],
                                bank[t2][rows, 0:256].rearrange("p (k h d) -> p h k d", k=2, h=2))
                        mm.then_inc(sem("tr_dve"), 1)
                    v.drain()
                    tt(MT[:, :, :], SC[:, :, 0:P], many(M_LOW0T, 4), MUL)
                    v.wait_ge(sem("x_full"), 24 * i + 6 * g + 1)
                    tt(XM[:, :, :], bank[2].rearrange("p (q c) -> p q c", q=4), many(M_LVL, 4), MUL)
                    v.drain()
                    tt(M[:, :, :], many(M_ID, 4), XM[:, :, :], SUB)
                    tt(MT[:, :, :], many(M_ID, 4), MT[:, :, :], SUB).then_inc(sem("m_ready"), 1)
                    for lv in range(1, LEVELS):
                        v.wait_ge(sem("x_full"), 24 * i + 6 * g + 1 + lv)
                        tt(XM[:, :, :], bank[2].rearrange("p (q c) -> p q c", q=4), many(M_LVL + lv, 4), MUL
                           ).then_inc(sem("x_out"), 1)
                        v.wait_ge(sem("mx_full"), 20 * i + 5 * g + lv)
                        if lv < LEVELS - 1:
                            tt(M[:, :, :], M[:, :, :], bank[3].rearrange("p (q c) -> p q c", q=4), SUB)
                        tt(MT[:, :, :], MT[:, :, :], bank[0].rearrange("p (q c) -> p q c", q=4), SUB
                           ).then_inc(sem("m_ready"), 1)
                    v.wait_ge(sem("rp_full"), 4 * i + g + 1)
                    rp = bank[3].rearrange("p (t x) -> p t x", t=2)
                    tt(RT[:, :, :], rp[:, :, 0:P], KR[:, 2 * g:2 * g + 2, 1, :], ADD)
                    tt(PT[:, :, :], rp[:, :, P:2 * P],
                       DG[:, 2 * g * P:2 * g * P + 2 * P].rearrange("p (t x) -> p t x", t=2), ADD
                       ).then_inc(sem("rt_pt"), 1)
                v.wait_ge(sem("gn_mean"), i + 1)
                stt(YB[:, :], flat(psa), -1.0 / CH, YB[:, :], MUL, ADD).then_inc(sem("gn_cent"), 1)
                v.wait_ge(sem("gn_var"), i + 1)
                ts(TM[:, :], flat(psb), 1.0 / CH, 64e-5, MUL, ADD).then_inc(sem("gn_ms"), 1)
                v.wait_ge(sem("gn_sd"), i + 1)
                v.reciprocal(TM[:, :], TM[:, :])
                v.drain()
                tt(YB[:, :], YB[:, :], TM[:, :], MUL).then_inc(sem("gn_nrm"), 1)
                v.wait_ge(sem("gn_aff"), i + 1)
                tt(YB[:, :], YB[:, :], BON[:, :], ADD)
                v.drain()
                tt(yrw[:, bass.ds(i, 1), :].rearrange("p a t -> p (a t)"), YB[:, :], G[:, :], MUL
                   ).then_inc(sem("yrw_done"), 1)
            split_low("yrw", yrw, yrw_hi, yrw_lo, PAIRS)
            with v.Fori(0, KT) as i:
                v.wait_ge(g_free[0], T_BRW // 2 + 2 + i)
                v.wait_ge(sem("mrw_stored"), 16 * i + 16)
                v.wait_ge(g_full, T_BRW + 2 + 2 * i)
                tt(br_out[:, 0, :], psg[1][:, :], br_sig[:, 0, :], MUL).then_inc(g_free[1], 1)

            v.wait_ge(sem("pos_in"), 16)
            v.tensor_copy(ang[:, :], posi[:, :])
            v.drain()
            ts(ang[:, :], ang[:, :], par_col("invf"), None, MUL)
            v.drain()
            for shift, tab in ((0.0, sin_t), (0.25, cos_t)):
                ts(kq[:, :], ang[:, :], float(1 / (2 * np.pi)), shift, MUL, ADD)
                v.drain()
                ts(kq[:, :], kq[:, :], MAGIC, None, ADD)
                v.drain()
                ts(kq[:, :], kq[:, :], MAGIC, None, SUB)
                v.drain()
                stt(tab[:, :], kq[:, :], -TWO_PI_A, ang[:, :], MUL, ADD)
                v.drain()
                stt(tab[:, :], kq[:, :], -TWO_PI_B, tab[:, :], MUL, ADD)
                v.drain()
                stt(tab[:, :], kq[:, :], -TWO_PI_C, tab[:, :], MUL, ADD)
                v.drain()
                ts(tab[:, :], tab[:, :], float(shift * 2 * np.pi), float(np.float32(3.1415925)), ADD, ALU.min)
                v.drain()
                ts(tab[:, :], tab[:, :], -float(np.float32(3.1415925)), None, ALU.max).then_inc(sem("angle"), 1)
            v.wait_ge(sem("sincos"), 1)
            v.sem_inc(sem("ret_free"), 1)

            def by_token(t):
                return t[:, :].rearrange("p (n c) -> p n c", c=P)

            def psn(ps):
                return ps[:].rearrange("p a (b c) -> p (a b) c", c=P)

            with v.Fori(0, PAIRS) as i:
                v.drain()
                v.tensor_copy(ec[:, 0:1], prm[:, bass.ds(COLS["cdecay"] + i, 1)])
                for j, buf in enumerate((RQ, RK)):
                    v.wait_ge(sem("rr_raw"), 2 * i + j + 1)
                    tt(rq_c[:, :], psg[j][:, :], cos_t[:, :], MUL).then_inc(g_free[j], 1)
                    v.wait_ge(sem("rr_swp"), 128 * i + 64 * j + 64)
                    tt(buf[:, :], rq_swp[:, :], sin_t[:, :], MUL)
                    v.drain()
                    tt(buf[:, :], buf[:, :], rq_c[:, :], ADD).then_inc(sem("rr_done"), 1)
                    v.drain()
                v.wait_ge(sem("tab_in"), 16 * i + 16)
                tt(by_token(RQD), by_token(RQ), RTAB[:, 2, :].unsqueeze(1).broadcast_to([P, NB, P]), MUL)
                tt(by_token(RKD), by_token(RK), RTAB[:, 3, :].unsqueeze(1).broadcast_to([P, NB, P]), MUL
                   ).then_inc(sem("rkd"), 1)
                for h in range(2):
                    v.wait_ge(sem("rg_sig"), 2 * i + h + 1)
                    tt(RG[:, h, :], RG[:, h, :], psg[h][:, :], MUL).then_inc(g_free[h], 1)
                v.wait_ge(sem("rk_tr"), i + 1)
                v.tensor_copy(RKT[:, :, :], psn(psa)).then_inc(sem("rk_tm"), 1)
                v.wait_ge(sem("kv_full"), i + 1)
                v.tensor_copy(RS[:, 1, :], psn(psb)[:, 0, :])
                for c in range(1, NB - 1):
                    v.drain()
                    mm = stt(RS[:, c + 1, :], RS[:, c, :], ec[:, 0:1], psn(psb)[:, c, :], MUL, ADD)
                mm.then_inc(sem("r_states"), 1)
                for h in range(2):
                    v.wait_ge(sem("rs_full"), 2 * i + h + 1)
                    tt(RP[:, :, :], psn(psa), RTAB[:, h, :].unsqueeze(1).broadcast_to([P, NB, P]), MUL
                       ).then_inc(sem("rs_ready"), 1)
                    v.wait_ge(sem("rgn_mean"), 2 * i + h + 1)
                    stt(RD[:, :], flat(psa), -1.0 / P, RD[:, :], MUL, ADD).then_inc(sem("rgn_cent"), 1)
                    v.wait_ge(sem("rgn_var"), 2 * i + h + 1)
                    ts(RE[:, :], flat(psb), 1.0 / P, 1e-5, MUL, ADD).then_inc(sem("rgn_ms"), 1)
                    v.wait_ge(sem("rgn_sd"), 2 * i + h + 1)
                    v.reciprocal(RE[:, :], RE[:, :])
                    v.drain()
                    tt(RD[:, :], RD[:, :], RE[:, :], MUL)
                    v.drain()
                    tt(yret[:, bass.ds(2 * i + h, 1), :].rearrange("p a t -> p (a t)"), RD[:, :], RG[:, h, :], MUL
                       ).then_inc(sem("yret_done"), 1)
                v.drain()
                v.sem_inc(sem("ret_free"), 1)
            split_low("yret", yret, yret_hi, yret_lo, KT)
            v.sem_inc(sem("mg_done"), 1)
            with v.Fori(0, KT) as i:
                v.wait_ge(g_free[0], T_MRG // 2 + 2 + i)
                v.wait_ge(g_full, T_MRG + 2 + 2 * i)
                tt(mg_b[:, :], psg[1][:, :], mg_sig[:, :], MUL).then_inc(g_free[1], 1)
                v.drain()
                v.wait_ge(sem("mg_landed"), 16 * i + 16)
                tt(merged[:, bass.ds(i, 1), :].rearrange("p a t -> p (a t)"), mg_b[:, :], mg_in[:, 0, :], ADD
                   ).then_inc(sem("mg_done"), 1)
            split_low("merged", merged, xhi, xlo, KT)

            start_sum("out", oacc)
            with v.Fori(0, KT // 2) as i:
                for u in range(2):
                    v.drain()
                    v.wait_ge(g_free[u], T_OUT // 2 + 2 + i)
                    tt(oacc[:, :], oacc[:, :], osq[:, u, :], ADD).then_inc(sem("out_added"), 1)

            def residual(name, y, gain, rstd, x, h, nxt, acc, sq):
                start_sum(nxt, acc)
                for j in range(KT + 1):
                    if j < KT:
                        stt(y[:, j, :], y[:, j, :], par_col(gain, j), rstd[:, :], MUL, MUL)
                    if j:
                        add_square(nxt, acc, sq[:, (j - 1) % 2, :], j - 1)
                    v.drain()
                    if j < KT:
                        tt(h[:, j, :], x[:, j, :], y[:, j, :], ADD).then_inc(sem(name + "_h"), 1)

            root("out", orstd)
            v.wait_ge(sem("oh_in"), 16)
            residual("out", oy, "g_mix_post", orstd, oh, oh, "pre", oacc, osq)
            root("pre", orstd)
            split_normed("pre", oh, "g_ffn_pre", orstd, otmp)
            v.wait_ge(sem("h_stored"), 16)
            v.sem_inc(sem("f_done"), 1)

            with v.Fori(0, FT) as i:
                v.drain()
                v.tensor_copy(cp[:, :], prm[:, bass.ds(COLS["conv"] + 8 * i, 8)]).then_inc(sem("cp_ready"), 1)
                v.drain()
                for u, buf in enumerate((fg, fv)):
                    v.wait_ge(sem("cv_a"), 2 * i + u + 1)
                    stt(buf[:, 0, 1:T], psg[u][:, 0:T - 1], cp[:, 4 * u + 1:4 * u + 2], buf[:, 0, 1:T], MUL, ADD)
                    v.drain()
                    stt(buf[:, 0, 2:T], psg[u][:, 0:T - 2], cp[:, 4 * u:4 * u + 1], buf[:, 0, 2:T], MUL, ADD
                        ).then_inc(g_free[u], 1)
                v.drain()
                v.wait_ge(sem("gelu"), i + 1)
                tt(ff[:, bass.ds(i, 1), :].rearrange("p a t -> p (a t)"), fg[:, 0, :], fv[:, 0, :], MUL
                   ).then_inc(sem("f_done"), 1)
            start_sum("down", dacc)
            for half in range(2):
                cols = slice(half * HALF, (half + 1) * HALF)
                with v.Fori(0, FT // 2) as i:
                    for u in range(2):
                        v.wait_ge(sem("f_h"), half * FT + 2 * i + u + 1)
                        tt(flo[:, u, :], ff[:, bass.ds(2 * i + u, 1), cols].rearrange("p a t -> p (a t)"),
                           fhi[:, u, :].bitcast(F32), SUB).then_inc(sem("f_split"), 1)
                for j in range(KT):
                    v.drain()
                    v.wait_ge(sem("down_sq"), half * KT + j + 1)
                    tt(dacc[:, cols], dacc[:, cols], dsq[:, j % 2, :], ADD).then_inc(sem("down_added"), 1)
            root("down", drstd)
            v.wait_ge(sem("dh_in"), 16)
            residual("down", dy, "g_ffn_post", drstd, dh, h2, "h2", dacc, dtmp)
            root("h2", drstd)
            split_normed("h2", h2, "g2_pre", drstd, dtmp)

            for g in range(4):
                win = 2 ** (g + 1)
                v.wait_ge(g_free[0], T_P2 // 2 + g + 2)
                src, dst = pu, ps2
                for k in range(g + 1):
                    s = 2 ** k
                    v.tensor_copy(dst[:, 0:s], src[:, 0:s])
                    tt(dst[:, s:T], src[:, s:T], src[:, 0:T - s], ADD)
                    v.drain()
                    src, dst = dst, (ps4 if dst is ps2 else ps2)
                c = COLS["counts"] + 15 * g
                tt(src[:, 0:win - 1], src[:, 0:win - 1], prm[:, c:c + win - 1], MUL)
                v.drain()
                stt(pu[:, :], src[:, :], 1.0 / win, pu[:, :], MUL, SUB).then_inc(sem("pooled"), 1)
                v.wait_ge(sem("pg_sig"), g + 1)
                tt(pgt[:, :], pgt[:, :], psg[1][:, :], MUL).then_inc(g_free[1], 1)
                v.drain()
                v.wait_ge(sem("mixed"), g + 1)
                stt(cat[:, g, :], flat(psa), par_col("pscale", g), pgt[:, :], MUL, MUL
                    ).then_inc(sem("pool_done"), 1)
            v.drain()
            v.memset(kd[:, :, 0:P], 0.0)
            v.memset(vt2[:, 0, :], 0.0).then_inc(sem("kv_zero"), 1)

            v.sem_inc(sem("ao_out"), 1)
            for kv in range(2):
                with v.Fori(0, 2) as ii:
                    v.drain()
                    v.tensor_copy(sm[:, 0:2], prm[:, bass.ds(COLS["sinks"] + 4 * kv + 2 * ii, 2)])
                    v.wait_ge(sem("ag_sig"), 2 * kv + ii + 1)
                    tt(ag[:, :], ag[:, :], psg[1][:, :], MUL).then_inc(g_free[1], 1)
                    v.wait_ge(sem("ab_in"), 32 * kv + 16 * ii + 16)
                    snk = sm[:, 0:2].unsqueeze(2).broadcast_to([P, 2, 2])
                    for s in range(4):
                        n = 8 * kv + 4 * ii + s
                        v.wait_ge(sem("as_full"), n + 1)
                        for h in range(2):
                            if s == 0:
                                for b in range(2):
                                    stt(ap_[:, 2 * h + b, :], psa[:, h, b * 256:b * 256 + 256], 0.125,
                                        ab[:, 1 - b, h, :], MUL, ADD)
                            else:
                                stt(ap_[:, 2 * h:2 * h + 2, :], psa[:, h, :].rearrange("p (b c) -> p b c", b=2), 0.125,
                                    ab[:, 0, h, :].unsqueeze(1).broadcast_to([P, 2, 256]), MUL, ADD)
                        v.drain()
                        v.tensor_reduce(sm[:, 4:8], ap_[:, :, :], AX_X, ALU.max)
                        v.drain()
                        tt(sm[:, 8:12].rearrange("p (h b) -> p h b", h=2),
                           sm[:, 4:8].rearrange("p (h b) -> p h b", h=2), snk, ALU.max)
                        v.drain()
                        ts(sm[:, 8:12], sm[:, 8:12], -1.0, None, MUL)
                        v.drain()
                        tt(sm[:, 12:16].rearrange("p (h b) -> p h b", h=2),
                           sm[:, 8:12].rearrange("p (h b) -> p h b", h=2), snk, ADD).then_inc(sem("am_ready"), 1)
                        v.wait_ge(sem("ae_ready"), n + 1)
                        tt(sm[:, 20:24], sm[:, 16:20], sm[:, 12:16], ADD)
                        v.drain()
                        v.reciprocal(sm[:, 20:24], sm[:, 20:24])
                        v.drain()
                        tt(ap_[:, :, :], ap_[:, :, :], sm[:, 20:24].unsqueeze(2).broadcast_to([P, 4, 256]), MUL
                           ).then_inc(sem("ap_ready"), 1)
                        v.wait_ge(sem("apt_full"), n + 1)
                        v.tensor_copy(apt[:].rearrange("p a b c -> p (a b c)"), flat(psb)).then_inc(sem("apt_ready"), 1)
                        v.wait_ge(sem("ao_full"), n + 1)
                        tt(cat[:, bass.ds(4 + 2 * kv + ii, 1), s * 256:s * 256 + 256].rearrange("p a t -> p (a t)"),
                           psb[:, 0, 0:256], ag[:, s * 256:s * 256 + 256], MUL).then_inc(sem("ao_out"), 1)
            split_low("cat", cat, xhi, xlo, KT)
            start_sum("fin", q2acc)
            with v.Fori(0, KT // 2) as i:
                for u in range(2):
                    v.drain()
                    v.wait_ge(g_free[u], T_O2 // 2 + 2 + i)
                    tt(q2acc[:, :], q2acc[:, :], q2sq[:, u, :], ADD).then_inc(sem("fin_added"), 1)
            root("fin", q2rstd)
            for j in range(KT):
                stt(y2[:, j, :], y2[:, j, :], par_col("g2_post", j), q2rstd[:, :], MUL, MUL)
                v.drain()
                tt(y2[:, j, :], y2[:, j, :], h2[:, j, :], ADD).then_inc(sem("y_done"), 1)

        @block.scalar
        def _(s):
            act = s.activation
            SIG, SQ, CP, IDN, SQRT, EXP = ACT.Sigmoid, ACT.Square, ACT.Copy, ACT.Identity, ACT.Sqrt, ACT.Exp

            def root(name, rstd):
                s.wait_ge(sem("norm_ms"), NORM[name] + 1)
                act(rstd[:, :], rstd[:, :], SQRT).then_inc(sem("norm_sd"), 1)

            def squares(name, ready, src, sq):
                for j in range(KT):
                    s.wait_ge(ready, j + 1)
                    s.wait_ge(sem(name + "_added"), j + 1)
                    act(sq[:, j % 2, :], src[:, j, :], SQ).then_inc(sem(name + "_sq"), 1)

            def split_high(name, tmp):
                for j in range(KT):
                    s.wait_ge(sem("normed"), KT * SPLIT[name] + j + 1)
                    act(xhi[:, j, :], tmp[:, j % 2, :], CP).then_inc(sem("norm_high"), 1)

            def high(name, src, hi, n):
                for j in range(n):
                    act(hi[:, j, :], src[:, j, :], CP).then_inc(sem(name + "_h"), 1)

            for j in range(0, KT, 2):
                s.dma_start(xres[:, j:j + 2, :], xt[:, j:j + 2, :]).then_inc(sem(f"x_in{j // 2}"), 16)
            s.dma_start(mat[:, :, :], mats).then_inc(consts_in, 16)
            s.dma_start(prm[:, :], par).then_inc(consts_in, 16)
            for j in range(KT):
                s.wait_ge(sem(f"x_in{j // 2}"), 16)
                s.wait_ge(sem("a_added"), j + 1)
                act(pa_sq[:, j % 2, :], xres[:, j, :], SQ).then_inc(sem("a_sq"), 1)
            root("a", pa_rstd)
            split_high("x", pa_tmp)

            s.wait_ge(sem("low_par"), 1)
            for u, buf in enumerate((R, K)):
                s.wait_ge(g_full, u + 1)
                act(buf[:, :], psg[u][:, :], IDN, scale=pp[:, 10 + u:11 + u]).then_inc(sem("low_a"), 1)
            s.wait_ge(g_free[0], 2)
            act(R[0:CH, :], R[0:CH, :], ACT.Tanh)
            s.wait_ge(g_free[1], 2)
            act(K[:, :], K[:, :], SIG)
            s.drain()
            act(ta_hi[:, :], R[:, :], CP).then_inc(sem("low_hi"), 1)
            act(sg_hi[:, :], K[:, :], CP).then_inc(sem("low_hi"), 1)

            with s.Fori(0, PAIRS) as i:
                s.wait_ge(sem("pp_ready"), i + 1)
                for j, buf in enumerate((R, K, V)):
                    s.wait_ge(g_full, 6 * i + T_RW + j + 1)
                    act(buf[:, :], psg[j % 2][:, :], IDN, scale=pp[:, 10 + j:11 + j]).then_inc(sem("sh_a"), 1)
                s.wait_ge(g_full, 6 * i + T_RW + 4)
                act(SG[:, :], psg[1][:, :], SIG, bias=pp[:, 3:4]).then_inc(g_free[1], 1)
                s.wait_ge(g_full, 6 * i + T_RW + 5)
                act(A[:, :], psg[0][:, :], SIG, bias=pp[:, 4:5]).then_inc(g_free[0], 1)
                s.wait_ge(g_full, 6 * i + T_RW + 6)
                act(G[:, :], psg[1][:, :], CP).then_inc(g_free[1], 1)
                s.wait_ge(sem("kk_ready"), i + 1)
                act(TM[:, :], KK[:, :], SQ).then_inc(sem("kk_sq"), 1)
                s.wait_ge(sem("kk_max"), i + 1)
                act(TM[:, :], TM[:, :], SQRT).then_inc(sem("kk_root"), 1)
                act(E1[:, :], CS[:, :], EXP, scale=-C0)
                act(EN[:, :], CS[:, :], EXP, scale=C0)
                act(SG[:, :], SG[:, :], EXP, scale=-C0).then_inc(sem("exp_ready"), 1)
                for g in range(GROUPS):
                    for t2 in range(2):
                        s.wait_ge(sem("tr_dve"), 8 * i + 2 * g + t2 + 1)
                        act(VT[:, 2 * t2:2 * t2 + 2, :], bank[t2][:, 256:384].rearrange("p (h d) -> p h d", h=2), CP)
                        act(Z[:, 2 * t2:2 * t2 + 2, 0:CH], bank[t2][:, 384:512].rearrange("p (h d) -> p h d", h=2), CP
                            ).then_inc(sem("tr_act"), 1)
                    s.wait_ge(sem("dv_full"), 4 * i + g + 1)
                    act(Z[:, :, CH:P], bank[1][:, 0:256].rearrange("p (q d) -> p q d", q=4), CP
                        ).then_inc(sem("z_ready"), 1)
                    s.wait_ge(sem("gh_full"), 4 * i + g + 1)
                    act(GH[:, :, :], bank[2].rearrange("p (q c) -> p q c", q=4), CP, scale=-1.0
                        ).then_inc(sem("gh_ready"), 1)
                    for t2 in range(2):
                        tl = 2 * g + t2
                        for c in range(2):
                            step = 4 * g + 2 * t2 + c
                            s.wait_ge(sem("s_full"), 16 * i + step + 1)
                            act(ST[:, (step + 1) % 2, :], bank[1 + c][:, 0:CH], CP).then_inc(sem("s_new"), 1)
                        s.wait_ge(sem("y_full"), 8 * i + tl + 1)
                        act(YB[:, tl * P:tl * P + P], (bank[0] if t2 == 0 else bank[3])[:, 0:P], CP
                            ).then_inc(sem("y_out"), 1)
                s.wait_ge(sem("gn_cent"), i + 1)
                act(TM[:, :], YB[:, :], SQ).then_inc(sem("gn_sq"), 1)
                s.wait_ge(sem("gn_ms"), i + 1)
                act(TM[:, :], TM[:, :], SQRT).then_inc(sem("gn_sd"), 1)
                s.wait_ge(sem("gn_nrm"), i + 1)
                act(YB[:, :], YB[:, :], IDN, scale=pp[:, 8:9], bias=pp[:, 9:10]).then_inc(sem("gn_aff"), 1)
            s.wait_ge(sem("yrw_done"), PAIRS)
            high("yrw", yrw, yrw_hi, PAIRS)
            s.sem_inc(sem("mrw_stored"), 16)
            with s.Fori(0, KT) as i:
                s.wait_ge(g_free[1], T_BRW // 2 + 1 + i)
                s.wait_ge(g_full, T_BRW + 1 + 2 * i)
                act(br_sig[:, 0, :], psg[0][:, :], SIG).then_inc(g_free[0], 1)
                s.wait_ge(g_free[1], T_BRW // 2 + 2 + i)
                s.dma_start(mrw_d[:, bass.ds(i, 1), :].rearrange("p a t -> p (a t)"), br_out[:, 0, :]
                            ).then_inc(sem("mrw_stored"), 16)

            s.wait_ge(sem("mrw_stored"), 16 * KT + 16)
            s.dma_start(posi[:, :], pos).then_inc(sem("pos_in"), 16)
            s.wait_ge(sem("angle"), 2)
            act(sin_t[:, :], sin_t[:, :], ACT.Sin, scale=par_col("sgn"))
            act(cos_t[:, :], cos_t[:, :], ACT.Sin).then_inc(sem("sincos"), 1)

            with s.Fori(0, PAIRS) as i:
                s.wait_ge(sem("ret_free"), i + 1)
                s.dma_start(RTAB[:, :, :], ret_tab[bass.ds(i, 1)].rearrange("a p j c -> p (a j) c")
                            ).then_inc(sem("tab_in"), 16)
                for j in range(2):
                    s.wait_ge(g_full, T_RET + 6 * i + j + 1)
                    act(rq_raw[:, :], psg[j][:, :], CP).then_inc(sem("rr_raw"), 1)
                    s.wait_ge(sem("rr_raw"), 2 * i + j + 1)
                    for q in range(4):
                        dst, src = q * 32, (q ^ 1) * 32
                        s.dma_start(rq_swp[dst:dst + 32, :], rq_raw[src:src + 32, :]).then_inc(sem("rr_swp"), 16)
                    s.wait_ge(sem("rr_done"), 2 * i + j + 1)
                    s.sem_inc(go, 1)
                for h in range(2):
                    s.wait_ge(g_full, T_RET + 6 * i + 2 + h + 1)
                    act(RV[:, :], psg[h][:, :], CP).then_inc(g_free[h], 1)
                    s.wait_ge(sem("rv_tr"), 2 * i + h + 1)
                    act(RVT[:, h, :, :], psb[:].rearrange("p a (b c) -> p (a b) c", c=P), CP
                        ).then_inc(sem("rv_tm"), 1)
                for h in range(2):
                    s.wait_ge(g_full, T_RET + 6 * i + 4 + h + 1)
                    act(RG[:, h, :], psg[h][:, :], SIG).then_inc(sem("rg_sig"), 1)
                for h in range(2):
                    s.wait_ge(sem("ro_full"), 2 * i + h + 1)
                    act(RD[:, :], flat(psb), CP).then_inc(sem("rd_raw"), 1)
                    s.wait_ge(sem("rgn_cent"), 2 * i + h + 1)
                    act(RE[:, :], RD[:, :], SQ).then_inc(sem("rgn_sq"), 1)
                    s.wait_ge(sem("rgn_ms"), 2 * i + h + 1)
                    act(RE[:, :], RE[:, :], SQRT).then_inc(sem("rgn_sd"), 1)
            s.wait_ge(sem("yret_done"), KT)
            high("yret", yret, yret_hi, KT)
            s.wait_ge(sem("yret_split"), KT)
            with s.Fori(0, KT) as i:
                s.wait_ge(sem("mg_done"), i + 1)
                s.dma_start(mg_in[:, 0, :], mrw_d[:, bass.ds(i, 1), :].rearrange("p a t -> p (a t)")
                            ).then_inc(sem("mg_landed"), 16)
                s.wait_ge(g_full, T_MRG + 1 + 2 * i)
                act(mg_sig[:, :], psg[0][:, :], SIG).then_inc(g_free[0], 1)
            s.wait_ge(sem("mg_done"), KT + 1)
            s.dma_start(oh[:, :, :], xt).then_inc(sem("oh_in"), 16)
            high("merged", merged, xhi, KT)

            def evacuate(t0, name, y, sq):
                with s.Fori(0, KT // 2) as i:
                    for u in range(2):
                        s.wait_ge(sem(name + "_added"), 2 * i + u + 1)
                        s.wait_ge(g_full, t0 + 2 * i + u + 1)
                        s.sem_inc(go, 1)
                        act(y[:, bass.ds(2 * i + u, 1), :].rearrange("p a t -> p (a t)"), psg[u][:, :], CP)
                        act(sq[:, u, :], psg[u][:, :], SQ).then_inc(g_free[u], 1)

            evacuate(T_OUT, "out", oy, osq)
            root("out", orstd)
            squares("pre", sem("out_h"), oh, osq)
            s.dma_start(h_d, oh[:, :, :]).then_inc(sem("h_stored"), 16)
            root("pre", orstd)
            split_high("pre", otmp)

            with s.Fori(0, FT) as i:
                s.wait_ge(sem("f_done"), i + 1)
                s.wait_ge(sem("cp_ready"), i + 1)
                s.wait_ge(g_full, T_UP + 2 * i + 1)
                act(fg[:, 0, :], psg[0][:, :], IDN, scale=cp[:, 2:3], bias=cp[:, 3:4]).then_inc(sem("cv_a"), 1)
                s.wait_ge(g_free[0], T_UP // 2 + 2 + i)
                act(fg[:, 0, :], fg[:, 0, :], ACT.Gelu_apprx_tanh).then_inc(sem("gelu"), 1)
                s.wait_ge(g_full, T_UP + 2 * i + 2)
                act(fv[:, 0, :], psg[1][:, :], IDN, scale=cp[:, 6:7], bias=cp[:, 7:8]).then_inc(sem("cv_a"), 1)
            s.wait_ge(sem("f_done"), FT + 1)
            s.dma_start(dh[:, :, :], h_d).then_inc(sem("dh_in"), 16)
            banks = [psg[0][:, 0:HALF], psg[0][:, HALF:T], psg[1][:, 0:HALF], psg[1][:, HALF:T]] + bank
            s.sem_inc(sem("f_used"), 2)
            for half in range(2):
                cols = slice(half * HALF, (half + 1) * HALF)
                with s.Fori(0, FT // 2) as i:
                    for u in range(2):
                        s.wait_ge(sem("f_used"), half * FT + 2 * i + u + 1)
                        s.sem_inc(go, 1)
                        act(fhi[:, u, :], ff[:, bass.ds(2 * i + u, 1), cols].rearrange("p a t -> p (a t)"), CP
                            ).then_inc(sem("f_h"), 1)
                s.wait_ge(sem("f_used"), half * FT + FT + 2)
                for j in range(KT):
                    s.wait_ge(sem("down_added"), half * KT + j + 1)
                    act(dy[:, j, cols], banks[j], CP)
                    act(dsq[:, j % 2, :], banks[j], SQ).then_inc(sem("down_sq"), 1)
            root("down", drstd)
            squares("h2", sem("down_h"), h2, dtmp)
            root("h2", drstd)
            split_high("h2", dtmp)

            for g in range(4):
                if g:
                    s.wait_ge(sem("pool_done"), g)
                s.dma_start(pw[:, :], pool_w[g]).then_inc(sem("pw_in"), 16)
                s.wait_ge(g_full, T_P2 + 2 * g + 1)
                act(pu[:, :], psg[0][:, :], CP).then_inc(g_free[0], 1)
                s.wait_ge(g_full, T_P2 + 2 * g + 2)
                act(pgt[:, :], psg[1][:, :], SIG).then_inc(sem("pg_sig"), 1)
            s.wait_ge(sem("kv_zero"), 1)
            s.wait_ge(g_full, T_P2 + 9)
            for kv in range(2):
                for h in range(2):
                    mm = act(kd[h * CH:h * CH + CH, kv, P:], psg[0][kv * CH:kv * CH + CH, :], CP)
            mm.then_inc(g_free[0], 1)
            s.wait_ge(g_full, T_P2 + 10)
            act(kv_f[:, :], psg[1][:, :], CP).then_inc(g_free[1], 1)
            s.wait_ge(sem("v2_tr"), 1)
            act(vt2[:, 1:, :], psb[:].rearrange("p a (b c) -> p (a b) c", c=P), CP).then_inc(sem("v2_ready"), 1)
            for kv in range(2):
                with s.Fori(0, 2) as ii:
                    s.wait_ge(sem("ao_out"), 8 * kv + 4 * ii + 1)
                    s.dma_start(ab[:, :, :, :], att_bias[bass.ds(2 * kv + ii, 1)].rearrange("a p x h c -> (a p) x h c")
                                ).then_inc(sem("ab_in"), 16)
                    s.wait_ge(g_full, T_P2 + 10 + 4 * kv + 2 * ii + 1)
                    act(aq[:, :], psg[0][:, :], CP).then_inc(g_free[0], 1)
                    s.wait_ge(g_full, T_P2 + 10 + 4 * kv + 2 * ii + 2)
                    act(ag[:, :], psg[1][:, :], SIG).then_inc(sem("ag_sig"), 1)
                    for st in range(4):
                        s.wait_ge(sem("am_ready"), 8 * kv + 4 * ii + st + 1)
                        for q in range(4):
                            act(ap_[:, q, :], ap_[:, q, :], EXP, bias=sm[:, 8 + q:9 + q], accum_out=sm[:, 16 + q:17 + q])
                        act(sm[:, 12:16], sm[:, 12:16], EXP).then_inc(sem("ae_ready"), 1)
            s.wait_ge(sem("ao_out"), 17)
            high("cat", cat, xhi, KT)
            evacuate(T_O2, "fin", y2, q2sq)
            root("fin", q2rstd)
            for j in range(KT):
                s.wait_ge(sem("y_done"), j + 1)
                s.dma_start(out[:, j, :], y2[:, j, :]).then_inc(sem("stored"), 16)
            s.wait_ge(sem("stored"), 16 * KT)


def constants():
    i = np.arange(P)
    t, s = i[:, None], i[None, :]
    mats = np.zeros((NMAT, P, P), np.float32)
    mats[M_ID] = np.eye(P)
    mats[M_ONES] = 1
    same = (t // CH) == (s // CH)
    mats[M_BLK] = same
    mats[M_STRICT] = same & (t < s)
    mats[M_INCL] = same & (t <= s)
    for lv in range(LEVELS):
        low = ((t >> (lv + 1)) == (s >> (lv + 1))) & ((t >> lv) % 2 == 1) & ((s >> lv) % 2 == 0)
        mats[M_LVL + lv] = low
        if lv == 0:
            mats[M_LOW0T] = low.T
    lg = np.log1p(-np.exp2(-5.0 - np.arange(8)))
    ret = np.zeros((PAIRS, P, 4, P), np.float32)
    cdec = np.zeros((P, PAIRS), np.float32)
    for p in range(PAIRS):
        for h in range(2):
            g = lg[2 * p + h]
            rel = s - t
            ret[p, :, h, :] = np.where(rel >= 0, np.exp(np.maximum(rel, 0) * g), 0) * 0.125
            rows = slice(h * CH, h * CH + CH)
            ret[p, rows, 2, :] = np.exp((i + 1.0) * g)[None, :]
            ret[p, rows, 3, :] = np.exp((P - 1.0 - i) * g)[None, :] * 0.125
            cdec[rows, p] = np.exp(P * g)
    slopes = np.exp2(-8.0 * np.arange(1, 9) / 8)
    q, k = np.arange(P)[:, None], np.arange(2 * P)[None, :]
    dist = q + P - k
    win = (dist >= 0) & (dist < P)
    bias = np.zeros((PAIRS, P, 2, 2, 2 * P), np.float32)
    for p in range(PAIRS):
        for h in range(2):
            b = -slopes[2 * p + h] * dist
            bias[p, :, 0, h, :] = np.where(win, b, NEG)
            bias[p, :, 1, h, :] = np.where(win & (k >= P), b, NEG)
    invf = (10000.0 ** (-np.arange(32, dtype=np.float64) / 32)).astype(np.float32)
    counts = np.ones((4, 15), np.float32)
    for g in range(4):
        w = 2 ** (g + 1)
        counts[g, :w - 1] = w / np.arange(1.0, w)
    tab = {"cdecay": cdec, "invf": invf[i % 32][:, None], "sgn": np.where(i % 64 < 32, -1.0, 1.0)[:, None],
           "counts": np.broadcast_to(counts.reshape(1, 60), (P, 60))}
    return mats.transpose(1, 0, 2), ret, bias, {k: v.astype(np.float32) for k, v in tab.items()}


def columns(vec):
    return vec.reshape(-1, P).T


def kernel(**inputs):
    import concourse.bacc as bacc
    from concourse.bass_utils import run_bass_kernel_spmd

    f = {k: np.asarray(v) for k, v in inputs.items()}
    mats, ret, bias, tab = constants()

    def blocks(wm):
        k, n = wm.shape
        b = wm.reshape(k // P, P, n // P, P).transpose(2, 1, 0, 3).reshape(n // P, P, k)
        if k < D:
            b = np.concatenate([b, np.zeros((n // P, P, D - k), wm.dtype)], axis=2)
        return b

    w_in = blocks(f["w_in"][0])
    rw, ret_w, gates = w_in[:14], w_in[14:38], w_in[38:]
    brw, bret, wout = blocks(f["w_branch_rw"][0]), blocks(f["w_branch_ret"][0]), blocks(f["w_out"][0])
    up = blocks(f["ffn_w_up"][0])
    down = f["ffn_w_down"][0].reshape(FT, P, D)
    in2, out2 = blocks(f["w_in_2"][0]), blocks(f["w_out_2"][0])
    low = np.zeros((PAIRS, P, D), np.float32)
    for p in range(PAIRS):
        c = slice(p * P, (p + 1) * P)
        low[p, 0:CH, 0:P] = f["rw_w2"][0][:, c]
        low[p, CH:P, P:2 * P] = f["rw_a2"][0][:, c]
        low[p, :, 2 * P:3 * P] = f["rw_g2"][0][:, c]
    order = [rw[12], rw[13]]
    for p in range(PAIRS):
        order += [rw[p], rw[4 + p], rw[8 + p], low[p]]
    for j in range(8):
        order += [gates[j], brw[j]]
    for p in range(PAIRS):
        order += [ret_w[p], ret_w[4 + p], ret_w[8 + 2 * p], ret_w[9 + 2 * p], ret_w[16 + 2 * p], ret_w[17 + 2 * p]]
    for j in range(8):
        order += [gates[8 + j], bret[j]]
    order += list(wout)
    for j in range(FT):
        order += [up[j], up[FT + j]]
    order += list(down)
    for g in range(4):
        order += [in2[g], in2[4 + g]]
    order += [in2[12], in2[13]]
    for p in range(PAIRS):
        order += [in2[8 + p], in2[14 + p]]
    order += list(out2)
    w = np.stack(order)
    assert w.shape[0] == NSTORED

    mu = columns(f["rw_mu"][0])
    vecs = [columns(f[n][0]) for n in ("rw_w0", "rw_a0", "rw_k_k", "rw_k_a", "rw_r_k", "rw_lnx_w", "rw_lnx_b")]
    cw, cb = f["ffn_conv_w"][0], f["ffn_conv_b"][0]
    cw = [columns(cw[n]) for n in range(3)] + [columns(cb)]
    table = {"g_mix_pre": columns(f["norm_mix_pre"][0]), "g_mix_post": columns(f["norm_mix_post"][0]),
             "g_ffn_pre": columns(f["norm_ffn_pre"][0]), "g_ffn_post": columns(f["norm_ffn_post"][0]),
             "g2_pre": columns(f["norm_pre_2"][0]), "g2_post": columns(f["norm_post_2"][0]),
             "mu_low": mu[:, 12:14],
             "rw": np.concatenate([np.stack([mu[:, p], mu[:, 4 + p], mu[:, 8 + p]] + [v[:, p] for v in vecs], axis=1)
                                   for p in range(PAIRS)], axis=1),
             "conv": np.concatenate([np.stack([c[:, j + o] for o in (0, FT) for c in cw], axis=1)
                                     for j in range(FT)], axis=1),
             "pscale": columns(f["pool_scale_2"][0]),
             "sinks": np.broadcast_to(f["attn_sinks_2"][0][None, :], (P, 8))}
    table.update(tab)
    par = np.concatenate([table[n] for n in COLS], axis=1)

    def feature_major(x):
        return x.T.reshape(KT, P, T).transpose(1, 0, 2)

    given = {"xt": feature_major(f["x"][0]), "pos": np.broadcast_to(f["positions"], (P, T)), "w": w, "par": par,
             "mats": mats, "ret_tab": ret, "att_bias": bias, "pool_w": f["pool_w_2"][0]}
    nc = bacc.Bacc("TRN2", target_bir_lowering=False, num_devices=1)
    arrays, args = {}, []
    for name, a in given.items():
        a = np.ascontiguousarray(a)
        arrays[name] = a
        args.append(nc.dram_tensor(name, a.shape, mybir.dt.from_np(a.dtype), kind="ExternalInput").ap())
    args.append(nc.dram_tensor("out", (P, KT, T), F32, kind="ExternalOutput").ap())
    build(nc, *args)
    r = run_bass_kernel_spmd(nc, [arrays], core_ids=[0])
    return r.results[0]["out"].transpose(1, 0, 2).reshape(D, T).T.reshape(1, T, D)
```

```python
from contextlib import ExitStack

import numpy as np

import concourse.bass as bass
from concourse import mybir

F32 = mybir.dt.float32
F32R = mybir.dt.float32r
I32 = mybir.dt.int32
ALU = mybir.AluOpType
ACT = mybir.ActivationFunctionType
AX_X = mybir.AxisListType.X

P = 128
T = 1024
HALF = 512
D = 1024
KT = D // P
FF = 2816
FT = FF // P
PAIRS = 4
CH = 64
GROUPS = 4
LEVELS = 6
NB = T // P
C0 = float(np.exp(-0.5))
TWO_PI_A = 6.28125
TWO_PI_B = float(np.float32(2 * np.pi - 6.28125))
TWO_PI_C = float(2 * np.pi - 6.28125 - np.float32(2 * np.pi - 6.28125))
MAGIC = float(1.5 * 2 ** 23)
NEG = -1e30

COLS = {}
_n = 0
for _name, _w in (("g_mix_pre", 8), ("g_mix_post", 8), ("g_ffn_pre", 8), ("g_ffn_post", 8), ("g2_pre", 8),
                  ("g2_post", 8), ("mu_low", 2), ("rw", 40), ("conv", 176), ("pscale", 4), ("sinks", 8),
                  ("cdecay", 4), ("invf", 1), ("sgn", 1), ("counts", 60)):
    COLS[_name] = _n
    _n += _w
NPAR = _n

NORM = {n: i for i, n in enumerate(("a", "out", "pre", "down", "h2", "fin"))}
SPLIT = {n: i for i, n in enumerate(("x", "pre", "h2"))}

M_ID, M_CENT, M_BLK, M_STRICT, M_INCL, M_LOW0T, M_LVL = 0, 1, 2, 3, 4, 5, 6
NMAT = M_LVL + LEVELS
M_CENT_RET = NMAT

LATER = 10
B_LORA, T_LORA = 0, 0
B_RW, T_RW = 2, 2
RW_B, RW_T = 4 + LATER, 6 + LATER
B_BRW, T_BRW = B_RW + RW_B * PAIRS, T_RW + RW_T * PAIRS
B_MRG, T_MRG = B_BRW + KT, T_BRW + KT
B_OUT, T_OUT = B_MRG + KT, T_MRG + KT
B_UP, T_UP = B_OUT + 8, T_OUT + 8
B_DOWN = B_UP + 2 * FT
B_P2, T_P2 = B_DOWN + 2 * FT, T_UP + 2 * FT
B_O2, T_O2 = B_P2 + 18, T_P2 + 18
NBLK = B_O2 + 8
S_GRW, S_GRET, S_BRW = 24, 32, 40
NSTORED = NBLK - FT


def build(nc, xt, pos, w, par, mats, ret_tab, att_bias, pool_w, out):
    later_d = nc.dram_tensor("later_scratch", [48, P, T], F32).ap()
    yrw_d = nc.dram_tensor("yrw_scratch", [P, PAIRS, T], F32).ap()
    h_d = nc.dram_tensor("h_scratch", [P, KT, T], F32).ap()

    with ExitStack() as ctx:
        base = [((nc.sbuf_base + 31) // 32) * 32]

        def at(name, offset, shape, dt=F32):
            return nc.alloc_sbuf_tensor_at(name, shape, dt, offset=offset)

        def sb(name, shape, dt=F32):
            size = 4 * int(np.prod(shape[1:]))
            t = at(name, base[0], shape, dt)
            base[0] += (size + 31) // 32 * 32
            return t

        wraw = sb("wraw", [P, 2, 1024])
        whi = sb("whi", [P, 2, 1024], F32R)
        wlo = sb("wlo", [P, 2, 1024], F32R)
        mat = sb("mat", [P, NMAT, P])
        prm = sb("prm", [P, NPAR])
        pp = sb("pp", [P, 15])
        cp = sb("cp", [P, 8])
        ec = sb("ec", [P, 16])
        id2 = sb("id2", [P, CH])
        sm = sb("sm", [P, 24])
        x_at = base[0]
        xhi = sb("xhi", [P, KT, T], F32R)
        xlo = sb("xlo", [P, KT, T], F32R)
        arena = base[0]
        assert arena + 28 * 4096 <= nc.sbuf_usable_end, (arena + 28 * 4096, nc.sbuf_usable_end)

        def tiles(name, i, shape, dt=F32):
            return at(name, arena + 4096 * i, shape, dt)

        def m(i):
            return mat[:, i, :]

        def many(i, n):
            return m(i).unsqueeze(1).broadcast_to([P, n, P])

        def par_col(name, j=0):
            c = COLS[name] + j
            return prm[:, c:c + 1]

        psg = [ctx.enter_context(nc.psum_tensor(f"psg{b}", [P, T], F32)) for b in range(2)]
        psa = ctx.enter_context(nc.psum_tensor("psa", [P, 2, HALF], F32))
        psb = ctx.enter_context(nc.psum_tensor("psb", [P, 2, HALF], F32))
        bank = [psa[:, 0, :], psa[:, 1, :], psb[:, 0, :], psb[:, 1, :]]

        def flat(ps):
            return ps[:].rearrange("p a b -> p (a b)")

        sems = {}

        def sem(name):
            if name not in sems:
                sems[name] = ctx.enter_context(nc.semaphore(name))
            return sems[name]

        w_landed = [sem("w_landed0"), sem("w_landed1")]
        w_ready = sem("w_ready")
        w_used = sem("w_used")
        g_full = sem("g_full")
        g_free = [sem("g_free0"), sem("g_free1")]
        go = sem("go")
        consts_in = sem("consts_in")
        x_in = sem("x_in")

        xres = tiles("xres", 0, [P, KT, T])
        pa_sq = tiles("pa_sq", 8, [P, 2, T])
        pa_acc = tiles("pa_acc", 10, [P, T])
        pa_rstd = tiles("pa_rstd", 11, [P, T])
        pa_tmp = tiles("pa_tmp", 12, [P, 2, T])

        stage = tiles("stage", 0, [P, 2, T])
        ATH, ATL = tiles("rw_ATH", 2, [P, 4, P], F32R), at("rw_ATL", arena + 2 * 4096 + 2048, [P, 4, P], F32R)
        M, MT = tiles("rw_M", 3, [P, 4, P], F32R), at("rw_MT", arena + 3 * 4096 + 2048, [P, 4, P], F32R)
        ta_hi, ta_lo = tiles("ta_hi", 4, [P, T], F32R), tiles("ta_lo", 5, [P, T], F32R)
        sg_hi, sg_lo = tiles("sg_hi", 6, [P, T], F32R), tiles("sg_lo", 7, [P, T], F32R)
        R, K, V, KK, SG, A, CS, E1, EN, G, BON = (
            tiles(f"rw_{n}", 8 + i, [P, T]) for i, n in enumerate("R K V KK SG A CS E1 EN G BON".split()))
        KR = tiles("rw_KR", 19, [P, NB, 2, P])
        TM = tiles("rw_TM", 21, [P, T])
        SC = tiles("rw_SC", 22, [P, 4, 768])
        s_at = arena + 25 * 4096
        VT = at("rw_VT", s_at, [P, 4, CH])
        Z = at("rw_Z", s_at + 1024, [P, 4, P])
        GH = at("rw_GH", s_at + 3072, [P, 4, P])
        XM = at("rw_XM", s_at + 5120, [P, 4, P], F32R)
        MTF = at("rw_MTF", s_at + 7168, [P, 4, P])
        idr = at("rw_idr", s_at + 9216, [P, P], F32R)
        e_at = arena + 15 * 4096
        RT = at("rw_RT", e_at, [P, 2, P])
        PT = at("rw_PT", e_at + 1024, [P, 2, P])
        ST = at("rw_ST", e_at + 2048, [P, 2, CH])
        YB = EN
        DG = R
        BE, KE = A, CS

        def spare(name, i, shape, dt=F32):
            return at(name, x_at + (4096 * (4 + i) if i < 4 else 32768 + 4096 * i), shape, dt)

        yret = tiles("yret", 0, [P, KT, T])
        cos_t, sin_t = tiles("cos_t", 8, [P, T]), tiles("sin_t", 9, [P, T])
        rstage = tiles("rstage", 10, [P, 2, T])
        RQ, RK, RQD, RKD = (tiles(n, 12 + i, [P, T]) for i, n in enumerate(("RQ", "RK", "RQD", "RKD")))
        RV, RG = tiles("RV", 16, [P, 2, T]), tiles("RG", 18, [P, 2, T])
        RGS = tiles("RGS", 20, [P, 2, T])
        RVT = tiles("RVT", 22, [P, 2, NB, P])
        RKT, RS = tiles("RKT", 24, [P, NB, P]), tiles("RS", 25, [P, NB, P])
        RP, RC = tiles("RP", 26, [P, NB, P]), tiles("RC", 27, [P, P])
        rraw = spare("rraw", 0, [P, 2, T])
        rswp = spare("rswp", 2, [P, 2, T])
        RE, RTAB = spare("RE", 4, [P, T]), spare("RTAB", 5, [P, 4, P])
        ang, kq = spare("ang", 0, [P, T]), spare("kq", 1, [P, T])
        posi = spare("posi", 2, [P, T], I32)
        yrw = tiles("yrw", 12, [P, PAIRS, T])

        mgr, mgt, mbr = tiles("mgr", 8, [P, 2, T]), tiles("mgt", 10, [P, 2, T]), tiles("mbr", 12, [P, 2, T])
        merged = tiles("merged", 0, [P, KT, T])

        oy = tiles("oy", 8, [P, KT, T])
        osq = tiles("osq", 16, [P, 2, T])
        oacc, orstd = tiles("oacc", 18, [P, T]), tiles("orstd", 19, [P, T])
        oh = tiles("oh", 20, [P, KT, T])
        otmp = tiles("otmp", 0, [P, 2, T])

        ff = tiles("ff", 0, [P, FT, T])
        fg, fv = tiles("fg", 22, [P, 2, T]), tiles("fv", 24, [P, 2, T])
        dy = at("dy", x_at, [P, KT, T])
        dh = at("dh", x_at + 32768, [P, KT, T])
        fhi, flo = tiles("fhi", 22, [P, 2, HALF], F32R), tiles("flo", 23, [P, 2, HALF], F32R)
        dsq = tiles("dsq", 24, [P, 2, HALF])
        dacc, drstd = tiles("dacc", 25, [P, T]), tiles("drstd", 26, [P, T])
        h2 = tiles("h2", 0, [P, KT, T])
        dtmp = tiles("dtmp", 8, [P, 2, T])

        cat = tiles("cat", 8, [P, KT, T])
        pu, ps2 = tiles("pu", 16, [P, T]), tiles("ps2", 17, [P, T])
        ps4, pgt = tiles("ps4", 18, [P, T]), tiles("pgt", 19, [P, T])
        pw = tiles("pw", 20, [P, P])
        kd = tiles("kd", 16, [P, 2, T + P])
        vt2 = at("vt2", arena + 16 * 4096 + 9216, [P, NB + 1, P])
        ab = tiles("ab", 20, [P, 2, 2, 2 * P])
        aq, ag = tiles("aq", 21, [P, T]), tiles("ag", 22, [P, T])
        kv_f = tiles("kv_f", 21, [P, T])
        ap_ = tiles("ap_", 23, [P, 4, 2 * P])
        apt = tiles("apt", 24, [P, 4, 2, P])
        y2 = tiles("y2", 16, [P, KT, T])
        q2sq = tiles("q2sq", 24, [P, 2, T])
        q2acc, q2rstd = tiles("q2acc", 26, [P, T]), tiles("q2rstd", 27, [P, T])

        block = ctx.enter_context(nc.Block())

        @block.sync
        def _(sp):
            def stream(first, end, shift):
                with sp.Fori(first // 2, end // 2) as i:
                    for u in range(2):
                        sp.wait_ge(w_ready, 2 * i + u + 1)
                        sp.dma_start(wraw[:, u, :], w[bass.ds(2 * i + u - shift, 1)].rearrange("n p c -> p (n c)")
                                     ).then_inc(w_landed[u], 16)

            stream(0, B_DOWN + FT, 0)
            stream(B_DOWN + FT, NBLK, FT)

        @block.gpsimd
        def _(pool):
            pool.sem_inc(w_ready, 2)

            def split_blocks(first, end):
                with pool.Fori(first // 2, end // 2) as i:
                    for u in range(2):
                        pool.wait_ge(w_landed[u], 16 * i + 16)
                        pool.wait_ge(w_used, 2 * i + u + 1)
                        pool.sem_inc(go, 1)
                        pool.tensor_copy(whi[:, u, :], wraw[:, u, :])
                        pool.drain()
                        pool.tensor_tensor(wlo[:, u, :], wraw[:, u, :], whi[:, u, :].bitcast(F32),
                                           ALU.subtract).then_inc(w_ready, 1)

            split_blocks(0, B_DOWN)
            with pool.Fori(0, FT) as i:
                for u in range(2):
                    pool.wait_ge(sem("w_high"), 2 * i + u + 1)
                    pool.sem_inc(go, 1)
                    pool.tensor_tensor(wlo[:, u, :], wraw[:, u, :], whi[:, u, :].bitcast(F32),
                                       ALU.subtract).then_inc(w_ready, 1)
            split_blocks(B_P2, NBLK)

        @block.tensor
        def _(pe):
            pe.sem_inc(w_used, 1)

            def product(n, t, slot, b, use, rhs_hi, rhs_lo, kts=KT, col=0, first=True):
                pe.wait_ge(w_ready, n + 3)
                pe.wait_ge(g_free[b], use + 1)
                for half in range(2):
                    cols = slice(half * HALF, (half + 1) * HALF)
                    for k in range(kts):
                        w_cols = slice(col + k * P, col + (k + 1) * P)
                        mm = pe.matmul(psg[b][:, cols], whi[:, slot, w_cols], rhs_hi(k, cols),
                                       start=(k == 0), stop=False)
                        if first and half == 0 and k == 0:
                            mm.then_inc(w_used, 1)
                        pe.matmul(psg[b][:, cols], whi[:, slot, w_cols], rhs_lo(k, cols), start=False, stop=False)
                        mm = pe.matmul(psg[b][:, cols], wlo[:, slot, w_cols], rhs_hi(k, cols),
                                       start=False, stop=(k == kts - 1))
                mm.then_inc(g_full, 1)

            def x_h(k, cols):
                return xhi[:, k, cols]

            def x_l(k, cols):
                return xlo[:, k, cols]

            def sum_rows(ps, which, src):
                for half in range(2):
                    mm = pe.matmul(ps[:, half, :], m(which), src[:, half * HALF:(half + 1) * HALF],
                                   start=True, stop=True)
                return mm

            def token_sums(src, head_cols=False):
                w_sum = m(M_BLK)[:, CH - 1:CH + 1] if head_cols else pp[:, 14:15]
                n = 2 if head_cols else 1
                for c in range(NB):
                    mm = pe.matmul(psa[:, 0, n * c:n * c + n], src[:, c * P:c * P + P], w_sum, start=True, stop=True)
                return mm

            def spread(src):
                for c in range(NB):
                    mm = pe.transpose(psa[:, c // 4, (c % 4) * P:(c % 4 + 1) * P], src[:, c * P:c * P + P], m(M_ID))
                return mm

            def norm_factor(acc, rstd, name, adds=KT):
                pe.wait_ge(sem(name + "_added"), adds + 2)
                token_sums(acc).then_inc(sem("norm_tot"), 1)
                pe.wait_ge(sem("norm_exp"), NORM[name] + 1)
                spread(rstd).then_inc(sem("norm_rep"), 1)

            pe.wait_ge(consts_in, 32)
            norm_factor(pa_acc, pa_rstd, "a")
            pe.wait_ge(sem("norm_split"), KT)

            for u in range(2):
                product(B_LORA + u, T_LORA + u, u, u, 0, x_h, x_l)

            pe.wait_ge(sem("lora_split"), 2)
            with pe.Fori(0, PAIRS) as i:
                def later_products():
                    for f in range(LATER):
                        j = 6 + f
                        pe.wait_ge(w_ready, B_RW + RW_B * i + 4 + f + 3)
                        pe.wait_ge(g_free[j % 2], 8 * i + j // 2 + 2)
                        slot, ps = f % 2, psg[j % 2]
                        for half in range(2):
                            cols = slice(half * HALF, (half + 1) * HALF)
                            for k in range(KT):
                                w_cols = slice(k * P, (k + 1) * P)
                                mm = pe.matmul(ps[:, cols], whi[:, slot, w_cols], xhi[:, k, cols],
                                               start=(k == 0), stop=False)
                                if half == 0 and k == 0:
                                    mm.then_inc(w_used, 1)
                                yield
                                pe.matmul(ps[:, cols], whi[:, slot, w_cols], xlo[:, k, cols], start=False, stop=False)
                                yield
                                mm = pe.matmul(ps[:, cols], wlo[:, slot, w_cols], xhi[:, k, cols],
                                               start=False, stop=(k == KT - 1))
                                if half == 1 and k == KT - 1:
                                    mm.then_inc(g_full, 1)
                                yield

                later = later_products()

                def fill(n):
                    for _ in range(n):
                        next(later)

                for j in range(3):
                    product(B_RW + RW_B * i + j, T_RW + j, j % 2, j % 2, 8 * i + 1 + j // 2, x_h, x_l)
                for j in range(3, 6):
                    hi, lo = (ta_hi, ta_lo) if j < 5 else (sg_hi, sg_lo)
                    product(B_RW + RW_B * i + 3, T_RW + j, 1, j % 2, 8 * i + 1 + j // 2, lambda k, c, s=hi: s[:, c],
                            lambda k, c, s=lo: s[:, c], kts=1, col=(j - 3) * P, first=(j == 3))
                pe.wait_ge(sem("hd_sq"), 2 * i + 1)
                token_sums(TM, True).then_inc(sem("hd_sum"), 1)
                fill(16)
                pe.wait_ge(sem("hd_exp"), 2 * i + 1)
                spread(TM).then_inc(sem("hd_rep"), 1)
                fill(32)
                pe.wait_ge(sem("rk_prod"), i + 1)
                sum_rows(psb, M_BLK, TM).then_inc(sem("bonus_sum"), 1)
                pe.wait_ge(sem("rw_prep"), i + 1)
                for g in range(GROUPS):
                    if g:
                        pe.wait_ge(sem("y_out"), 8 * i + 2 * g)
                        pe.wait_ge(sem("s_new"), 16 * i + 4 * g)
                        pe.sem_inc(go, 1)
                    for tt in range(2):
                        tl = 2 * g + tt
                        for h in range(2):
                            rows = slice(h * CH, h * CH + CH)
                            kr = KR[rows, tl, :, :].rearrange("p a b -> p (a b)")
                            pe.matmul(bank[2 * tt + h][:, 0:256], KK[rows, tl * P:tl * P + P], kr,
                                      start=True, stop=True)
                            pe.matmul(bank[2 * tt + h][:, 256:512], K[rows, tl * P:tl * P + P], kr,
                                      start=True, stop=True).then_inc(sem("scores"), 1)
                    for tt in range(2):
                        tl = 2 * g + tt
                        pe.wait_ge(sem("sc_out"), 16 * i + 4 * g + tt + 1)
                        pe.matmul(bank[tt][:, 2 * P:3 * P], V[:, tl * P:tl * P + P], m(M_CENT), start=True, stop=True)
                        for j, src in ((0, BE[:, tl * P:tl * P + P]), (1, KE[:, tl * P:tl * P + P]),
                                       (3, KR[:, tl, 0, :])):
                            mm = pe.transpose(bank[tt][:, j * P:j * P + P], src, m(M_ID))
                        mm.then_inc(sem("tr_full"), 1)
                    fill(6)
                    pe.wait_ge(sem("sc_out"), 16 * i + 4 * g + 4)
                    for q in range(4):
                        mm = pe.transpose(bank[2][:, q * P:q * P + P], SC[:, q, 0:P], m(M_ID))
                    mm.then_inc(sem("x_full"), 1)
                    fill(5)
                    pe.wait_ge(sem("tr_act"), 8 * i + 2 * g + 2)
                    for q in range(4):
                        mm = pe.matmul(bank[1][:, q * CH:q * CH + CH], SC[:, q, 384:512], VT[:, q, :],
                                       start=True, stop=True)
                    mm.then_inc(sem("dv_full"), 1)
                    fill(5)
                    for lv in range(1, LEVELS):
                        if lv == 1:
                            pe.wait_ge(sem("m_init"), 4 * i + g + 1)
                        else:
                            pe.wait_ge(sem("m_act"), 20 * i + 5 * g + lv - 1)
                            pe.wait_ge(sem("mt_dve"), 16 * i + 4 * g + lv - 1)
                        for q in range(4):
                            mm = pe.matmul(bank[2][:, q * P:q * P + P], ATH[:, q, :], M[:, q, :],
                                           start=True, stop=True)
                        mm.then_inc(sem("x_full"), 1)
                        fill(5)
                        pe.wait_ge(sem("x_out"), 20 * i + 5 * g + lv)
                        for q in range(4):
                            pe.matmul(bank[3][:, q * P:q * P + P], idr[:, :], M[:, q, :], start=True, stop=False)
                            mm = pe.matmul(bank[3][:, q * P:q * P + P], MT[:, q, :], XM[:, q, :],
                                           start=False, stop=True)
                        mm.then_inc(sem("m_full"), 1)
                        if lv < LEVELS - 1:
                            for q in range(4):
                                pe.matmul(bank[0][:, q * P:q * P + P], idr[:, :], MT[:, q, :], start=True, stop=False)
                                mm = pe.matmul(bank[0][:, q * P:q * P + P], XM[:, q, :], MT[:, q, :],
                                               start=False, stop=True)
                            mm.then_inc(sem("mt_full"), 1)
                        fill(5)
                    pe.wait_ge(sem("m_act"), 20 * i + 5 * g + 5)
                    for q in range(4):
                        o = bank[2][:, q * P:q * P + P]
                        pe.matmul(o, ATH[:, q, :], M[:, q, :], start=True, stop=False)
                        pe.matmul(o, ATL[:, q, :], M[:, q, :], start=False, stop=False)
                        mm = pe.matmul(o, idr[:, :], M[:, q, :], start=False, stop=True)
                    mm.then_inc(sem("e_full"), 1)
                    for q in range(4):
                        mm = pe.transpose(bank[0][:, q * P:q * P + P], M[:, q, :].bitcast(F32), m(M_ID))
                    mm.then_inc(sem("mt0_full"), 1)
                    fill(5)
                    pe.wait_ge(sem("e_ready"), 4 * i + g + 1)
                    pe.wait_ge(sem("mt0_ready"), 4 * i + g + 1)
                    for q in range(4):
                        mm = pe.matmul(bank[3][:, q * P:q * P + P], XM[:, q, :], MT[:, q, :], start=True, stop=True)
                    mm.then_inc(sem("fin_full"), 1)
                    fill(5)
                    pe.wait_ge(sem("mtf_ready"), 4 * i + g + 1)
                    pe.wait_ge(sem("z_ready"), 4 * i + g + 1)
                    for q in range(4):
                        mm = pe.matmul(bank[2][:, q * P:q * P + P], MTF[:, q, :], Z[:, q, :], start=True, stop=True)
                    mm.then_inc(sem("gh_full"), 1)
                    fill(5)
                    pe.wait_ge(sem("gh_ready"), 4 * i + g + 1)
                    for q in range(4):
                        h = q % 2
                        mm = pe.matmul(bank[3][h * CH:h * CH + CH, (q // 2) * 256:(q // 2) * 256 + 256],
                                       GH[:, q, 0:CH], SC[:, q, P:P + 256], start=True, stop=True)
                    mm.then_inc(sem("rp_full"), 1)
                    fill(3)
                    pe.wait_ge(sem("rt_pt"), 4 * i + g + 1)
                    for tt in range(2):
                        psy = bank[0] if tt == 0 else bank[3]
                        for h in range(2):
                            q, rows = 2 * tt + h, slice(h * CH, h * CH + CH)
                            pe.matmul(psy[rows, 0:P], GH[:, q, CH:P], SC[:, q, P:2 * P], start=True, stop=False)
                            pe.matmul(psy[rows, 0:P], VT[:, q, :], SC[:, q, 512:640], start=False, stop=False)
                        for c in range(2):
                            step = 4 * g + 2 * tt + c
                            pss = bank[1 + c]
                            if step >= 2:
                                pe.wait_ge(sem("s_new"), 16 * i + step - 1)
                                pe.sem_inc(go, 1)
                            for h in range(2):
                                q, rows = 2 * tt + h, slice(h * CH, h * CH + CH)
                                pe.matmul(pss[rows, 0:CH], SC[:, q, 256 + c * CH:256 + c * CH + CH],
                                          GH[:, q, CH:P], start=True, stop=False)
                                pe.matmul(pss[rows, 0:CH], SC[:, q, 640 + c * CH:640 + c * CH + CH],
                                          VT[:, q, :], start=False, stop=False)
                            if step >= 1:
                                pe.wait_ge(sem("s_new"), 16 * i + step)
                                pe.sem_inc(go, 1)
                            for h in range(2):
                                rows = slice(h * CH, h * CH + CH)
                                mm = pe.matmul(pss[rows, 0:CH], PT[rows, tt, c * CH:c * CH + CH],
                                               ST[rows, step % 2, :], start=False, stop=True)
                            mm.then_inc(sem("s_full"), 1)
                            for h in range(2):
                                rows = slice(h * CH, h * CH + CH)
                                mm = pe.matmul(psy[rows, c * CH:c * CH + CH], ST[rows, step % 2, :],
                                               RT[rows, tt, c * CH:c * CH + CH], start=False, stop=(c == 1))
                            if c == 1:
                                mm.then_inc(sem("y_full"), 1)
                            fill(2 if step % 4 < 3 else 6)
                pe.wait_ge(sem("y_out"), 8 * i + 8)
                fill(8)
                pe.wait_ge(sem("hd_sq"), 2 * i + 2)
                token_sums(TM, True).then_inc(sem("hd_sum"), 1)
                fill(20)
                pe.wait_ge(sem("hd_exp"), 2 * i + 2)
                spread(TM).then_inc(sem("hd_rep"), 1)
                fill(20)
                assert next(later, 'none left') == 'none left'

            pe.wait_ge(sem("yrw_split"), PAIRS)
            with pe.Fori(0, PAIRS) as i:
                def branch(u):
                    product(B_BRW + 2 * i + u, T_BRW + u, u, u, T_BRW // 2 + i, x_h, x_l, kts=PAIRS)

                pe.wait_ge(sem("ret_in"), 144 * i + 160)
                pe.wait_ge(sem("ret_free"), i + 1)
                for h in range(2):
                    if h:
                        pe.wait_ge(sem("rv_tm"), 2 * i + 1)
                    for c in range(NB):
                        mm = pe.matmul(psb[:, c // 4, (c % 4) * P:(c % 4 + 1) * P], RV[:, h, c * P:c * P + P],
                                       RC[:, :], start=True, stop=True)
                    mm.then_inc(sem("rv_tr"), 1)
                branch(0)
                pe.wait_ge(sem("rkd"), i + 1)
                for c in range(NB):
                    mm = pe.transpose(psa[:, c // 4, (c % 4) * P:(c % 4 + 1) * P], RKD[:, c * P:c * P + P], m(M_ID))
                mm.then_inc(sem("rk_tr"), 1)
                pe.wait_ge(sem("rv_tm"), 2 * i + 2)
                pe.wait_ge(sem("rk_tm"), i + 1)
                for c in range(NB):
                    for h in range(2):
                        mm = pe.matmul(psb[h * CH:h * CH + CH, c // 4, (c % 4) * P:(c % 4 + 1) * P],
                                       RKT[:, c, h * CH:h * CH + CH], RVT[:, h, c, :], start=True, stop=True)
                mm.then_inc(sem("kv_full"), 1)
                for h in range(2):
                    rows = slice(h * CH, h * CH + CH)
                    if h:
                        pe.wait_ge(sem("yret_done"), 2 * i + 1)
                    for c in range(NB):
                        mm = pe.matmul(psa[:, c // 4, (c % 4) * P:(c % 4 + 1) * P], RK[rows, c * P:c * P + P],
                                       RQ[rows, c * P:c * P + P], start=True, stop=True)
                    mm.then_inc(sem("rs_full"), 1)
                    if h == 0:
                        branch(1)
                        pe.wait_ge(sem("r_states"), i + 1)
                    pe.wait_ge(sem("rs_ready"), 2 * i + h + 1)
                    for c in range(NB):
                        o = psb[:, c // 4, (c % 4) * P:(c % 4 + 1) * P]
                        mm = pe.matmul(o, RVT[:, h, c, :], RP[:, c, :], start=True, stop=(c == 0))
                        if c:
                            mm = pe.matmul(o, RS[rows, c, :], RQD[rows, c * P:c * P + P], start=False, stop=True)
                    mm.then_inc(sem("ro_full"), 1)
                    pe.wait_ge(sem("rgn_sq"), 2 * i + h + 1)
                    token_sums(RE).then_inc(sem("rgn_sum"), 1)
                    pe.wait_ge(sem("rgn_exp"), 2 * i + h + 1)
                    spread(RE).then_inc(sem("rgn_rep"), 1)

            def plain(b0, t0, pairs):
                with pe.Fori(0, pairs) as i:
                    for u in range(2):
                        product(b0 + 2 * i + u, t0 + u, u, u, t0 // 2 + i, x_h, x_l)

            pe.wait_ge(sem("yret_split"), KT)
            plain(B_MRG, T_MRG, KT // 2)

            pe.wait_ge(sem("merged_split"), KT)
            plain(B_OUT, T_OUT, KT // 2)
            norm_factor(oacc, orstd, "out")
            norm_factor(oacc, orstd, "pre")
            pe.wait_ge(sem("norm_split"), 2 * KT)
            plain(B_UP, T_UP, FT)
            banks = [psg[0][:, 0:HALF], psg[0][:, HALF:T], psg[1][:, 0:HALF], psg[1][:, HALF:T]] + bank

            def down(n, done, u, start, stop):
                pe.wait_ge(w_ready, n + 3)
                pe.wait_ge(sem("f_split"), done + 1)
                for j in range(KT):
                    w_cols = slice(j * P, j * P + P)
                    mm = pe.matmul(banks[j], whi[:, u, w_cols], fhi[:, u, :], start=start, stop=False)
                    if j == 0:
                        mm.then_inc(w_used, 1)
                    pe.matmul(banks[j], whi[:, u, w_cols], flo[:, u, :], start=False, stop=False)
                    mm = pe.matmul(banks[j], wlo[:, u, w_cols], fhi[:, u, :], start=False, stop=stop)
                mm.then_inc(sem("f_used"), 1)

            pe.wait_ge(g_free[0], T_P2 // 2 + 1)
            pe.wait_ge(g_free[1], T_P2 // 2 + 1)
            for half in range(2):
                if half:
                    pe.wait_ge(sem("down_sq"), KT)
                n0, k0 = B_DOWN + half * FT, half * FT
                down(n0, k0, 0, True, False)
                down(n0 + 1, k0 + 1, 1, False, False)
                with pe.Fori(1, FT // 2 - 1) as i:
                    for u in range(2):
                        down(n0 + 2 * i + u, k0 + 2 * i + u, u, False, False)
                down(n0 + FT - 2, k0 + FT - 2, 0, False, False)
                down(n0 + FT - 1, k0 + FT - 1, 1, False, True)
            pe.wait_ge(sem("down_sq"), 2 * KT)
            norm_factor(dacc, drstd, "down", 2 * KT)
            norm_factor(dacc, drstd, "h2")
            pe.wait_ge(sem("norm_split"), 3 * KT)

            for g in range(4):
                for u in range(2):
                    product(B_P2 + 2 * g + u, T_P2 + 2 * g + u, u, u, T_P2 // 2 + g, x_h, x_l)
                pe.wait_ge(sem("pw_in"), 16 * g + 16)
                pe.wait_ge(sem("pooled"), g + 1)
                for half in range(2):
                    mm = pe.matmul(psa[:, half, :], pw[:, :], pu[:, half * HALF:(half + 1) * HALF],
                                   start=True, stop=True)
                mm.then_inc(sem("mixed"), 1)
            for u in range(2):
                product(B_P2 + 8 + u, T_P2 + 8 + u, u, u, T_P2 // 2 + 4, x_h, x_l)
            pe.wait_ge(g_free[1], T_P2 // 2 + 6)
            for c in range(NB):
                mm = pe.transpose(psb[:, c // 4, (c % 4) * P:(c % 4 + 1) * P], kv_f[:, c * P:c * P + P], m(M_ID))
            mm.then_inc(sem("v2_tr"), 1)
            pe.wait_ge(sem("v2_ready"), 1)
            for kv in range(2):
                with pe.Fori(0, 2) as ii:
                    for u in range(2):
                        product(B_P2 + 10 + 4 * kv + 2 * ii + u, T_P2 + 10 + u, u, u, T_P2 // 2 + 5 + 2 * kv + ii,
                                x_h, x_l)
                    pe.wait_ge(g_free[0], T_P2 // 2 + 7 + 2 * kv + ii)
                    pe.sem_inc(go, 1)
                    for s in range(4):
                        n = 8 * kv + 4 * ii + s
                        for h in range(2):
                            rows = slice(h * CH, h * CH + CH)
                            for b in range(2):
                                nb = 2 * s + b
                                mm = pe.matmul(psa[:, h, b * 256:b * 256 + 256], aq[rows, nb * P:nb * P + P],
                                               kd[rows, kv, nb * P:nb * P + 256], start=True, stop=True)
                        mm.then_inc(sem("as_full"), 1)
                        pe.wait_ge(sem("ap_ready"), n + 1)
                        pe.wait_ge(sem("ao_out"), n + 1)
                        for q in range(4):
                            for kb in range(2):
                                mm = pe.transpose(psb[:, q // 2, (q % 2) * 256 + kb * P:(q % 2) * 256 + kb * P + P],
                                                  ap_[:, q, kb * P:kb * P + P], m(M_ID))
                        mm.then_inc(sem("apt_full"), 1)
                        pe.wait_ge(sem("apt_ready"), n + 1)
                        for h in range(2):
                            for b in range(2):
                                for kb in range(2):
                                    mm = pe.matmul(psb[h * CH:h * CH + CH, 0, b * P:b * P + P],
                                                   vt2[:, 2 * s + b + kb, kv * CH:kv * CH + CH],
                                                   apt[:, 2 * h + b, kb, :], start=(kb == 0), stop=(kb == 1))
                        mm.then_inc(sem("ao_full"), 1)

            pe.wait_ge(sem("cat_split"), KT)
            plain(B_O2, T_O2, KT // 2)
            norm_factor(q2acc, q2rstd, "fin")

        @block.vector
        def _(v):
            tt, ts, stt = v.tensor_tensor, v.tensor_scalar, v.scalar_tensor_tensor
            MUL, ADD, SUB = ALU.mult, ALU.add, ALU.subtract
            v.sem_inc(g_free[0], 1)
            v.sem_inc(g_free[1], 1)
            v.memset(pp[:, 14:15], 1.0)

            def start_sum(name, acc):
                v.memset(acc[:, :], 0.0)
                v.sem_inc(sem(name + "_added"), 2)

            def add_square(name, acc, sq, j):
                v.drain()
                v.wait_ge(sem(name + "_sq"), j + 1)
                tt(acc[:, :], acc[:, :], sq, ADD).then_inc(sem(name + "_added"), 1)

            def root(name, rstd):
                v.wait_ge(sem("norm_tot"), NORM[name] + 1)
                ts(sm[:, 0:NB], psa[:, 0, 0:NB], 1.0 / D, 1e-6, MUL, ADD).then_inc(sem("norm_ms"), 1)
                v.wait_ge(sem("norm_sd"), NORM[name] + 1)
                v.reciprocal(sm[:, 0:NB], sm[:, 0:NB])
                v.drain()
                v.tensor_copy(rstd[:, :].rearrange("p (n c) -> p n c", c=P),
                              sm[:, 0:NB].unsqueeze(2).broadcast_to([P, NB, P])).then_inc(sem("norm_exp"), 1)
                v.wait_ge(sem("norm_rep"), NORM[name] + 1)

            def head_factor(n):
                v.wait_ge(sem("hd_sd"), n)
                v.reciprocal(sm[:, 0:16], sm[:, 0:16])
                v.drain()
                v.tensor_copy(TM[:, :].rearrange("p (n c) -> p n c", c=CH),
                              sm[:, 0:16].unsqueeze(2).broadcast_to([P, 16, CH])).then_inc(sem("hd_exp"), 1)
                v.wait_ge(sem("hd_rep"), n)

            def split_normed(name, src, gain, rstd, tmp):
                for j in range(KT + 1):
                    if j < KT:
                        stt(tmp[:, j % 2, :], src[:, j, :], par_col(gain, j), flat(psa), MUL, MUL
                            ).then_inc(sem("normed"), 1)
                    if j:
                        v.wait_ge(sem("norm_high"), KT * SPLIT[name] + j)
                        tt(xlo[:, j - 1, :], tmp[:, (j - 1) % 2, :], xhi[:, j - 1, :].bitcast(F32), SUB
                           ).then_inc(sem("norm_split"), 1)
                    v.drain()

            def split_low(name, src, hi, lo, n):
                for j in range(n):
                    v.wait_ge(sem(name + "_h"), j + 1)
                    tt(lo[:, j, :], src[:, j, :], hi[:, j, :].bitcast(F32), SUB).then_inc(sem(name + "_split"), 1)

            start_sum("a", pa_acc)
            for j in range(KT):
                add_square("a", pa_acc, pa_sq[:, j % 2, :], j)
            v.wait_ge(consts_in, 32)
            root("a", pa_rstd)
            split_normed("x", xres, "g_mix_pre", pa_rstd, pa_tmp)
            tt(id2[:, :], m(M_ID)[:, 0:CH], m(M_ID)[:, CH:P], ADD)
            v.memset(SC[:, :, :], 0.0)
            v.tensor_copy(idr[:, :], m(M_ID))

            ts(pp[:, 10:12], prm[:, COLS["mu_low"]:COLS["mu_low"] + 2], -1.0, 1.0, MUL, ADD
               ).then_inc(sem("low_par"), 1)
            for u, buf in enumerate((R, K)):
                v.wait_ge(sem("low_a"), u + 1)
                stt(buf[:, 1:T], psg[u][:, 0:T - 1], par_col("mu_low", u), buf[:, 1:T], MUL, ADD
                    ).then_inc(g_free[u], 1)
            v.wait_ge(sem("low_hi"), 1)
            tt(ta_lo[:, :], R[:, :], ta_hi[:, :].bitcast(F32), SUB).then_inc(sem("lora_split"), 1)
            v.wait_ge(sem("low_hi"), 2)
            tt(sg_lo[:, :], K[:, :], sg_hi[:, :].bitcast(F32), SUB).then_inc(sem("lora_split"), 1)

            with v.Fori(0, PAIRS) as i:
                v.drain()
                v.tensor_copy(pp[:, 0:10], prm[:, bass.ds(COLS["rw"] + 10 * i, 10)])
                v.drain()
                ts(pp[:, 10:13], pp[:, 0:3], -1.0, 1.0, MUL, ADD)
                ts(pp[:, 13:14], pp[:, 6:7], -1.0, 1.0, MUL, ADD).then_inc(sem("pp_ready"), 1)
                for j, buf in enumerate((R, K, V)):
                    v.wait_ge(sem("sh_a"), 3 * i + j + 1)
                    stt(buf[:, 1:T], psg[j % 2][:, 0:T - 1], pp[:, j:j + 1], buf[:, 1:T], MUL, ADD
                        ).then_inc(g_free[j % 2], 1)
                v.drain()
                ts(KK[:, :], K[:, :], pp[:, 5:6], None, MUL).then_inc(sem("kk_ready"), 1)
                v.memset(E1[:, :], 1.0)
                v.drain()
                v.memset(E1[:, 0:T:CH], 0.0)
                v.drain()
                v.wait_ge(g_free[1], 8 * i + 4)
                v.tensor_tensor_scan(CS[:, :], E1[:, :], SG[:, :], 0.0, MUL, ADD)
                v.drain()
                tt(SG[:, :], CS[:, :], SG[:, :], SUB)
                v.wait_ge(g_free[0], 8 * i + 5)
                ts(BON[:, :], A[:, :], pp[:, 6:7], pp[:, 13:14], MUL, ADD)
                v.drain()
                tt(K[:, :], K[:, :], BON[:, :], MUL)
                v.wait_ge(sem("hd_sum"), 2 * i + 1)
                ts(sm[:, 0:16], psa[:, 0, 0:16], 1e-24, None, ALU.max).then_inc(sem("hd_ms"), 1)
                head_factor(2 * i + 1)
                tt(KK[:, :], KK[:, :], flat(psa), MUL)
                v.drain()
                stt(TM[:, :], R[:, :], pp[:, 7:8], K[:, :], MUL, MUL).then_inc(sem("rk_prod"), 1)
                v.wait_ge(sem("exp_ready"), i + 1)
                tt(KR[:, :, 0, :], KK[:, :].rearrange("p (n c) -> p n c", c=P),
                   SG[:, :].rearrange("p (n c) -> p n c", c=P), MUL)
                tt(KR[:, :, 1, :], R[:, :].rearrange("p (n c) -> p n c", c=P),
                   E1[:, :].rearrange("p (n c) -> p n c", c=P), MUL)
                tt(A[:, :], KK[:, :], A[:, :], MUL)
                v.tensor_copy(ec[:, :], E1[:, CH - 1:T:CH])
                tt(K[:, :], K[:, :], EN[:, :], MUL)
                v.drain()
                tt(KK[:, :], A[:, :], EN[:, :], MUL)
                v.drain()

                def by_chunk(t):
                    return t[:, :].rearrange("p (n c) -> p n c", c=CH)

                ecb = ec[:, :].unsqueeze(2).broadcast_to([P, 16, CH])
                tt(by_chunk(BE), by_chunk(KK), ecb, MUL)
                tt(by_chunk(KE), by_chunk(K), ecb, MUL)
                tt(by_chunk(DG), id2[:, :].unsqueeze(1).broadcast_to([P, 16, CH]), ecb, MUL)
                v.memset(ST[:, 0, :], 0.0)
                v.wait_ge(sem("bonus_sum"), i + 1)
                tt(BON[:, :], flat(psb), V[:, :], MUL).then_inc(sem("rw_prep"), 1)
                for g in range(GROUPS):
                    msk = mat[:, M_STRICT:M_STRICT + 2, :].rearrange("p a b -> p (a b)").unsqueeze(1
                                                                                    ).broadcast_to([P, 2, 256])
                    for q in range(4):
                        v.wait_ge(sem("scores"), 16 * i + 4 * g + q + 1)
                        tt(SC[:, q, :].rearrange("p (a x) -> p a x", a=2)[:, :, 0:256],
                           bank[q].rearrange("p (a x) -> p a x", a=2), msk, MUL).then_inc(sem("sc_out"), 1)
                    for t2 in range(2):
                        v.wait_ge(sem("tr_full"), 8 * i + 2 * g + t2 + 1)
                        for c in range(2):
                            rows = slice(c * CH, c * CH + CH)
                            mm = v.tensor_copy(
                                SC[rows, 2 * t2:2 * t2 + 2, :].rearrange("p h (k x) -> p h k x", k=2)[
                                    :, :, :, 256 + c * CH:256 + c * CH + CH],
                                bank[t2][rows, 0:256].rearrange("p (k h d) -> p h k d", k=2, h=2))
                        mm.then_inc(sem("tr_dve"), 1)
                    v.drain()
                    tt(MTF[:, :, :], SC[:, :, 0:P], many(M_LOW0T, 4), MUL)
                    v.wait_ge(sem("at_hi"), 4 * i + g + 1)
                    tt(ATL[:, :, :], SC[:, :, 0:P], ATH[:, :, :].bitcast(F32), SUB)
                    v.wait_ge(sem("x_full"), 24 * i + 6 * g + 1)
                    tt(XM[:, :, :], bank[2].rearrange("p (q c) -> p q c", q=4), many(M_LVL, 4), MUL)
                    v.drain()
                    tt(M[:, :, :], XM[:, :, :].bitcast(F32), many(M_ID, 4), ADD)
                    tt(MT[:, :, :], MTF[:, :, :], many(M_ID, 4), ADD).then_inc(sem("m_init"), 1)
                    for lv in range(1, LEVELS):
                        v.wait_ge(sem("x_full"), 24 * i + 6 * g + 1 + lv)
                        tt(XM[:, :, :], bank[2].rearrange("p (q c) -> p q c", q=4), many(M_LVL + lv, 4), MUL
                           ).then_inc(sem("x_out"), 1)
                        if lv < LEVELS - 1:
                            v.wait_ge(sem("mt_full"), 16 * i + 4 * g + lv)
                            v.tensor_copy(MT[:, :, :], bank[0].rearrange("p (q c) -> p q c", q=4)
                                          ).then_inc(sem("mt_dve"), 1)
                    v.wait_ge(sem("e_full"), 4 * i + g + 1)
                    tt(XM[:, :, :], many(M_ID, 4), bank[2].rearrange("p (q c) -> p q c", q=4), SUB
                       ).then_inc(sem("e_ready"), 1)
                    v.wait_ge(sem("fin_full"), 4 * i + g + 1)
                    tt(MTF[:, :, :], MT[:, :, :].bitcast(F32), bank[3].rearrange("p (q c) -> p q c", q=4), ADD
                       ).then_inc(sem("mtf_ready"), 1)
                    v.wait_ge(sem("rp_full"), 4 * i + g + 1)
                    rp = bank[3].rearrange("p (t x) -> p t x", t=2)
                    tt(RT[:, :, :], rp[:, :, 0:P], KR[:, 2 * g:2 * g + 2, 1, :], ADD)
                    tt(PT[:, :, :], rp[:, :, P:2 * P],
                       DG[:, 2 * g * P:2 * g * P + 2 * P].rearrange("p (t x) -> p t x", t=2), ADD
                       ).then_inc(sem("rt_pt"), 1)
                v.wait_ge(sem("hd_sum"), 2 * i + 2)
                ts(sm[:, 0:16], psa[:, 0, 0:16], 1.0 / CH, 64e-5, MUL, ADD).then_inc(sem("hd_ms"), 1)
                head_factor(2 * i + 2)
                tt(YB[:, :], YB[:, :], flat(psa), MUL).then_inc(sem("gn_nrm"), 1)
                v.wait_ge(sem("gn_aff"), i + 1)
                tt(YB[:, :], YB[:, :], BON[:, :], ADD)
                v.drain()
                tt(YB[:, :], YB[:, :], G[:, :], MUL).then_inc(sem("yrw_done"), 1)
            split_low("yrw", yrw, xhi, xlo, PAIRS)

            v.wait_ge(sem("pos_in"), 16)
            v.tensor_copy(ang[:, :], posi[:, :])
            v.drain()
            ts(ang[:, :], ang[:, :], par_col("invf"), None, MUL)
            v.drain()
            for shift, tab in ((0.0, sin_t), (0.25, cos_t)):
                ts(kq[:, :], ang[:, :], float(1 / (2 * np.pi)), shift, MUL, ADD)
                v.drain()
                ts(kq[:, :], kq[:, :], MAGIC, None, ADD)
                v.drain()
                ts(kq[:, :], kq[:, :], MAGIC, None, SUB)
                v.drain()
                stt(tab[:, :], kq[:, :], -TWO_PI_A, ang[:, :], MUL, ADD)
                v.drain()
                stt(tab[:, :], kq[:, :], -TWO_PI_B, tab[:, :], MUL, ADD)
                v.drain()
                stt(tab[:, :], kq[:, :], -TWO_PI_C, tab[:, :], MUL, ADD)
                v.drain()
                ts(tab[:, :], tab[:, :], float(shift * 2 * np.pi), float(np.float32(3.1415925)), ADD, ALU.min)
                v.drain()
                ts(tab[:, :], tab[:, :], -float(np.float32(3.1415925)), None, ALU.max).then_inc(sem("angle"), 1)
            v.wait_ge(sem("sincos"), 1)
            v.sem_inc(sem("ret_free"), 1)

            def by_token(t):
                return t[:, :].rearrange("p (n c) -> p n c", c=P)

            def psn(ps):
                return ps[:].rearrange("p a (b c) -> p (a b) c", c=P)

            with v.Fori(0, PAIRS) as i:
                v.drain()
                v.tensor_copy(ec[:, 0:1], prm[:, bass.ds(COLS["cdecay"] + i, 1)])
                v.wait_ge(sem("ret_in"), 144 * i + 160)
                tt(RGS[:, 0, :], rraw[:, 0, :], cos_t[:, :], MUL)
                tt(RGS[:, 1, :], rraw[:, 1, :], cos_t[:, :], MUL)
                tt(RQ[:, :], rswp[:, 0, :], sin_t[:, :], MUL)
                tt(RK[:, :], rswp[:, 1, :], sin_t[:, :], MUL)
                v.drain()
                tt(RQ[:, :], RQ[:, :], RGS[:, 0, :], ADD)
                tt(RK[:, :], RK[:, :], RGS[:, 1, :], ADD)
                v.drain()
                tt(by_token(RKD), by_token(RK), RTAB[:, 3, :].unsqueeze(1).broadcast_to([P, NB, P]), MUL
                   ).then_inc(sem("rkd"), 1)
                tt(by_token(RQD), by_token(RQ), RTAB[:, 2, :].unsqueeze(1).broadcast_to([P, NB, P]), MUL
                   ).then_inc(sem("rqd"), 1)
                v.wait_ge(sem("rg_sig"), i + 1)
                tt(RGS[:, :, :], RGS[:, :, :], RG[:, :, :], MUL).then_inc(sem("rg_done"), 1)
                v.wait_ge(sem("kv_full"), i + 1)
                v.tensor_copy(RS[:, 1, :], psn(psb)[:, 0, :])
                for c in range(1, NB - 1):
                    v.drain()
                    mm = stt(RS[:, c + 1, :], RS[:, c, :], ec[:, 0:1], psn(psb)[:, c, :], MUL, ADD)
                mm.then_inc(sem("r_states"), 1)
                for h in range(2):
                    v.wait_ge(sem("rs_full"), 2 * i + h + 1)
                    tt(RP[:, :, :], psn(psa), RTAB[:, h, :].unsqueeze(1).broadcast_to([P, NB, P]), MUL
                       ).then_inc(sem("rs_ready"), 1)
                    v.wait_ge(sem("rgn_sum"), 2 * i + h + 1)
                    ts(sm[:, 0:NB], psa[:, 0, 0:NB], 1.0 / P, 1e-5, MUL, ADD).then_inc(sem("rgn_ms"), 1)
                    v.wait_ge(sem("rgn_sd"), 2 * i + h + 1)
                    v.reciprocal(sm[:, 0:NB], sm[:, 0:NB])
                    v.drain()
                    v.tensor_copy(by_token(RE), sm[:, 0:NB].unsqueeze(2).broadcast_to([P, NB, P])
                                  ).then_inc(sem("rgn_exp"), 1)
                    v.wait_ge(sem("rgn_rep"), 2 * i + h + 1)
                    tt(RGS[:, h, :], RGS[:, h, :], flat(psa), MUL)
                    v.drain()
                    tt(yret[:, bass.ds(2 * i + h, 1), :].rearrange("p a t -> p (a t)"), flat(psb), RGS[:, h, :], MUL
                       ).then_inc(sem("yret_done"), 1)
                v.drain()
                v.sem_inc(sem("ret_free"), 1)
            split_low("yret", yret, xhi, xlo, KT)
            v.sem_inc(sem("mg_done"), 2)
            with v.Fori(0, KT // 2) as i:
                for u in range(2):
                    v.wait_ge(sem("mg_sig"), 2 * i + u + 1)
                    tt(mgr[:, u, :], mgr[:, u, :], mbr[:, u, :], MUL)
                    v.wait_ge(g_full, T_MRG + 2 * i + u + 1)
                    tt(mgt[:, u, :], mgt[:, u, :], psg[u][:, :], MUL).then_inc(g_free[u], 1)
                    v.drain()
                    tt(merged[:, bass.ds(2 * i + u, 1), :].rearrange("p a t -> p (a t)"), mgr[:, u, :], mgt[:, u, :],
                       ADD).then_inc(sem("mg_done"), 1)
            split_low("merged", merged, xhi, xlo, KT)

            start_sum("out", oacc)
            with v.Fori(0, KT // 2) as i:
                for u in range(2):
                    v.drain()
                    v.wait_ge(g_free[u], T_OUT // 2 + 2 + i)
                    tt(oacc[:, :], oacc[:, :], osq[:, u, :], ADD).then_inc(sem("out_added"), 1)

            def residual(name, y, gain, rstd, x, h, nxt, acc, sq):
                start_sum(nxt, acc)
                for j in range(KT + 1):
                    if j < KT:
                        stt(y[:, j, :], y[:, j, :], par_col(gain, j), flat(psa), MUL, MUL)
                    if j:
                        add_square(nxt, acc, sq[:, (j - 1) % 2, :], j - 1)
                    v.drain()
                    if j < KT:
                        tt(h[:, j, :], x[:, j, :], y[:, j, :], ADD).then_inc(sem(name + "_h"), 1)

            root("out", orstd)
            v.wait_ge(sem("oh_in"), 16)
            residual("out", oy, "g_mix_post", orstd, oh, oh, "pre", oacc, osq)
            root("pre", orstd)
            split_normed("pre", oh, "g_ffn_pre", orstd, otmp)
            v.wait_ge(sem("h_stored"), 16)
            v.sem_inc(sem("f_done"), 1)

            with v.Fori(0, FT) as i:
                v.drain()
                v.tensor_copy(cp[:, :], prm[:, bass.ds(COLS["conv"] + 8 * i, 8)]).then_inc(sem("cp_ready"), 1)
                v.drain()
                for u, buf in enumerate((fg, fv)):
                    v.wait_ge(sem("cv_a"), 2 * i + u + 1)
                    stt(buf[:, 0, 1:T], psg[u][:, 0:T - 1], cp[:, 4 * u + 1:4 * u + 2], buf[:, 0, 1:T], MUL, ADD)
                    v.drain()
                    stt(buf[:, 0, 2:T], psg[u][:, 0:T - 2], cp[:, 4 * u:4 * u + 1], buf[:, 0, 2:T], MUL, ADD
                        ).then_inc(g_free[u], 1)
                v.drain()
                v.wait_ge(sem("gelu"), i + 1)
                tt(ff[:, bass.ds(i, 1), :].rearrange("p a t -> p (a t)"), fg[:, 0, :], fv[:, 0, :], MUL
                   ).then_inc(sem("f_done"), 1)
            start_sum("down", dacc)
            for half in range(2):
                cols = slice(half * HALF, (half + 1) * HALF)
                with v.Fori(0, FT // 2) as i:
                    for u in range(2):
                        v.wait_ge(sem("f_h"), half * FT + 2 * i + u + 1)
                        tt(flo[:, u, :], ff[:, bass.ds(2 * i + u, 1), cols].rearrange("p a t -> p (a t)"),
                           fhi[:, u, :].bitcast(F32), SUB).then_inc(sem("f_split"), 1)
                for j in range(KT):
                    v.drain()
                    v.wait_ge(sem("down_sq"), half * KT + j + 1)
                    tt(dacc[:, cols], dacc[:, cols], dsq[:, j % 2, :], ADD).then_inc(sem("down_added"), 1)
            root("down", drstd)
            v.wait_ge(sem("dh_in"), 16)
            residual("down", dy, "g_ffn_post", drstd, dh, h2, "h2", dacc, dtmp)
            root("h2", drstd)
            split_normed("h2", h2, "g2_pre", drstd, dtmp)

            for g in range(4):
                win = 2 ** (g + 1)
                v.wait_ge(g_free[0], T_P2 // 2 + g + 2)
                src, dst = pu, ps2
                for k in range(g + 1):
                    s = 2 ** k
                    v.tensor_copy(dst[:, 0:s], src[:, 0:s])
                    tt(dst[:, s:T], src[:, s:T], src[:, 0:T - s], ADD)
                    v.drain()
                    src, dst = dst, (ps4 if dst is ps2 else ps2)
                c = COLS["counts"] + 15 * g
                tt(src[:, 0:win - 1], src[:, 0:win - 1], prm[:, c:c + win - 1], MUL)
                v.drain()
                stt(pu[:, :], src[:, :], 1.0 / win, pu[:, :], MUL, SUB).then_inc(sem("pooled"), 1)
                v.wait_ge(sem("pg_sig"), g + 1)
                tt(pgt[:, :], pgt[:, :], psg[1][:, :], MUL).then_inc(g_free[1], 1)
                v.drain()
                v.wait_ge(sem("mixed"), g + 1)
                stt(cat[:, g, :], flat(psa), par_col("pscale", g), pgt[:, :], MUL, MUL
                    ).then_inc(sem("pool_done"), 1)
            v.drain()
            v.memset(kd[:, :, 0:P], 0.0)
            v.memset(vt2[:, 0, :], 0.0).then_inc(sem("kv_zero"), 1)

            v.sem_inc(sem("ao_out"), 1)
            for kv in range(2):
                with v.Fori(0, 2) as ii:
                    v.drain()
                    v.tensor_copy(sm[:, 0:2], prm[:, bass.ds(COLS["sinks"] + 4 * kv + 2 * ii, 2)])
                    v.wait_ge(sem("ag_sig"), 2 * kv + ii + 1)
                    tt(ag[:, :], ag[:, :], psg[1][:, :], MUL).then_inc(g_free[1], 1)
                    v.wait_ge(sem("ab_in"), 32 * kv + 16 * ii + 16)
                    snk = sm[:, 0:2].unsqueeze(2).broadcast_to([P, 2, 2])
                    for s in range(4):
                        n = 8 * kv + 4 * ii + s
                        v.wait_ge(sem("as_full"), n + 1)
                        for h in range(2):
                            if s == 0:
                                for b in range(2):
                                    stt(ap_[:, 2 * h + b, :], psa[:, h, b * 256:b * 256 + 256], 0.125,
                                        ab[:, 1 - b, h, :], MUL, ADD)
                            else:
                                stt(ap_[:, 2 * h:2 * h + 2, :], psa[:, h, :].rearrange("p (b c) -> p b c", b=2), 0.125,
                                    ab[:, 0, h, :].unsqueeze(1).broadcast_to([P, 2, 256]), MUL, ADD)
                        v.drain()
                        v.tensor_reduce(sm[:, 4:8], ap_[:, :, :], AX_X, ALU.max)
                        v.drain()
                        tt(sm[:, 8:12].rearrange("p (h b) -> p h b", h=2),
                           sm[:, 4:8].rearrange("p (h b) -> p h b", h=2), snk, ALU.max)
                        v.drain()
                        ts(sm[:, 8:12], sm[:, 8:12], -1.0, None, MUL)
                        v.drain()
                        tt(sm[:, 12:16].rearrange("p (h b) -> p h b", h=2),
                           sm[:, 8:12].rearrange("p (h b) -> p h b", h=2), snk, ADD).then_inc(sem("am_ready"), 1)
                        v.wait_ge(sem("ae_ready"), n + 1)
                        tt(sm[:, 20:24], sm[:, 16:20], sm[:, 12:16], ADD)
                        v.drain()
                        v.reciprocal(sm[:, 20:24], sm[:, 20:24])
                        v.drain()
                        tt(ap_[:, :, :], ap_[:, :, :], sm[:, 20:24].unsqueeze(2).broadcast_to([P, 4, 256]), MUL
                           ).then_inc(sem("ap_ready"), 1)
                        v.wait_ge(sem("apt_full"), n + 1)
                        v.tensor_copy(apt[:].rearrange("p a b c -> p (a b c)"), flat(psb)).then_inc(sem("apt_ready"), 1)
                        v.wait_ge(sem("ao_full"), n + 1)
                        tt(cat[:, bass.ds(4 + 2 * kv + ii, 1), s * 256:s * 256 + 256].rearrange("p a t -> p (a t)"),
                           psb[:, 0, 0:256], ag[:, s * 256:s * 256 + 256], MUL).then_inc(sem("ao_out"), 1)
            split_low("cat", cat, xhi, xlo, KT)
            start_sum("fin", q2acc)
            with v.Fori(0, KT // 2) as i:
                for u in range(2):
                    v.drain()
                    v.wait_ge(g_free[u], T_O2 // 2 + 2 + i)
                    tt(q2acc[:, :], q2acc[:, :], q2sq[:, u, :], ADD).then_inc(sem("fin_added"), 1)
            root("fin", q2rstd)
            for j in range(KT):
                stt(y2[:, j, :], y2[:, j, :], par_col("g2_post", j), flat(psa), MUL, MUL)
                v.drain()
                tt(y2[:, j, :], y2[:, j, :], h2[:, j, :], ADD).then_inc(sem("y_done"), 1)

        @block.scalar
        def _(s):
            act = s.activation
            SIG, SQ, CP, IDN, SQRT, EXP = ACT.Sigmoid, ACT.Square, ACT.Copy, ACT.Identity, ACT.Sqrt, ACT.Exp

            def root(name):
                s.wait_ge(sem("norm_ms"), NORM[name] + 1)
                act(sm[:, 0:NB], sm[:, 0:NB], SQRT).then_inc(sem("norm_sd"), 1)

            def squares(name, ready, src, sq):
                for j in range(KT):
                    s.wait_ge(ready, j + 1)
                    s.wait_ge(sem(name + "_added"), j + 1)
                    act(sq[:, j % 2, :], src[:, j, :], SQ).then_inc(sem(name + "_sq"), 1)

            def split_high(name, tmp):
                for j in range(KT):
                    s.wait_ge(sem("normed"), KT * SPLIT[name] + j + 1)
                    act(xhi[:, j, :], tmp[:, j % 2, :], CP).then_inc(sem("norm_high"), 1)

            def high(name, src, hi, n):
                for j in range(n):
                    act(hi[:, j, :], src[:, j, :], CP).then_inc(sem(name + "_h"), 1)

            for j in range(0, KT, 2):
                s.dma_start(xres[:, j:j + 2, :], xt[:, j:j + 2, :]).then_inc(sem(f"x_in{j // 2}"), 16)
            s.dma_start(mat[:, :, :], mats[:, 0:NMAT, :]).then_inc(consts_in, 16)
            s.dma_start(prm[:, :], par).then_inc(consts_in, 16)
            for j in range(KT):
                s.wait_ge(sem(f"x_in{j // 2}"), 16)
                s.wait_ge(sem("a_added"), j + 1)
                act(pa_sq[:, j % 2, :], xres[:, j, :], SQ).then_inc(sem("a_sq"), 1)
            root("a")
            split_high("x", pa_tmp)

            s.wait_ge(sem("low_par"), 1)
            for u, buf in enumerate((R, K)):
                s.wait_ge(g_full, u + 1)
                act(buf[:, :], psg[u][:, :], IDN, scale=pp[:, 10 + u:11 + u]).then_inc(sem("low_a"), 1)
            s.wait_ge(g_free[0], 2)
            act(R[0:CH, :], R[0:CH, :], ACT.Tanh)
            s.wait_ge(g_free[1], 2)
            act(K[:, :], K[:, :], SIG)
            s.drain()
            act(ta_hi[:, :], R[:, :], CP).then_inc(sem("low_hi"), 1)
            act(sg_hi[:, :], K[:, :], CP).then_inc(sem("low_hi"), 1)

            for b in range(2):
                s.sem_inc(sem(f"stored{b}"), 16)
            s.sem_inc(sem("yrw_stored"), 16)

            with s.Fori(0, PAIRS) as i:
                def put_later(f):
                    j = 6 + f
                    b = j % 2
                    s.wait_ge(sem(f"stored{b}"), 80 * i + 16 * (f // 2) + 16)
                    s.wait_ge(g_full, T_RW + RW_T * i + j + 1)
                    act(stage[:, b, :], psg[b][:, :], CP).then_inc(g_free[b], 1)
                    s.wait_ge(g_free[b], 8 * i + j // 2 + 3)
                    s.dma_start(later_d[bass.ds(LATER * i + f, 1)].rearrange("a p t -> (a p) t"), stage[:, b, :]
                                ).then_inc(sem(f"stored{b}"), 16)

                s.wait_ge(sem("pp_ready"), i + 1)
                for j, buf in enumerate((R, K, V)):
                    s.wait_ge(g_full, RW_T * i + T_RW + j + 1)
                    act(buf[:, :], psg[j % 2][:, :], IDN, scale=pp[:, 10 + j:11 + j]).then_inc(sem("sh_a"), 1)
                s.wait_ge(g_full, RW_T * i + T_RW + 4)
                act(SG[:, :], psg[1][:, :], SIG, bias=pp[:, 3:4]).then_inc(g_free[1], 1)
                s.wait_ge(g_full, RW_T * i + T_RW + 5)
                act(A[:, :], psg[0][:, :], SIG, bias=pp[:, 4:5]).then_inc(g_free[0], 1)
                s.wait_ge(g_full, RW_T * i + T_RW + 6)
                act(G[:, :], psg[1][:, :], CP).then_inc(g_free[1], 1)
                s.wait_ge(sem("kk_ready"), i + 1)
                act(TM[:, :], KK[:, :], SQ).then_inc(sem("hd_sq"), 1)
                s.wait_ge(sem("hd_ms"), 2 * i + 1)
                act(sm[:, 0:16], sm[:, 0:16], SQRT).then_inc(sem("hd_sd"), 1)
                act(E1[:, :], CS[:, :], EXP, scale=-C0)
                s.wait_ge(sem("yrw_stored"), 16 * i + 16)
                act(EN[:, :], CS[:, :], EXP, scale=C0)
                act(SG[:, :], SG[:, :], EXP, scale=-C0).then_inc(sem("exp_ready"), 1)
                put_later(0)
                for g in range(GROUPS):
                    s.wait_ge(sem("sc_out"), 16 * i + 4 * g + 4)
                    act(ATH[:, :, :], SC[:, :, 0:P], CP).then_inc(sem("at_hi"), 1)
                    for t2 in range(2):
                        s.wait_ge(sem("tr_dve"), 8 * i + 2 * g + t2 + 1)
                        act(VT[:, 2 * t2:2 * t2 + 2, :], bank[t2][:, 256:384].rearrange("p (h d) -> p h d", h=2), CP)
                        act(Z[:, 2 * t2:2 * t2 + 2, 0:CH], bank[t2][:, 384:512].rearrange("p (h d) -> p h d", h=2), CP
                            ).then_inc(sem("tr_act"), 1)
                    s.wait_ge(sem("dv_full"), 4 * i + g + 1)
                    act(Z[:, :, CH:P], bank[1][:, 0:256].rearrange("p (q d) -> p q d", q=4), CP
                        ).then_inc(sem("z_ready"), 1)
                    for lv in range(1, LEVELS):
                        s.wait_ge(sem("m_full"), 20 * i + 5 * g + lv)
                        act(M[:, :, :], bank[3].rearrange("p (q c) -> p q c", q=4), CP).then_inc(sem("m_act"), 1)
                        if lv == 4:
                            put_later(2 * g + 1)
                    s.wait_ge(sem("mt0_full"), 4 * i + g + 1)
                    act(MT[:, :, :], bank[0].rearrange("p (q c) -> p q c", q=4), CP).then_inc(sem("mt0_ready"), 1)
                    s.wait_ge(sem("gh_full"), 4 * i + g + 1)
                    act(GH[:, :, :], bank[2].rearrange("p (q c) -> p q c", q=4), CP, scale=-1.0
                        ).then_inc(sem("gh_ready"), 1)
                    for t2 in range(2):
                        tl = 2 * g + t2
                        for c in range(2):
                            step = 4 * g + 2 * t2 + c
                            s.wait_ge(sem("s_full"), 16 * i + step + 1)
                            act(ST[:, (step + 1) % 2, :], bank[1 + c][:, 0:CH], CP).then_inc(sem("s_new"), 1)
                        s.wait_ge(sem("y_full"), 8 * i + tl + 1)
                        act(YB[:, tl * P:tl * P + P], (bank[0] if t2 == 0 else bank[3])[:, 0:P], CP
                            ).then_inc(sem("y_out"), 1)
                    put_later(2 * g + 2)
                s.drain()
                act(TM[:, :], YB[:, :], SQ).then_inc(sem("hd_sq"), 1)
                s.wait_ge(sem("hd_ms"), 2 * i + 2)
                act(sm[:, 0:16], sm[:, 0:16], SQRT).then_inc(sem("hd_sd"), 1)
                s.wait_ge(sem("gn_nrm"), i + 1)
                act(YB[:, :], YB[:, :], IDN, scale=pp[:, 8:9], bias=pp[:, 9:10]).then_inc(sem("gn_aff"), 1)
                put_later(9)
                s.wait_ge(sem("yrw_done"), i + 1)
                s.dma_start(yrw_d[:, bass.ds(i, 1), :].rearrange("p a t -> p (a t)"), YB[:, :]
                            ).then_inc(sem("yrw_stored"), 16)
            s.wait_ge(sem("yrw_stored"), 16 * PAIRS + 16)
            for b in range(2):
                s.wait_ge(sem(f"stored{b}"), 80 * PAIRS + 16)
            s.dma_start(yrw[:, :, :], yrw_d).then_inc(sem("yrw_in"), 16)
            s.dma_start(posi[:, :], pos).then_inc(sem("pos_in"), 16)
            s.wait_ge(sem("yrw_in"), 16)
            high("yrw", yrw, xhi, PAIRS)

            s.wait_ge(sem("angle"), 2)
            act(sin_t[:, :], sin_t[:, :], ACT.Sin, scale=par_col("sgn"))
            act(cos_t[:, :], cos_t[:, :], ACT.Sin).then_inc(sem("sincos"), 1)

            def load_pair(n):
                rows = later_d[bass.ds(6 * n, 6)]
                s.dma_start(rraw[:, :, :], rows[0:2].rearrange("a p t -> p a t")).then_inc(sem("ret_in"), 16)
                for q in range(4):
                    dst, src = q * 32, (q ^ 1) * 32
                    s.dma_start(rswp[dst:dst + 32, :, :], rows[0:2, src:src + 32, :].rearrange("a p t -> p a t")
                                ).then_inc(sem("ret_in"), 16)
                s.dma_start(RV[:, :, :], rows[2:4].rearrange("a p t -> p a t")).then_inc(sem("ret_in"), 16)
                s.dma_start(RG[:, :, :], rows[4:6].rearrange("a p t -> p a t")).then_inc(sem("ret_in"), 16)

            def put_branch(i, u):
                s.wait_ge(sem(f"stored{u}"), 80 * PAIRS + 16 + 16 * i)
                s.wait_ge(g_full, T_BRW + 2 * i + u + 1)
                act(rstage[:, u, :], psg[u][:, :], CP).then_inc(g_free[u], 1)
                s.wait_ge(g_free[u], T_BRW // 2 + 2 + i)
                s.dma_start(later_d[bass.ds(S_BRW + 2 * i + u, 1)].rearrange("a p t -> (a p) t"), rstage[:, u, :]
                            ).then_inc(sem(f"stored{u}"), 16)

            s.wait_ge(sem("ret_free"), 1)
            s.dma_start(RC[:, :], mats[:, M_CENT_RET, :]).then_inc(sem("ret_in"), 16)
            load_pair(0)
            with s.Fori(0, PAIRS) as i:
                s.wait_ge(sem("ret_free"), i + 1)
                s.dma_start(RTAB[:, 0:2, :], ret_tab[bass.ds(i, 1), :, 0:2].rearrange("a p j c -> p (a j) c")
                            ).then_inc(sem("ret_in"), 16)
                s.dma_start(RTAB[:, 2:4, :], ret_tab[bass.ds(i, 1), :, 2:4].rearrange("a p j c -> p (a j) c")
                            ).then_inc(sem("ret_in"), 16)
                for h in range(2):
                    s.wait_ge(sem("rv_tr"), 2 * i + h + 1)
                    act(RVT[:, h, :, :], psb[:].rearrange("p a (b c) -> p (a b) c", c=P), CP
                        ).then_inc(sem("rv_tm"), 1)
                s.wait_ge(sem("rqd"), i + 1)
                act(RGS[:, :, :], RG[:, :, :], SIG).then_inc(sem("rg_sig"), 1)
                s.wait_ge(sem("rk_tr"), i + 1)
                act(RKT[:, :, :], psa[:].rearrange("p a (b c) -> p (a b) c", c=P), CP).then_inc(sem("rk_tm"), 1)
                put_branch(i, 0)
                s.wait_ge(sem("rg_done"), i + 1)
                load_pair(i + 1)
                put_branch(i, 1)
                for h in range(2):
                    s.wait_ge(sem("ro_full"), 2 * i + h + 1)
                    act(RE[:, :], flat(psb), SQ).then_inc(sem("rgn_sq"), 1)
                    s.wait_ge(sem("rgn_ms"), 2 * i + h + 1)
                    act(sm[:, 0:NB], sm[:, 0:NB], SQRT).then_inc(sem("rgn_sd"), 1)
            s.wait_ge(sem("yret_done"), KT)
            s.wait_ge(sem("ret_in"), 144 * PAIRS + 128)
            high("yret", yret, xhi, KT)
            for b in range(2):
                s.wait_ge(sem(f"stored{b}"), 80 * PAIRS + 16 + 16 * PAIRS)
            with s.Fori(0, KT // 2) as i:
                for u in range(2):
                    s.wait_ge(sem("mg_done"), 2 * i + u + 1)
                    for buf, row in ((mgr, S_GRW), (mgt, S_GRET), (mbr, S_BRW)):
                        s.dma_start(buf[:, u, :], later_d[bass.ds(row + 2 * i + u, 1)].rearrange("a p t -> (a p) t")
                                    ).then_inc(sem(f"mg_in{u}"), 16)
                    s.wait_ge(sem(f"mg_in{u}"), 48 * i + 48)
                    act(mgr[:, u, :], mgr[:, u, :], SIG)
                    act(mgt[:, u, :], mgt[:, u, :], SIG).then_inc(sem("mg_sig"), 1)
            s.wait_ge(sem("mg_done"), KT + 2)
            s.dma_start(oh[:, :, :], xt).then_inc(sem("oh_in"), 16)
            high("merged", merged, xhi, KT)

            def evacuate(t0, name, y, sq):
                with s.Fori(0, KT // 2) as i:
                    for u in range(2):
                        s.wait_ge(sem(name + "_added"), 2 * i + u + 1)
                        s.wait_ge(g_full, t0 + 2 * i + u + 1)
                        s.sem_inc(go, 1)
                        act(y[:, bass.ds(2 * i + u, 1), :].rearrange("p a t -> p (a t)"), psg[u][:, :], CP)
                        act(sq[:, u, :], psg[u][:, :], SQ).then_inc(g_free[u], 1)

            evacuate(T_OUT, "out", oy, osq)
            root("out")
            squares("pre", sem("out_h"), oh, osq)
            s.dma_start(h_d, oh[:, :, :]).then_inc(sem("h_stored"), 16)
            root("pre")
            split_high("pre", otmp)

            with s.Fori(0, FT) as i:
                s.wait_ge(sem("f_done"), i + 1)
                s.wait_ge(sem("cp_ready"), i + 1)
                s.wait_ge(g_full, T_UP + 2 * i + 1)
                act(fg[:, 0, :], psg[0][:, :], IDN, scale=cp[:, 2:3], bias=cp[:, 3:4]).then_inc(sem("cv_a"), 1)
                s.wait_ge(g_free[0], T_UP // 2 + 2 + i)
                act(fg[:, 0, :], fg[:, 0, :], ACT.Gelu_apprx_tanh).then_inc(sem("gelu"), 1)
                s.wait_ge(g_full, T_UP + 2 * i + 2)
                act(fv[:, 0, :], psg[1][:, :], IDN, scale=cp[:, 6:7], bias=cp[:, 7:8]).then_inc(sem("cv_a"), 1)

            def weights_high(half, i, u):
                s.wait_ge(w_landed[u], 16 * (B_DOWN // 2) + half * 8 * FT + 16 * i + 16)
                s.wait_ge(w_used, B_DOWN + half * FT + 2 * i + u + 1)
                s.sem_inc(go, 1)
                act(whi[:, u, :], wraw[:, u, :], CP).then_inc(sem("w_high"), 1)

            s.wait_ge(sem("f_done"), FT + 1)
            s.dma_start(dh[:, :, :], h_d).then_inc(sem("dh_in"), 16)
            banks = [psg[0][:, 0:HALF], psg[0][:, HALF:T], psg[1][:, 0:HALF], psg[1][:, HALF:T]] + bank
            s.sem_inc(sem("f_used"), 2)
            for half in range(2):
                cols = slice(half * HALF, (half + 1) * HALF)
                with s.Fori(0, FT // 2) as i:
                    for u in range(2):
                        s.wait_ge(sem("f_used"), half * FT + 2 * i + u + 1)
                        s.sem_inc(go, 1)
                        act(fhi[:, u, :], ff[:, bass.ds(2 * i + u, 1), cols].rearrange("p a t -> p (a t)"), CP
                            ).then_inc(sem("f_h"), 1)
                        weights_high(half, i, u)
                s.wait_ge(sem("f_used"), half * FT + FT + 2)
                for j in range(KT):
                    s.wait_ge(sem("down_added"), half * KT + j + 1)
                    act(dy[:, j, cols], banks[j], CP)
                    act(dsq[:, j % 2, :], banks[j], SQ).then_inc(sem("down_sq"), 1)
            root("down")
            squares("h2", sem("down_h"), h2, dtmp)
            root("h2")
            split_high("h2", dtmp)

            for g in range(4):
                if g:
                    s.wait_ge(sem("pool_done"), g)
                s.dma_start(pw[:, :], pool_w[g]).then_inc(sem("pw_in"), 16)
                s.wait_ge(g_full, T_P2 + 2 * g + 1)
                act(pu[:, :], psg[0][:, :], CP).then_inc(g_free[0], 1)
                s.wait_ge(g_full, T_P2 + 2 * g + 2)
                act(pgt[:, :], psg[1][:, :], SIG).then_inc(sem("pg_sig"), 1)
            s.wait_ge(sem("kv_zero"), 1)
            s.wait_ge(g_full, T_P2 + 9)
            for kv in range(2):
                for h in range(2):
                    mm = act(kd[h * CH:h * CH + CH, kv, P:], psg[0][kv * CH:kv * CH + CH, :], CP)
            mm.then_inc(g_free[0], 1)
            s.wait_ge(g_full, T_P2 + 10)
            act(kv_f[:, :], psg[1][:, :], CP).then_inc(g_free[1], 1)
            s.wait_ge(sem("v2_tr"), 1)
            act(vt2[:, 1:, :], psb[:].rearrange("p a (b c) -> p (a b) c", c=P), CP).then_inc(sem("v2_ready"), 1)
            for kv in range(2):
                with s.Fori(0, 2) as ii:
                    s.wait_ge(sem("ao_out"), 8 * kv + 4 * ii + 1)
                    s.dma_start(ab[:, :, :, :], att_bias[bass.ds(2 * kv + ii, 1)].rearrange("a p x h c -> (a p) x h c")
                                ).then_inc(sem("ab_in"), 16)
                    s.wait_ge(g_full, T_P2 + 10 + 4 * kv + 2 * ii + 1)
                    act(aq[:, :], psg[0][:, :], CP).then_inc(g_free[0], 1)
                    s.wait_ge(g_full, T_P2 + 10 + 4 * kv + 2 * ii + 2)
                    act(ag[:, :], psg[1][:, :], SIG).then_inc(sem("ag_sig"), 1)
                    for st in range(4):
                        s.wait_ge(sem("am_ready"), 8 * kv + 4 * ii + st + 1)
                        for q in range(4):
                            act(ap_[:, q, :], ap_[:, q, :], EXP, bias=sm[:, 8 + q:9 + q], accum_out=sm[:, 16 + q:17 + q])
                        act(sm[:, 12:16], sm[:, 12:16], EXP).then_inc(sem("ae_ready"), 1)
            s.wait_ge(sem("ao_out"), 17)
            high("cat", cat, xhi, KT)
            evacuate(T_O2, "fin", y2, q2sq)
            root("fin")
            for j in range(KT):
                s.wait_ge(sem("y_done"), j + 1)
                s.dma_start(out[:, j, :], y2[:, j, :]).then_inc(sem("stored"), 16)
            s.wait_ge(sem("stored"), 16 * KT)


def constants():
    i = np.arange(P)
    t, s = i[:, None], i[None, :]
    mats = np.zeros((NMAT + 1, P, P), np.float32)
    mats[M_ID] = np.eye(P)
    same = (t // CH) == (s // CH)
    mats[M_CENT] = np.eye(P) - same / CH
    mats[M_CENT_RET] = np.eye(P) - 1 / P
    mats[M_BLK] = same
    mats[M_STRICT] = same & (t < s)
    mats[M_INCL] = same & (t <= s)
    for lv in range(LEVELS):
        low = ((t >> (lv + 1)) == (s >> (lv + 1))) & ((t >> lv) % 2 == 1) & ((s >> lv) % 2 == 0)
        mats[M_LVL + lv] = -1.0 * low
        if lv == 0:
            mats[M_LOW0T] = -1.0 * low.T
    lg = np.log1p(-np.exp2(-5.0 - np.arange(8)))
    ret = np.zeros((PAIRS, P, 4, P), np.float32)
    cdec = np.zeros((P, PAIRS), np.float32)
    for p in range(PAIRS):
        for h in range(2):
            g = lg[2 * p + h]
            rel = s - t
            ret[p, :, h, :] = np.where(rel >= 0, np.exp(np.maximum(rel, 0) * g), 0) * 0.125
            rows = slice(h * CH, h * CH + CH)
            ret[p, rows, 2, :] = np.exp((i + 1.0) * g)[None, :]
            ret[p, rows, 3, :] = np.exp((P - 1.0 - i) * g)[None, :] * 0.125
            cdec[rows, p] = np.exp(P * g)
    slopes = np.exp2(-8.0 * np.arange(1, 9) / 8)
    q, k = np.arange(P)[:, None], np.arange(2 * P)[None, :]
    dist = q + P - k
    win = (dist >= 0) & (dist < P)
    bias = np.zeros((PAIRS, P, 2, 2, 2 * P), np.float32)
    for p in range(PAIRS):
        for h in range(2):
            b = -slopes[2 * p + h] * dist
            bias[p, :, 0, h, :] = np.where(win, b, NEG)
            bias[p, :, 1, h, :] = np.where(win & (k >= P), b, NEG)
    invf = (10000.0 ** (-np.arange(32, dtype=np.float64) / 32)).astype(np.float32)
    counts = np.ones((4, 15), np.float32)
    for g in range(4):
        w = 2 ** (g + 1)
        counts[g, :w - 1] = w / np.arange(1.0, w)
    tab = {"cdecay": cdec, "invf": invf[i % 32][:, None], "sgn": np.where(i % 64 < 32, -1.0, 1.0)[:, None],
           "counts": np.broadcast_to(counts.reshape(1, 60), (P, 60))}
    return mats.transpose(1, 0, 2), ret, bias, {k: v.astype(np.float32) for k, v in tab.items()}


def columns(vec):
    return vec.reshape(-1, P).T


def kernel(**inputs):
    import concourse.bacc as bacc
    from concourse.bass_utils import run_bass_kernel_spmd

    f = {k: np.asarray(v) for k, v in inputs.items()}
    mats, ret, bias, tab = constants()

    def blocks(wm):
        k, n = wm.shape
        b = wm.reshape(k // P, P, n // P, P).transpose(2, 1, 0, 3).reshape(n // P, P, k)
        if k < D:
            b = np.concatenate([b, np.zeros((n // P, P, D - k), wm.dtype)], axis=2)
        return b

    w_in = blocks(f["w_in"][0])
    rw, ret_w, gates = w_in[:14], w_in[14:38], w_in[38:]
    brw, bret, wout = blocks(f["w_branch_rw"][0]), blocks(f["w_branch_ret"][0]), blocks(f["w_out"][0])
    up = blocks(f["ffn_w_up"][0])
    down = f["ffn_w_down"][0].reshape(FT, P, D)
    in2, out2 = blocks(f["w_in_2"][0]), blocks(f["w_out_2"][0])
    low = np.zeros((PAIRS, P, D), np.float32)
    for p in range(PAIRS):
        c = slice(p * P, (p + 1) * P)
        low[p, 0:CH, 0:P] = f["rw_w2"][0][:, c]
        low[p, CH:P, P:2 * P] = f["rw_a2"][0][:, c]
        low[p, :, 2 * P:3 * P] = f["rw_g2"][0][:, c]
    order = [rw[12], rw[13]]
    later = []
    for p in range(PAIRS):
        later += [ret_w[p], ret_w[4 + p], ret_w[8 + 2 * p], ret_w[9 + 2 * p], ret_w[16 + 2 * p], ret_w[17 + 2 * p]]
    later += list(gates)
    for p in range(PAIRS):
        order += [rw[p], rw[4 + p], rw[8 + p], low[p]] + later[LATER * p:LATER * (p + 1)]
    order += list(brw) + list(bret)
    order += list(wout)
    for j in range(FT):
        order += [up[j], up[FT + j]]
    order += list(down)
    for g in range(4):
        order += [in2[g], in2[4 + g]]
    order += [in2[12], in2[13]]
    for p in range(PAIRS):
        order += [in2[8 + p], in2[14 + p]]
    order += list(out2)
    w = np.stack(order)
    assert w.shape[0] == NSTORED

    mu = columns(f["rw_mu"][0])
    vecs = [columns(f[n][0]) for n in ("rw_w0", "rw_a0", "rw_k_k", "rw_k_a", "rw_r_k", "rw_lnx_w", "rw_lnx_b")]
    cw, cb = f["ffn_conv_w"][0], f["ffn_conv_b"][0]
    cw = [columns(cw[n]) for n in range(3)] + [columns(cb)]
    table = {"g_mix_pre": columns(f["norm_mix_pre"][0]), "g_mix_post": columns(f["norm_mix_post"][0]),
             "g_ffn_pre": columns(f["norm_ffn_pre"][0]), "g_ffn_post": columns(f["norm_ffn_post"][0]),
             "g2_pre": columns(f["norm_pre_2"][0]), "g2_post": columns(f["norm_post_2"][0]),
             "mu_low": mu[:, 12:14],
             "rw": np.concatenate([np.stack([mu[:, p], mu[:, 4 + p], mu[:, 8 + p]] + [v[:, p] for v in vecs], axis=1)
                                   for p in range(PAIRS)], axis=1),
             "conv": np.concatenate([np.stack([c[:, j + o] for o in (0, FT) for c in cw], axis=1)
                                     for j in range(FT)], axis=1),
             "pscale": columns(f["pool_scale_2"][0]),
             "sinks": np.broadcast_to(f["attn_sinks_2"][0][None, :], (P, 8))}
    table.update(tab)
    par = np.concatenate([table[n] for n in COLS], axis=1)

    def feature_major(x):
        return x.T.reshape(KT, P, T).transpose(1, 0, 2)

    given = {"xt": feature_major(f["x"][0]), "pos": np.broadcast_to(f["positions"], (P, T)), "w": w, "par": par,
             "mats": mats, "ret_tab": ret, "att_bias": bias, "pool_w": f["pool_w_2"][0]}
    nc = bacc.Bacc("TRN2", target_bir_lowering=False, num_devices=1)
    arrays, args = {}, []
    for name, a in given.items():
        a = np.ascontiguousarray(a)
        arrays[name] = a
        args.append(nc.dram_tensor(name, a.shape, mybir.dt.from_np(a.dtype), kind="ExternalInput").ap())
    args.append(nc.dram_tensor("out", (P, KT, T), F32, kind="ExternalOutput").ap())
    build(nc, *args)
    r = run_bass_kernel_spmd(nc, [arrays], core_ids=[0])
    return r.results[0]["out"].transpose(1, 0, 2).reshape(D, T).T.reshape(1, T, D)
```

```python
from contextlib import ExitStack

import numpy as np

import concourse.bass as bass
from concourse import mybir

F32 = mybir.dt.float32
F32R = mybir.dt.float32r
I32 = mybir.dt.int32
ALU = mybir.AluOpType
ACT = mybir.ActivationFunctionType
AX_X = mybir.AxisListType.X

P = 128
T = 1024
HALF = 512
D = 1024
KT = D // P
FF = 2816
FT = FF // P
PAIRS = 4
CH = 64
GROUPS = 4
LEVELS = 6
NB = T // P
C0 = float(np.exp(-0.5))
TWO_PI_A = 6.28125
TWO_PI_B = float(np.float32(2 * np.pi - 6.28125))
TWO_PI_C = float(2 * np.pi - 6.28125 - np.float32(2 * np.pi - 6.28125))
MAGIC = float(1.5 * 2 ** 23)
NEG = -1e30

COLS = {}
_n = 0
for _name, _w in (("g_mix_pre", 8), ("g_mix_post", 8), ("g_ffn_pre", 8), ("g_ffn_post", 8), ("g2_pre", 8),
                  ("g2_post", 8), ("mu_low", 2), ("rw", 40), ("conv", 176), ("pscale", 4), ("sinks", 8),
                  ("cdecay", 4), ("invf", 1), ("sgn", 1), ("counts", 60)):
    COLS[_name] = _n
    _n += _w
NPAR = _n

NORM = {n: i for i, n in enumerate(("a", "out", "pre", "down", "h2", "fin"))}
SPLIT_BEFORE = {"yrw": 0, "yret": 4, "merged": 12, "cat": 20}

M_ID, M_CENT, M_BLK, M_STRICT, M_INCL, M_LOW0T, M_LVL = 0, 1, 2, 3, 4, 5, 6
NMAT = M_LVL + LEVELS
M_CENT_RET = NMAT

LATER = 10
B_LORA, T_LORA = 0, 0
B_RW, T_RW = 2, 2
RW_B, RW_T = 4 + LATER, 6 + LATER
B_BRW, T_BRW = B_RW + RW_B * PAIRS, T_RW + RW_T * PAIRS
B_MRG, T_MRG = B_BRW + KT, T_BRW + KT
B_OUT, T_OUT = B_MRG + KT, T_MRG + KT
B_UP, T_UP = B_OUT + 8, T_OUT + 8
B_DOWN = B_UP + 2 * FT
B_P2, T_P2 = B_DOWN + 2 * FT, T_UP + 2 * FT
B_O2, T_O2 = B_P2 + 18, T_P2 + 18
NBLK = B_O2 + 8
S_GRW, S_GRET, S_BRW = 24, 32, 40
BY_POOL = (0, 2, 4)
NSTORED = NBLK - FT


def build(nc, xt, pos, w, par, mats, ret_tab, att_bias, pool_w, out):
    later_d = nc.dram_tensor("later_scratch", [48, P, T], F32).ap()
    yrw_d = nc.dram_tensor("yrw_scratch", [P, PAIRS, T], F32).ap()
    rot_d = nc.dram_tensor("rotary_scratch", [P, 2, T], F32).ap()
    h_d = nc.dram_tensor("h_scratch", [P, KT, T], F32).ap()

    with ExitStack() as ctx:
        base = [((nc.sbuf_base + 31) // 32) * 32]

        def at(name, offset, shape, dt=F32):
            return nc.alloc_sbuf_tensor_at(name, shape, dt, offset=offset)

        def sb(name, shape, dt=F32):
            size = 4 * int(np.prod(shape[1:]))
            t = at(name, base[0], shape, dt)
            base[0] += (size + 31) // 32 * 32
            return t

        wraw = sb("wraw", [P, 2, 1024])
        whi = sb("whi", [P, 2, 1024], F32R)
        wlo = sb("wlo", [P, 2, 1024], F32R)
        mat_at = base[0]
        mat = sb("mat", [P, NMAT, P])
        prm = sb("prm", [P, NPAR])
        pp = sb("pp", [P, 15])
        cp = sb("cp", [P, 8])
        ec = sb("ec", [P, 16])
        id2 = sb("id2", [P, CH])
        sm = sb("sm", [P, 24])
        x_at = base[0]
        xhi = sb("xhi", [P, KT, T], F32R)
        xlo = sb("xlo", [P, KT, T], F32R)
        arena = base[0]
        assert arena + 28 * 4096 <= nc.sbuf_usable_end, (arena + 28 * 4096, nc.sbuf_usable_end)

        def tiles(name, i, shape, dt=F32):
            return at(name, arena + 4096 * i, shape, dt)

        def m(i):
            return mat[:, i, :]

        def many(i, n):
            return m(i).unsqueeze(1).broadcast_to([P, n, P])

        def par_col(name, j=0):
            c = COLS[name] + j
            return prm[:, c:c + 1]

        psg = [ctx.enter_context(nc.psum_tensor(f"psg{b}", [P, T], F32)) for b in range(2)]
        psa = ctx.enter_context(nc.psum_tensor("psa", [P, 2, HALF], F32))
        psb = ctx.enter_context(nc.psum_tensor("psb", [P, 2, HALF], F32))
        bank = [psa[:, 0, :], psa[:, 1, :], psb[:, 0, :], psb[:, 1, :]]

        def flat(ps):
            return ps[:].rearrange("p a b -> p (a b)")

        sems = {}

        def sem(name):
            if name not in sems:
                sems[name] = ctx.enter_context(nc.semaphore(name))
            return sems[name]

        w_landed = [sem("w_landed0"), sem("w_landed1")]
        w_ready = sem("w_ready")
        w_used = sem("w_used")
        g_full = sem("g_full")
        g_free = [sem("g_free0"), sem("g_free1")]
        go = sem("go")
        consts_in = sem("consts_in")

        xres = tiles("xres", 0, [P, KT, T])
        pa_sq = tiles("pa_sq", 8, [P, 2, T])
        pa_acc = tiles("pa_acc", 10, [P, T])
        pa_rstd = tiles("pa_rstd", 11, [P, T])
        pa_tmp = tiles("pa_tmp", 12, [P, 2, T])

        rot, ang, kq = tiles("rot", 14, [P, 2, T]), tiles("ang", 16, [P, T]), tiles("kq", 17, [P, T])
        posi = tiles("posi", 20, [P, T], I32)
        stage = tiles("stage", 0, [P, 2, T])
        ATH, ATL = tiles("rw_ATH", 2, [P, 4, P], F32R), at("rw_ATL", arena + 2 * 4096 + 2048, [P, 4, P], F32R)
        M, MT = tiles("rw_M", 3, [P, 4, P], F32R), at("rw_MT", arena + 3 * 4096 + 2048, [P, 4, P], F32R)
        ta_hi, ta_lo = tiles("ta_hi", 4, [P, T], F32R), tiles("ta_lo", 5, [P, T], F32R)
        sg_hi, sg_lo = tiles("sg_hi", 6, [P, T], F32R), tiles("sg_lo", 7, [P, T], F32R)
        R, K, V, KK, SG, A, CS, E1, EN, G, BON = (
            tiles(f"rw_{n}", 8 + i, [P, T]) for i, n in enumerate("R K V KK SG A CS E1 EN G BON".split()))
        KR = tiles("rw_KR", 19, [P, NB, 2, P])
        TM = tiles("rw_TM", 21, [P, T])
        SC = tiles("rw_SC", 22, [P, 4, 768])
        s_at = arena + 25 * 4096
        VT = at("rw_VT", s_at, [P, 4, CH])
        Z = at("rw_Z", s_at + 1024, [P, 4, P])
        GH = at("rw_GH", s_at + 3072, [P, 4, P])
        XM = at("rw_XM", s_at + 5120, [P, 4, P], F32R)
        MTF = at("rw_MTF", s_at + 7168, [P, 4, P])
        idr = at("rw_idr", s_at + 9216, [P, P], F32R)
        e_at = arena + 15 * 4096
        RT = at("rw_RT", e_at, [P, 2, P])
        PT = at("rw_PT", e_at + 1024, [P, 2, P])
        ST = at("rw_ST", e_at + 2048, [P, 2, CH])
        YB = EN
        DG = R
        BE, KE = A, CS

        def spare(name, i, shape, dt=F32):
            return at(name, x_at + (4096 * (4 + i) if i < 4 else 32768 + 4096 * i), shape, dt)

        yret = tiles("yret", 0, [P, KT, T])
        yrw = tiles("yrw", 4, [P, PAIRS, T])
        rott = tiles("rott", 8, [P, 2, T])
        rstage = tiles("rstage", 10, [P, 2, T])
        RV, RG = tiles("RV", 12, [P, 2, T]), tiles("RG", 14, [P, 2, T])
        RQD, RKD = tiles("RQD", 16, [P, T]), tiles("RKD", 17, [P, T])
        RGS = tiles("RGS", 20, [P, 2, T])
        RVT = tiles("RVT", 22, [P, 2, NB, P])
        RKT, RS = tiles("RKT", 24, [P, NB, P]), tiles("RS", 25, [P, NB, P])
        RP, RC = [tiles("RP0", 26, [P, NB, P]), spare("RP1", 6, [P, NB, P])], tiles("RC", 27, [P, P])
        rraw = [spare("rraw0", 0, [P, 2, T]), tiles("rraw1", 18, [P, 2, T])]
        rswp = spare("rswp", 2, [P, 2, T])
        RE = [spare("RE0", 4, [P, T]), spare("RE1", 7, [P, T])]
        RTAB = spare("RTAB", 5, [P, 2, 4, P])

        mgr, mgt, mbr = tiles("mgr", 8, [P, 2, T]), tiles("mgt", 10, [P, 2, T]), tiles("mbr", 12, [P, 2, T])
        merged = tiles("merged", 0, [P, KT, T])

        oy = tiles("oy", 8, [P, KT, T])
        osq = tiles("osq", 16, [P, 2, T])
        oacc, orstd = tiles("oacc", 18, [P, T]), tiles("orstd", 19, [P, T])
        oh = tiles("oh", 20, [P, KT, T])

        ff = tiles("ff", 0, [P, FT, T])
        frs = tiles("frs", 27, [P, T])
        fg, fv = tiles("fg", 22, [P, 2, T]), tiles("fv", 24, [P, 2, T])
        dy = at("dy", x_at, [P, KT, T])
        dh = at("dh", x_at + 32768, [P, KT, T])
        fhi, flo = tiles("fhi", 26, [P, 2, HALF], F32R), tiles("flo", 27, [P, 2, HALF], F32R)
        dsq = tiles("dsq", 24, [P, 2, HALF])
        dacc, drstd = tiles("dacc", 25, [P, T]), tiles("drstd", 26, [P, T])
        h2 = tiles("h2", 0, [P, KT, T])
        dsq8 = tiles("dsq8", 8, [P, KT, T])

        cat = tiles("cat", 8, [P, KT, T])
        pu, ps2 = tiles("pu", 16, [P, T]), tiles("ps2", 17, [P, T])
        ps4, pgt = tiles("ps4", 18, [P, T]), tiles("pgt", 19, [P, T])
        pgs = tiles("pgs", 21, [P, T])
        pw = tiles("pw", 20, [P, P])
        kd = tiles("kd", 16, [P, 2, T + P])
        vt2 = at("vt2", arena + 16 * 4096 + 9216, [P, NB + 1, P])
        ab = [tiles(f"ab{u}", 20 + 7 * u, [P, 2, 2, 2 * P]) for u in range(2)]
        aq = tiles("aq", 21, [P, 2, T])
        kv_f, kk_f = tiles("kv_f", 21, [P, T]), tiles("kk_f", 22, [P, T])
        rs2 = drstd
        gsig = at("gsig", mat_at + 4 * P * M_STRICT, [P, T])
        ap_ = tiles("ap_", 23, [P, 2, 4, 2 * P])
        apt = tiles("apt", 25, [P, 4, 2, P])
        y2 = tiles("y2", 16, [P, KT, T])
        q2sq = tiles("q2sq", 24, [P, 2, T])
        q2acc, q2rstd = tiles("q2acc", 26, [P, T]), tiles("q2rstd", 27, [P, T])

        block = ctx.enter_context(nc.Block())

        @block.sync
        def _(sp):
            def stream(first, end, shift):
                with sp.Fori(first // 2, end // 2) as i:
                    for u in range(2):
                        sp.wait_ge(w_ready, 2 * i + u + 1)
                        sp.dma_start(wraw[:, u, :], w[bass.ds(2 * i + u - shift, 1)].rearrange("n p c -> p (n c)")
                                     ).then_inc(w_landed[u], 16)

            stream(0, B_DOWN + FT, 0)
            stream(B_DOWN + FT, NBLK, FT)

        @block.gpsimd
        def _(pool):
            pool.sem_inc(w_ready, 2)

            def split_block(i, u, width=D):
                pool.wait_ge(w_landed[u], 16 * i + 16)
                pool.wait_ge(w_used, 2 * i + u + 1)
                pool.sem_inc(go, 1)
                pool.tensor_copy(whi[:, u, 0:width], wraw[:, u, 0:width])
                pool.drain()
                pool.tensor_tensor(wlo[:, u, 0:width], wraw[:, u, 0:width], whi[:, u, 0:width].bitcast(F32),
                                   ALU.subtract).then_inc(w_ready, 1)

            def split_blocks(first, end, width=D):
                with pool.Fori(first // 2, end // 2) as i:
                    for u in range(2):
                        split_block(i, u, width)

            def add_squares(name, sq, acc):
                pool.wait_ge(sem(name + "_sq"), 2)
                pool.tensor_tensor(acc[:, :], sq[:, 0, :], sq[:, 1, :], ALU.add).then_inc(sem(name + "_added"), 2)
                for j in range(2, KT):
                    pool.drain()
                    pool.wait_ge(sem(name + "_sq"), j + 1)
                    pool.tensor_tensor(acc[:, :], acc[:, :], sq[:, j, :], ALU.add).then_inc(sem(name + "_added"), 1)

            pool.memset(pp[:, 14:15], 1.0)
            pool.memset(pa_acc[:, :], 0.0)
            pool.drain()
            pool.sem_inc(sem("a_added"), 2)
            for j in range(KT // 2):
                pool.drain()
                pool.wait_ge(sem("a_sq"), j + 1)
                pool.tensor_tensor(pa_acc[:, :], pa_acc[:, :], pa_sq[:, j % 2, :], ALU.add
                                   ).then_inc(sem("a_added"), 1)
            split_blocks(0, B_BRW)
            split_blocks(B_BRW, B_MRG, PAIRS * P)
            split_blocks(B_MRG, B_UP)
            for u in range(2):
                split_block(B_UP // 2, u)
            add_squares("pre", oy, oacc)
            split_blocks(B_UP + 2, B_DOWN)
            with pool.Fori(0, FT) as i:
                for u in range(2):
                    pool.wait_ge(sem("w_high"), 2 * i + u + 1)
                    pool.sem_inc(go, 1)
                    pool.tensor_tensor(wlo[:, u, :], wraw[:, u, :], whi[:, u, :].bitcast(F32),
                                       ALU.subtract).then_inc(w_ready, 1)
            for u in range(2):
                split_block(B_P2 // 2, u)
            add_squares("h2", dsq8, dacc)
            split_blocks(B_P2 + 2, NBLK)
            for j in BY_POOL:
                pool.wait_ge(sem("y_scaled"), j + 1)
                pool.tensor_tensor(y2[:, j, :], y2[:, j, :], h2[:, j, :], ALU.add).then_inc(sem("y_pool"), 1)

        @block.tensor
        def _(pe):
            pe.sem_inc(w_used, 1)

            def product(n, t, slot, b, use, rhs_hi, rhs_lo, kts=KT, col=0, first=True):
                pe.wait_ge(w_ready, n + 3)
                pe.wait_ge(g_free[b], use + 1)
                for half in range(2):
                    cols = slice(half * HALF, (half + 1) * HALF)
                    for k in range(kts):
                        w_cols = slice(col + k * P, col + (k + 1) * P)
                        mm = pe.matmul(psg[b][:, cols], whi[:, slot, w_cols], rhs_hi(k, cols),
                                       start=(k == 0), stop=False)
                        if first and half == 0 and k == 0:
                            mm.then_inc(w_used, 1)
                        pe.matmul(psg[b][:, cols], whi[:, slot, w_cols], rhs_lo(k, cols), start=False, stop=False)
                        mm = pe.matmul(psg[b][:, cols], wlo[:, slot, w_cols], rhs_hi(k, cols),
                                       start=False, stop=(k == kts - 1))
                mm.then_inc(g_full, 1)

            def x_h(k, cols):
                return xhi[:, k, cols]

            def x_l(k, cols):
                return xlo[:, k, cols]

            def sum_rows(ps, which, src):
                for half in range(2):
                    mm = pe.matmul(ps[:, half, :], m(which), src[:, half * HALF:(half + 1) * HALF],
                                   start=True, stop=True)
                return mm

            def streamed(b0, t0, split, before, early=0, late=None):
                def feature(u, k, begins=False):
                    for half in range(2):
                        cols = slice(half * HALF, (half + 1) * HALF)
                        w_cols = slice(k * P, (k + 1) * P)
                        mm = pe.matmul(psg[u][:, cols], whi[:, u, w_cols], xhi[:, k, cols], start=(k == 0), stop=False)
                        if begins and half == 0:
                            mm.then_inc(w_used, 1)
                        pe.matmul(psg[u][:, cols], whi[:, u, w_cols], xlo[:, k, cols], start=False, stop=False)
                        mm = pe.matmul(psg[u][:, cols], wlo[:, u, w_cols], xhi[:, k, cols],
                                       start=False, stop=(k == KT - 1))
                    if k == KT - 1:
                        mm.then_inc(g_full, 1)

                def ready(u):
                    pe.wait_ge(w_ready, b0 + u + 3)
                    pe.wait_ge(g_free[u], t0 // 2 + 1)

                ready(0)
                for k in range(KT):
                    pe.wait_ge(split, before + k + 1)
                    feature(0, k, begins=(k == 0))
                    j = k - (KT - early)
                    if j >= 0:
                        if j == 0:
                            ready(1)
                        feature(1, j)
                if not early:
                    ready(1)
                for k in range(early, KT):
                    if late and k == KT - 2:
                        pe.wait_ge(sem(late[0] + "_added"), KT)
                        token_sums(late[1]).then_inc(sem("norm_tot"), 1)
                    feature(1, k, begins=(k == early))
                if late:
                    pe.wait_ge(sem("norm_exp"), NORM[late[0]] + 1)
                    spread(late[2]).then_inc(sem("norm_rep"), 1)

            def token_sums(src, head_cols=False):
                w_sum = m(M_BLK)[:, CH - 1:CH + 1] if head_cols else pp[:, 14:15]
                n = 2 if head_cols else 1
                for c in range(NB):
                    mm = pe.matmul(psa[:, 0, n * c:n * c + n], src[:, c * P:c * P + P], w_sum, start=True, stop=True)
                return mm

            def spread(src):
                for c in range(NB):
                    mm = pe.transpose(psa[:, c // 4, (c % 4) * P:(c % 4 + 1) * P], src[:, c * P:c * P + P], m(M_ID))
                return mm

            def norm_factor(acc, rstd, name, adds=KT):
                pe.wait_ge(sem(name + "_added"), adds + 2)
                token_sums(acc).then_inc(sem("norm_tot"), 1)
                pe.wait_ge(sem("norm_exp"), NORM[name] + 1)
                spread(rstd).then_inc(sem("norm_rep"), 1)

            pe.wait_ge(consts_in, 16)
            norm_factor(pa_acc, pa_rstd, "a")

            streamed(B_LORA, T_LORA, sem("norm_split"), 0, early=4)

            with pe.Fori(0, PAIRS) as i:
                def later_products():
                    for f in range(LATER):
                        j = 6 + f
                        pe.wait_ge(w_ready, B_RW + RW_B * i + 4 + f + 3)
                        pe.wait_ge(g_free[j % 2], 8 * i + j // 2 + 2)
                        slot, ps = f % 2, psg[j % 2]
                        for half in range(2):
                            cols = slice(half * HALF, (half + 1) * HALF)
                            for k in range(KT):
                                w_cols = slice(k * P, (k + 1) * P)
                                mm = pe.matmul(ps[:, cols], whi[:, slot, w_cols], xhi[:, k, cols],
                                               start=(k == 0), stop=False)
                                if half == 0 and k == 0:
                                    mm.then_inc(w_used, 1)
                                yield
                                pe.matmul(ps[:, cols], whi[:, slot, w_cols], xlo[:, k, cols], start=False, stop=False)
                                yield
                                mm = pe.matmul(ps[:, cols], wlo[:, slot, w_cols], xhi[:, k, cols],
                                               start=False, stop=(k == KT - 1))
                                if half == 1 and k == KT - 1:
                                    mm.then_inc(g_full, 1)
                                yield

                later = later_products()

                def fill(n):
                    for _ in range(n):
                        next(later)

                for j in range(3):
                    product(B_RW + RW_B * i + j, T_RW + j, j % 2, j % 2, 8 * i + 1 + j // 2, x_h, x_l)
                pe.wait_ge(sem("lora_split"), 2)
                for j in range(3, 6):
                    hi, lo = (ta_hi, ta_lo) if j < 5 else (sg_hi, sg_lo)
                    product(B_RW + RW_B * i + 3, T_RW + j, 1, j % 2, 8 * i + 1 + j // 2, lambda k, c, s=hi: s[:, c],
                            lambda k, c, s=lo: s[:, c], kts=1, col=(j - 3) * P, first=(j == 3))
                fill(8)
                pe.wait_ge(sem("hd_sq"), 2 * i + 1)
                token_sums(TM, True).then_inc(sem("hd_sum"), 1)
                fill(10)
                pe.wait_ge(sem("hd_exp"), 2 * i + 1)
                spread(TM).then_inc(sem("hd_rep"), 1)
                fill(14)
                pe.wait_ge(sem("rk_prod"), i + 1)
                sum_rows(psb, M_BLK, TM).then_inc(sem("bonus_sum"), 1)
                fill(38)
                pe.wait_ge(sem("rw_prep"), i + 1)
                for g in range(GROUPS):
                    if g:
                        pe.wait_ge(sem("y_out"), 8 * i + 2 * g)
                        pe.wait_ge(sem("s_new"), 16 * i + 4 * g)
                        pe.sem_inc(go, 1)
                    for tt in range(2):
                        tl = 2 * g + tt
                        for h in range(2):
                            rows = slice(h * CH, h * CH + CH)
                            kr = KR[rows, tl, :, :].rearrange("p a b -> p (a b)")
                            pe.matmul(bank[2 * tt + h][:, 0:256], KK[rows, tl * P:tl * P + P], kr,
                                      start=True, stop=True)
                            pe.matmul(bank[2 * tt + h][:, 256:512], K[rows, tl * P:tl * P + P], kr,
                                      start=True, stop=True).then_inc(sem("scores"), 1)
                    for tt in range(2):
                        tl = 2 * g + tt
                        pe.wait_ge(sem("sc_out"), 16 * i + 4 * g + tt + 1)
                        pe.matmul(bank[tt][:, 2 * P:3 * P], V[:, tl * P:tl * P + P], m(M_CENT), start=True, stop=True)
                        for j, src in ((0, BE[:, tl * P:tl * P + P]), (1, KE[:, tl * P:tl * P + P]),
                                       (3, KR[:, tl, 0, :])):
                            mm = pe.transpose(bank[tt][:, j * P:j * P + P], src, m(M_ID))
                        mm.then_inc(sem("tr_full"), 1)
                    fill(6)
                    pe.wait_ge(sem("sc_out"), 16 * i + 4 * g + 4)
                    for q in range(4):
                        mm = pe.transpose(bank[2][:, q * P:q * P + P], SC[:, q, 0:P], m(M_ID))
                    mm.then_inc(sem("x_full"), 1)
                    fill(5)
                    pe.wait_ge(sem("tr_act"), 8 * i + 2 * g + 2)
                    for q in range(4):
                        mm = pe.matmul(bank[1][:, q * CH:q * CH + CH], SC[:, q, 384:512], VT[:, q, :],
                                       start=True, stop=True)
                    mm.then_inc(sem("dv_full"), 1)
                    fill(5)
                    for lv in range(1, LEVELS):
                        if lv == 1:
                            pe.wait_ge(sem("m_init"), 4 * i + g + 1)
                        else:
                            pe.wait_ge(sem("m_act"), 20 * i + 5 * g + lv - 1)
                            pe.wait_ge(sem("mt_dve"), 16 * i + 4 * g + lv - 1)
                        for q in range(4):
                            mm = pe.matmul(bank[2][:, q * P:q * P + P], ATH[:, q, :], M[:, q, :],
                                           start=True, stop=True)
                        mm.then_inc(sem("x_full"), 1)
                        fill(5)
                        pe.wait_ge(sem("x_out"), 20 * i + 5 * g + lv)
                        pe.matmul(bank[3], idr[:, :], M[:].rearrange("p q c -> p (q c)"), start=True, stop=False)
                        for q in range(4):
                            mm = pe.matmul(bank[3][:, q * P:q * P + P], MT[:, q, :], XM[:, q, :],
                                           start=False, stop=(q == 3))
                        mm.then_inc(sem("m_full"), 1)
                        if lv < LEVELS - 1:
                            pe.matmul(bank[0], idr[:, :], MT[:].rearrange("p q c -> p (q c)"), start=True, stop=False)
                            for q in range(4):
                                mm = pe.matmul(bank[0][:, q * P:q * P + P], XM[:, q, :], MT[:, q, :],
                                               start=False, stop=(q == 3))
                            mm.then_inc(sem("mt_full"), 1)
                        fill(5)
                    pe.wait_ge(sem("m_act"), 20 * i + 5 * g + 5)
                    pe.matmul(bank[2], idr[:, :], M[:].rearrange("p q c -> p (q c)"), start=True, stop=False)
                    for q in range(4):
                        o = bank[2][:, q * P:q * P + P]
                        pe.matmul(o, ATH[:, q, :], M[:, q, :], start=False, stop=False)
                        mm = pe.matmul(o, ATL[:, q, :], M[:, q, :], start=False, stop=(q == 3))
                    mm.then_inc(sem("e_full"), 1)
                    for q in range(4):
                        mm = pe.transpose(bank[0][:, q * P:q * P + P], M[:, q, :].bitcast(F32), m(M_ID))
                    mm.then_inc(sem("mt0_full"), 1)
                    fill(5)
                    pe.wait_ge(sem("e_ready"), 4 * i + g + 1)
                    pe.wait_ge(sem("mt0_ready"), 4 * i + g + 1)
                    for q in range(4):
                        mm = pe.matmul(bank[3][:, q * P:q * P + P], XM[:, q, :], MT[:, q, :], start=True, stop=True)
                    mm.then_inc(sem("fin_full"), 1)
                    fill(5)
                    pe.wait_ge(sem("mtf_ready"), 4 * i + g + 1)
                    pe.wait_ge(sem("z_ready"), 4 * i + g + 1)
                    for q in range(4):
                        mm = pe.matmul(bank[2][:, q * P:q * P + P], MTF[:, q, :], Z[:, q, :], start=True, stop=True)
                    mm.then_inc(sem("gh_full"), 1)
                    fill(5)
                    pe.wait_ge(sem("gh_ready"), 4 * i + g + 1)
                    for q in range(4):
                        h = q % 2
                        mm = pe.matmul(bank[3][h * CH:h * CH + CH, (q // 2) * 256:(q // 2) * 256 + 256],
                                       GH[:, q, 0:CH], SC[:, q, P:P + 256], start=True, stop=True)
                    mm.then_inc(sem("rp_full"), 1)
                    fill(3)
                    pe.wait_ge(sem("rt_pt"), 4 * i + g + 1)
                    for tt in range(2):
                        psy = bank[0] if tt == 0 else bank[3]
                        for h in range(2):
                            q, rows = 2 * tt + h, slice(h * CH, h * CH + CH)
                            pe.matmul(psy[rows, 0:P], GH[:, q, CH:P], SC[:, q, P:2 * P], start=True, stop=False)
                            pe.matmul(psy[rows, 0:P], VT[:, q, :], SC[:, q, 512:640], start=False, stop=False)
                        for c in range(2):
                            step = 4 * g + 2 * tt + c
                            pss = bank[1 + c]
                            if step >= 2:
                                pe.wait_ge(sem("s_new"), 16 * i + step - 1)
                                pe.sem_inc(go, 1)
                            for h in range(2):
                                q, rows = 2 * tt + h, slice(h * CH, h * CH + CH)
                                pe.matmul(pss[rows, 0:CH], SC[:, q, 256 + c * CH:256 + c * CH + CH],
                                          GH[:, q, CH:P], start=True, stop=False)
                                pe.matmul(pss[rows, 0:CH], SC[:, q, 640 + c * CH:640 + c * CH + CH],
                                          VT[:, q, :], start=False, stop=False)
                            if step >= 1:
                                pe.wait_ge(sem("s_new"), 16 * i + step)
                                pe.sem_inc(go, 1)
                            for h in range(2):
                                rows = slice(h * CH, h * CH + CH)
                                mm = pe.matmul(pss[rows, 0:CH], PT[rows, tt, c * CH:c * CH + CH],
                                               ST[rows, step % 2, :], start=False, stop=True)
                            mm.then_inc(sem("s_full"), 1)
                            for h in range(2):
                                rows = slice(h * CH, h * CH + CH)
                                mm = pe.matmul(psy[rows, c * CH:c * CH + CH], ST[rows, step % 2, :],
                                               RT[rows, tt, c * CH:c * CH + CH], start=False, stop=(c == 1))
                            if c == 1:
                                mm.then_inc(sem("y_full"), 1)
                            fill(1 if step % 4 < 3 else 4)
                pe.wait_ge(sem("y_out"), 8 * i + 8)
                fill(13)
                pe.wait_ge(sem("hd_sq"), 2 * i + 2)
                token_sums(TM, True).then_inc(sem("hd_sum"), 1)
                fill(20)
                pe.wait_ge(sem("hd_exp"), 2 * i + 2)
                spread(TM).then_inc(sem("hd_rep"), 1)
                fill(13)
                assert next(later, 'none left') == 'none left'

            def branch_products():
                for j in range(KT):
                    pe.wait_ge(w_ready, B_BRW + j + 3)
                    if j:
                        pe.wait_ge(sem("br_free"), j)
                    else:
                        pe.wait_ge(g_free[0], T_BRW // 2 + 1)
                        pe.wait_ge(sem("op_split"), SPLIT_BEFORE["yrw"] + PAIRS)
                    for half in range(2):
                        cols = slice(half * HALF, (half + 1) * HALF)
                        for k in range(PAIRS):
                            w_cols = slice(k * P, (k + 1) * P)
                            mm = pe.matmul(psg[0][:, cols], whi[:, j % 2, w_cols], xhi[:, k, cols],
                                           start=(k == 0), stop=False)
                            if half == 0 and k == 0:
                                mm.then_inc(w_used, 1)
                            yield
                            pe.matmul(psg[0][:, cols], whi[:, j % 2, w_cols], xlo[:, k, cols], start=False, stop=False)
                            yield
                            mm = pe.matmul(psg[0][:, cols], wlo[:, j % 2, w_cols], xhi[:, k, cols],
                                           start=False, stop=(k == PAIRS - 1))
                            if half == 1 and k == PAIRS - 1:
                                mm.then_inc(g_full, 1)
                            yield

            branch = branch_products()

            def fill_branch(k):
                for _ in range(k):
                    next(branch)

            psb_t = psb[:].rearrange("p a (b c) -> p (a b) c", c=P)
            psa_t = psa[:].rearrange("p a (b c) -> p (a b) c", c=P)
            psc_t = psg[1][:].rearrange("p (b c) -> p b c", c=P)
            out_t = [psb_t, psc_t]

            def ret_values(p, h):
                if h == 0:
                    pe.wait_ge(sem("rv_in"), 16 * p + 32)
                    if p:
                        pe.wait_ge(sem("yret_done"), 2 * p - 1)
                else:
                    pe.wait_ge(sem("rv_tm"), 2 * p + 1)
                for c in range(NB):
                    mm = pe.matmul(psb_t[:, c, :], RV[:, h, c * P:c * P + P], RC[:, :], start=True, stop=True)
                mm.then_inc(sem("rv_tr"), 1)

            def ret_keys(p):
                pe.wait_ge(sem("rv_tm"), 2 * p + 2)
                pe.wait_ge(sem("rkd"), p + 1)
                for c in range(NB):
                    mm = pe.transpose(psb_t[:, c, :], RKD[:, c * P:c * P + P], m(M_ID))
                mm.then_inc(sem("rk_tr"), 1)

            def ret_sums(p, h):
                pe.wait_ge(sem("rgn_sq"), 2 * p + h + 1)
                token_sums(RE[h]).then_inc(sem("rgn_sum"), 1)

            def ret_spread(p, h):
                pe.wait_ge(sem("rgn_exp"), 2 * p + h + 1)
                spread(RE[h]).then_inc(sem("rgn_rep"), 1)

            ret_values(0, 0)
            ret_values(0, 1)
            ret_keys(0)
            for p in range(PAIRS):
                q_k = rraw[p % 2]
                pe.wait_ge(sem("rk_tm"), p + 1)
                for c in range(NB):
                    for h in range(2):
                        mm = pe.matmul(psb_t[h * CH:h * CH + CH, c, :], RKT[:, c, h * CH:h * CH + CH],
                                       RVT[:, h, c, :], start=True, stop=True)
                mm.then_inc(sem("kv_full"), 1)
                if p:
                    pe.wait_ge(sem("yret_done"), 2 * p)
                else:
                    pe.wait_ge(sem("rqd"), 1)
                for h in range(2):
                    rows = slice(h * CH, h * CH + CH)
                    for c in range(NB):
                        mm = pe.matmul((psa_t, psc_t)[h][:, c, :], q_k[rows, 1, c * P:c * P + P],
                                       q_k[rows, 0, c * P:c * P + P], start=True, stop=True)
                    mm.then_inc(sem("rs_full"), 1)
                    if h == 0:
                        fill_branch(12)
                for h in range(2):
                    rows = slice(h * CH, h * CH + CH)
                    if h == 0:
                        pe.wait_ge(sem("r_states"), p + 1)
                        pe.wait_ge(sem("rqd"), p + 1)
                    pe.wait_ge(sem("rs_ready"), 2 * p + h + 1)
                    for c in range(NB):
                        mm = pe.matmul(out_t[h][:, c, :], RVT[:, h, c, :], RP[h][:, c, :], start=True, stop=(c == 0))
                        if c:
                            mm = pe.matmul(out_t[h][:, c, :], RS[rows, c, :], RQD[rows, c * P:c * P + P],
                                           start=False, stop=True)
                    mm.then_inc(sem("ro_full"), 1)
                    if h == 0:
                        fill_branch(12)
                ret_sums(p, 0)
                fill_branch(12)
                ret_spread(p, 0)
                fill_branch(12)
                if p + 1 < PAIRS:
                    ret_values(p + 1, 0)
                pe.wait_ge(sem("yret_done"), 2 * p + 1)
                ret_sums(p, 1)
                if p + 1 < PAIRS:
                    ret_values(p + 1, 1)
                ret_spread(p, 1)
                if p + 1 < PAIRS:
                    ret_keys(p + 1)

            def plain(b0, t0, pairs, first=0):
                with pe.Fori(first, pairs) as i:
                    for u in range(2):
                        product(b0 + 2 * i + u, t0 + u, u, u, t0 // 2 + i, x_h, x_l)

            streamed(B_MRG, T_MRG, sem("op_split"), SPLIT_BEFORE["yret"])
            plain(B_MRG, T_MRG, KT // 2, 1)

            streamed(B_OUT, T_OUT, sem("op_split"), SPLIT_BEFORE["merged"])
            plain(B_OUT, T_OUT, KT // 2, 1)
            norm_factor(oacc, orstd, "out")
            streamed(B_UP, T_UP, sem("norm_split"), KT, early=4, late=("pre", oacc, orstd))
            plain(B_UP, T_UP, FT, 1)
            banks = [psg[0][:, 0:HALF], psg[0][:, HALF:T], psg[1][:, 0:HALF], psg[1][:, HALF:T]] + bank

            def down(n, done, u, start, stop, after_copy=False):
                pe.wait_ge(w_ready, n + 3)
                pe.wait_ge(sem("f_split"), done + 1)
                for j in range(KT):
                    w_cols = slice(j * P, j * P + P)
                    if after_copy:
                        pe.wait_ge(sem("down_out"), j + 1)
                    mm = pe.matmul(banks[j], whi[:, u, w_cols], fhi[:, u, :], start=start, stop=False)
                    if j == 0:
                        mm.then_inc(w_used, 1)
                    pe.matmul(banks[j], whi[:, u, w_cols], flo[:, u, :], start=False, stop=False)
                    mm = pe.matmul(banks[j], wlo[:, u, w_cols], fhi[:, u, :], start=False, stop=stop)
                mm.then_inc(sem("f_used"), 1)

            pe.wait_ge(g_free[0], T_P2 // 2 + 1)
            pe.wait_ge(g_free[1], T_P2 // 2 + 1)
            for half in range(2):
                n0, k0 = B_DOWN + half * FT, half * FT
                down(n0, k0, 0, True, False, after_copy=(half == 1))
                down(n0 + 1, k0 + 1, 1, False, False)
                with pe.Fori(1, FT // 2 - 1) as i:
                    for u in range(2):
                        down(n0 + 2 * i + u, k0 + 2 * i + u, u, False, False)
                down(n0 + FT - 2, k0 + FT - 2, 0, False, False)
                down(n0 + FT - 1, k0 + FT - 1, 1, False, True)
            pe.wait_ge(sem("down_sq"), 2 * KT)
            norm_factor(dacc, drstd, "down", 2 * KT)
            streamed(B_P2, T_P2, sem("norm_split"), 2 * KT, early=4, late=("h2", dacc, drstd))

            def pool_product(g, u):
                product(B_P2 + 2 * g + u, T_P2 + 2 * g + u, u, u, T_P2 // 2 + g, x_h, x_l)

            for g in range(4):
                if g < 3:
                    pool_product(g + 1, 0)
                pe.wait_ge(sem("pw_in"), 16 * g + 16)
                pe.wait_ge(sem("pooled"), g + 1)
                for half in range(2):
                    mm = pe.matmul(psa[:, half, :], pw[:, :], pu[:, half * HALF:(half + 1) * HALF],
                                   start=True, stop=True)
                mm.then_inc(sem("mixed"), 1)
                if g < 3:
                    pool_product(g + 1, 1)
            for u in range(2):
                product(B_P2 + 8 + u, T_P2 + 8 + u, u, u, T_P2 // 2 + 4, x_h, x_l)
            pe.wait_ge(g_free[1], T_P2 // 2 + 6)
            for c in range(NB):
                mm = pe.transpose(psb[:, c // 4, (c % 4) * P:(c % 4 + 1) * P], kv_f[:, c * P:c * P + P], m(M_ID))
            mm.then_inc(sem("v2_tr"), 1)
            pe.wait_ge(sem("v2_ready"), 1)

            def query_gate(p):
                for u in range(2):
                    pe.wait_ge(w_ready, B_P2 + 10 + 2 * p + u + 3)
                    pe.wait_ge(g_free[u], T_P2 // 2 + 5 + p + 1)
                    for half in range(2):
                        cols = slice(half * HALF, (half + 1) * HALF)
                        for k in range(KT):
                            w_cols = slice(k * P, (k + 1) * P)
                            mm = pe.matmul(psg[u][:, cols], whi[:, u, w_cols], xhi[:, k, cols],
                                           start=(k == 0), stop=False)
                            if half == 0 and k == 0:
                                mm.then_inc(w_used, 1)
                            yield
                            pe.matmul(psg[u][:, cols], whi[:, u, w_cols], xlo[:, k, cols], start=False, stop=False)
                            yield
                            mm = pe.matmul(psg[u][:, cols], wlo[:, u, w_cols], xhi[:, k, cols],
                                           start=False, stop=(k == KT - 1))
                            if half == 1 and k == KT - 1:
                                mm.then_inc(g_full, 1)
                            yield

            def scores(n):
                p, st = n // 4, n % 4
                if st == 0:
                    pe.wait_ge(g_free[0], T_P2 // 2 + 7 + p)
                if n:
                    pe.wait_ge(sem("as_out"), n)
                for h in range(2):
                    rows = slice(h * CH, h * CH + CH)
                    for b in range(2):
                        nb = 2 * st + b
                        mm = pe.matmul(psa[:, h, b * 256:b * 256 + 256], aq[rows, p % 2, nb * P:nb * P + P],
                                       kd[rows, p // 2, nb * P:nb * P + 256], start=True, stop=True)
                mm.then_inc(sem("as_full"), 1)

            for _ in query_gate(0):
                pass
            scores(0)
            for p in range(PAIRS):
                later = query_gate(p + 1) if p + 1 < PAIRS else iter(())

                def fill(k):
                    for _ in range(k):
                        next(later, None)

                for st in range(4):
                    n = 4 * p + st
                    if n + 1 < 4 * PAIRS:
                        scores(n + 1)
                    fill(10)
                    pe.wait_ge(sem("ap_ready"), n + 1)
                    pe.wait_ge(sem("ao_out"), n + 1)
                    for q in range(4):
                        for kb in range(2):
                            mm = pe.transpose(psb[:, q // 2, (q % 2) * 256 + kb * P:(q % 2) * 256 + kb * P + P],
                                              ap_[:, n % 2, q, kb * P:kb * P + P], m(M_ID))
                    mm.then_inc(sem("apt_full"), 1)
                    fill(6)
                    pe.wait_ge(sem("apt_ready"), n + 1)
                    for h in range(2):
                        for b in range(2):
                            for kb in range(2):
                                mm = pe.matmul(psb[h * CH:h * CH + CH, 0, b * P:b * P + P],
                                               vt2[:, 2 * st + b + kb, (p // 2) * CH:(p // 2) * CH + CH],
                                               apt[:, 2 * h + b, kb, :], start=(kb == 0), stop=(kb == 1))
                    mm.then_inc(sem("ao_full"), 1)
                    fill(8)

            streamed(B_O2, T_O2, sem("op_split"), SPLIT_BEFORE["cat"])
            plain(B_O2, T_O2, KT // 2, 1)
            norm_factor(q2acc, q2rstd, "fin")

        @block.vector
        def _(v):
            tt, ts, stt = v.tensor_tensor, v.tensor_scalar, v.scalar_tensor_tensor
            MUL, ADD, SUB = ALU.mult, ALU.add, ALU.subtract
            v.sem_inc(g_free[0], 1)
            v.sem_inc(g_free[1], 1)

            def start_sum(name, acc):
                v.memset(acc[:, :], 0.0)
                v.sem_inc(sem(name + "_added"), 2)

            def root(name, rstd):
                v.wait_ge(sem("norm_tot"), NORM[name] + 1)
                ts(sm[:, 0:NB], psa[:, 0, 0:NB], 1.0 / D, 1e-6, MUL, ADD).then_inc(sem("norm_ms"), 1)
                v.wait_ge(sem("norm_sd"), NORM[name] + 1)
                v.reciprocal(sm[:, 0:NB], sm[:, 0:NB])
                v.drain()
                v.tensor_copy(rstd[:, :].rearrange("p (n c) -> p n c", c=P),
                              sm[:, 0:NB].unsqueeze(2).broadcast_to([P, NB, P])).then_inc(sem("norm_exp"), 1)
                v.wait_ge(sem("norm_rep"), NORM[name] + 1)

            def head_factor(n):
                v.wait_ge(sem("hd_sd"), n)
                v.reciprocal(sm[:, 0:16], sm[:, 0:16])
                v.drain()
                v.tensor_copy(TM[:, :].rearrange("p (n c) -> p n c", c=CH),
                              sm[:, 0:16].unsqueeze(2).broadcast_to([P, 16, CH])).then_inc(sem("hd_exp"), 1)
                v.wait_ge(sem("hd_rep"), n)

            def split_normed(name, src, gain, rstd, tmp):
                for j in range(KT + 1):
                    if j < KT:
                        stt(tmp[:, j % 2, :], src[:, j, :], par_col(gain, j), flat(psa), MUL, MUL
                            ).then_inc(sem("normed"), 1)
                    if j:
                        v.wait_ge(sem("norm_high"), j)
                        tt(xlo[:, j - 1, :], tmp[:, (j - 1) % 2, :], xhi[:, j - 1, :].bitcast(F32), SUB
                           ).then_inc(sem("norm_split"), 1)
                    v.drain()

            def split_low(name, src, hi, lo, n):
                for j in range(n):
                    v.wait_ge(sem("op_high"), SPLIT_BEFORE[name] + j + 1)
                    tt(lo[:, j, :], src[:, j, :], hi[:, j, :].bitcast(F32), SUB).then_inc(sem("op_split"), 1)

            v.wait_ge(sem("pos_in"), 32)
            v.tensor_copy(ang[:, :], posi[:, :])
            v.drain()
            ts(ang[:, :], ang[:, :], par_col("invf"), None, MUL)
            v.drain()

            def turns(shift, tab):
                ts(kq[:, :], ang[:, :], float(1 / (2 * np.pi)), shift, MUL, ADD)
                v.drain()
                ts(kq[:, :], kq[:, :], MAGIC, None, ADD)
                v.drain()
                ts(kq[:, :], kq[:, :], MAGIC, None, SUB)
                v.drain()
                stt(tab, kq[:, :], -TWO_PI_A, ang[:, :], MUL, ADD)
                v.drain()
                stt(tab, kq[:, :], -TWO_PI_B, tab, MUL, ADD)
                v.drain()
                stt(tab, kq[:, :], -TWO_PI_C, tab, MUL, ADD)
                v.drain()
                ts(tab, tab, float(shift * 2 * np.pi), float(np.float32(3.1415925)), ADD, ALU.min)
                v.drain()
                ts(tab, tab, -float(np.float32(3.1415925)), None, ALU.max).then_inc(sem("angle"), 1)

            turns(0.0, rot[:, 0, :])

            v.wait_ge(sem("a_added"), KT // 2 + 2)
            for j in range(KT // 2, KT):
                v.drain()
                v.wait_ge(sem("a_sq"), j + 1)
                tt(pa_acc[:, :], pa_acc[:, :], pa_sq[:, j % 2, :], ADD).then_inc(sem("a_added"), 1)
            root("a", pa_rstd)
            split_normed("x", xres, "g_mix_pre", pa_rstd, pa_tmp)
            v.wait_ge(consts_in, 16)
            tt(id2[:, :], m(M_ID)[:, 0:CH], m(M_ID)[:, CH:P], ADD)
            v.tensor_copy(idr[:, :], m(M_ID))

            ts(pp[:, 10:12], prm[:, COLS["mu_low"]:COLS["mu_low"] + 2], -1.0, 1.0, MUL, ADD
               ).then_inc(sem("pp_ready"), 1)
            turns(0.25, rot[:, 1, :])

            for u, buf in enumerate((R, K)):
                v.wait_ge(sem("low_a"), u + 1)
                stt(buf[:, 1:T], psg[u][:, 0:T - 1], par_col("mu_low", u), buf[:, 1:T], MUL, ADD
                    ).then_inc(g_free[u], 1)
            v.wait_ge(sem("low_hi"), 1)
            tt(ta_lo[:, :], R[:, :], ta_hi[:, :].bitcast(F32), SUB).then_inc(sem("lora_split"), 1)
            v.wait_ge(sem("low_hi"), 2)
            tt(sg_lo[:, :], K[:, :], sg_hi[:, :].bitcast(F32), SUB).then_inc(sem("lora_split"), 1)

            v.memset(SC[:, :, :], 0.0)
            with v.Fori(0, PAIRS) as i:
                v.drain()
                v.tensor_copy(pp[:, 0:10], prm[:, bass.ds(COLS["rw"] + 10 * i, 10)])
                v.drain()
                ts(pp[:, 10:13], pp[:, 0:3], -1.0, 1.0, MUL, ADD)
                ts(pp[:, 13:14], pp[:, 6:7], -1.0, 1.0, MUL, ADD).then_inc(sem("pp_ready"), 1)
                for j, buf in enumerate((R, K, V)):
                    v.wait_ge(sem("sh_a"), 3 * i + j + 1)
                    stt(buf[:, 1:T], psg[j % 2][:, 0:T - 1], pp[:, j:j + 1], buf[:, 1:T], MUL, ADD
                        ).then_inc(g_free[j % 2], 1)
                v.drain()
                ts(KK[:, :], K[:, :], pp[:, 5:6], None, MUL).then_inc(sem("kk_ready"), 1)
                v.memset(E1[:, :], 1.0)
                v.drain()
                v.memset(E1[:, 0:T:CH], 0.0)
                v.drain()
                v.wait_ge(g_free[1], 8 * i + 4)
                v.tensor_tensor_scan(CS[:, :], E1[:, :], SG[:, :], 0.0, MUL, ADD)
                v.drain()
                tt(SG[:, :], CS[:, :], SG[:, :], SUB)
                v.wait_ge(g_free[0], 8 * i + 5)
                ts(BON[:, :], A[:, :], pp[:, 6:7], pp[:, 13:14], MUL, ADD)
                v.drain()
                tt(K[:, :], K[:, :], BON[:, :], MUL)
                v.wait_ge(sem("hd_sum"), 2 * i + 1)
                ts(sm[:, 0:16], psa[:, 0, 0:16], 1e-24, None, ALU.max).then_inc(sem("hd_ms"), 1)
                head_factor(2 * i + 1)
                tt(KK[:, :], KK[:, :], flat(psa), MUL)
                v.drain()
                stt(TM[:, :], R[:, :], pp[:, 7:8], K[:, :], MUL, MUL).then_inc(sem("rk_prod"), 1)
                v.wait_ge(sem("exp_ready"), i + 1)
                tt(KR[:, :, 0, :], KK[:, :].rearrange("p (n c) -> p n c", c=P),
                   SG[:, :].rearrange("p (n c) -> p n c", c=P), MUL)
                tt(KR[:, :, 1, :], R[:, :].rearrange("p (n c) -> p n c", c=P),
                   E1[:, :].rearrange("p (n c) -> p n c", c=P), MUL)
                tt(A[:, :], KK[:, :], A[:, :], MUL)
                v.tensor_copy(ec[:, :], E1[:, CH - 1:T:CH])
                tt(K[:, :], K[:, :], EN[:, :], MUL)
                v.drain()
                tt(KK[:, :], A[:, :], EN[:, :], MUL)
                v.drain()

                def by_chunk(t):
                    return t[:, :].rearrange("p (n c) -> p n c", c=CH)

                ecb = ec[:, :].unsqueeze(2).broadcast_to([P, 16, CH])
                tt(by_chunk(BE), by_chunk(KK), ecb, MUL)
                tt(by_chunk(KE), by_chunk(K), ecb, MUL)
                tt(by_chunk(DG), id2[:, :].unsqueeze(1).broadcast_to([P, 16, CH]), ecb, MUL)
                v.memset(ST[:, 0, :], 0.0)
                v.wait_ge(sem("bonus_sum"), i + 1)
                tt(BON[:, :], flat(psb), V[:, :], MUL).then_inc(sem("rw_prep"), 1)
                for g in range(GROUPS):
                    msk = mat[:, M_STRICT:M_STRICT + 2, :].rearrange("p a b -> p (a b)").unsqueeze(1
                                                                                    ).broadcast_to([P, 2, 256])
                    for q in range(4):
                        v.wait_ge(sem("scores"), 16 * i + 4 * g + q + 1)
                        tt(SC[:, q, :].rearrange("p (a x) -> p a x", a=2)[:, :, 0:256],
                           bank[q].rearrange("p (a x) -> p a x", a=2), msk, MUL).then_inc(sem("sc_out"), 1)
                    for t2 in range(2):
                        v.wait_ge(sem("tr_full"), 8 * i + 2 * g + t2 + 1)
                        for c in range(2):
                            rows = slice(c * CH, c * CH + CH)
                            mm = v.tensor_copy(
                                SC[rows, 2 * t2:2 * t2 + 2, :].rearrange("p h (k x) -> p h k x", k=2)[
                                    :, :, :, 256 + c * CH:256 + c * CH + CH],
                                bank[t2][rows, 0:256].rearrange("p (k h d) -> p h k d", k=2, h=2))
                        mm.then_inc(sem("tr_dve"), 1)
                    v.drain()
                    tt(MTF[:, :, :], SC[:, :, 0:P], many(M_LOW0T, 4), MUL)
                    v.wait_ge(sem("at_hi"), 4 * i + g + 1)
                    tt(ATL[:, :, :], SC[:, :, 0:P], ATH[:, :, :].bitcast(F32), SUB)
                    v.wait_ge(sem("x_full"), 24 * i + 6 * g + 1)
                    tt(XM[:, :, :], bank[2].rearrange("p (q c) -> p q c", q=4), many(M_LVL, 4), MUL)
                    v.drain()
                    tt(M[:, :, :], XM[:, :, :].bitcast(F32), many(M_ID, 4), ADD)
                    tt(MT[:, :, :], MTF[:, :, :], many(M_ID, 4), ADD).then_inc(sem("m_init"), 1)
                    for lv in range(1, LEVELS):
                        v.wait_ge(sem("x_full"), 24 * i + 6 * g + 1 + lv)
                        tt(XM[:, :, :], bank[2].rearrange("p (q c) -> p q c", q=4), many(M_LVL + lv, 4), MUL
                           ).then_inc(sem("x_out"), 1)
                        if lv < LEVELS - 1:
                            v.wait_ge(sem("mt_full"), 16 * i + 4 * g + lv)
                            v.tensor_copy(MT[:, :, :], bank[0].rearrange("p (q c) -> p q c", q=4)
                                          ).then_inc(sem("mt_dve"), 1)
                    v.wait_ge(sem("e_full"), 4 * i + g + 1)
                    tt(XM[:, :, :], many(M_ID, 4), bank[2].rearrange("p (q c) -> p q c", q=4), SUB
                       ).then_inc(sem("e_ready"), 1)
                    v.wait_ge(sem("fin_full"), 4 * i + g + 1)
                    tt(MTF[:, :, :], MT[:, :, :].bitcast(F32), bank[3].rearrange("p (q c) -> p q c", q=4), ADD
                       ).then_inc(sem("mtf_ready"), 1)
                    v.wait_ge(sem("rp_full"), 4 * i + g + 1)
                    rp = bank[3].rearrange("p (t x) -> p t x", t=2)
                    tt(RT[:, :, :], rp[:, :, 0:P], KR[:, 2 * g:2 * g + 2, 1, :], ADD)
                    tt(PT[:, :, :], rp[:, :, P:2 * P],
                       DG[:, 2 * g * P:2 * g * P + 2 * P].rearrange("p (t x) -> p t x", t=2), ADD
                       ).then_inc(sem("rt_pt"), 1)
                v.wait_ge(sem("hd_sum"), 2 * i + 2)
                ts(sm[:, 0:16], psa[:, 0, 0:16], 1.0 / CH, 64e-5, MUL, ADD).then_inc(sem("hd_ms"), 1)
                head_factor(2 * i + 2)
                tt(YB[:, :], YB[:, :], flat(psa), MUL).then_inc(sem("gn_nrm"), 1)
                v.wait_ge(sem("gn_aff"), i + 1)
                tt(YB[:, :], YB[:, :], BON[:, :], ADD)
                v.drain()
                tt(YB[:, :], YB[:, :], G[:, :], MUL).then_inc(sem("yrw_done"), 1)
            def by_token(t):
                return t[:, :].rearrange("p (n c) -> p n c", c=P)

            def psn(ps):
                return ps[:].rearrange("p a (b c) -> p (a b) c", c=P)

            def rotate(p):
                q_k = rraw[p % 2]
                if p == 0:
                    v.wait_ge(sem("rot_in"), 16)
                for n, (lo, hi) in enumerate(((1, 2), (0, 1)) if p == 0 else ((0, 2),)):
                    if n == 0:
                        v.wait_ge(sem("ret_in"), 96 * p + 96)
                    else:
                        v.wait_ge(sem("rq_in"), 80)
                    tt(q_k[:, lo:hi, :], q_k[:, lo:hi, :], rott[:, 1:2, :].broadcast_to([P, hi - lo, T]), MUL)
                    tt(rswp[:, lo:hi, :], rswp[:, lo:hi, :], rott[:, 0:1, :].broadcast_to([P, hi - lo, T]), MUL)
                    v.drain()
                    tt(q_k[:, lo:hi, :], q_k[:, lo:hi, :], rswp[:, lo:hi, :], ADD)
                    if n == 0:
                        v.drain()
                        tt(by_token(RKD), q_k[:, 1, :].rearrange("p (n c) -> p n c", c=P),
                           RTAB[:, p % 2, 3:4, :].broadcast_to([P, NB, P]), MUL).then_inc(sem("rkd"), 1)
                    else:
                        v.drain()

            def decay_queries(p):
                tt(by_token(RQD), rraw[p % 2][:, 0, :].rearrange("p (n c) -> p n c", c=P),
                   RTAB[:, p % 2, 2:3, :].broadcast_to([P, NB, P]), MUL).then_inc(sem("rqd"), 1)

            rotate(0)
            v.wait_ge(sem("yrw_stored"), 16 * PAIRS + 16)
            decay_queries(0)
            split_low("yrw", yrw, xhi, xlo, PAIRS)
            for p in range(PAIRS):
                v.wait_ge(sem("kv_full"), p + 1)
                v.tensor_copy(RS[:, 1, :], psn(psb)[:, 0, :])
                for c in range(1, NB - 1):
                    v.drain()
                    mm = stt(RS[:, c + 1, :], RS[:, c, :], par_col("cdecay", p), psn(psb)[:, c, :], MUL, ADD)
                mm.then_inc(sem("r_states"), 1)
                for h in range(2):
                    v.wait_ge(sem("rs_full"), 2 * p + h + 1)
                    ps = psn(psa) if h == 0 else psg[1][:, :].rearrange("p (b c) -> p b c", c=P)
                    tt(RP[h][:, :, :], ps, RTAB[:, p % 2, h:h + 1, :].broadcast_to([P, NB, P]), MUL
                       ).then_inc(sem("rs_ready"), 1)
                v.wait_ge(sem("rg_sig"), p + 1)
                tt(RGS[:, :, :], RGS[:, :, :], RG[:, :, :], MUL).then_inc(sem("rg_done"), 1)
                if p + 1 < PAIRS:
                    rotate(p + 1)
                for h in range(2):
                    cols = slice(NB * h, NB * h + NB)
                    v.wait_ge(sem("rgn_sum"), 2 * p + h + 1)
                    ts(sm[:, cols], psa[:, 0, 0:NB], 1.0 / P, 1e-5, MUL, ADD).then_inc(sem("rgn_ms"), 1)
                    v.wait_ge(sem("rgn_sd"), 2 * p + h + 1)
                    v.reciprocal(sm[:, cols], sm[:, cols])
                    v.drain()
                    v.tensor_copy(by_token(RE[h]), sm[:, cols].unsqueeze(2).broadcast_to([P, NB, P])
                                  ).then_inc(sem("rgn_exp"), 1)
                    v.wait_ge(sem("rgn_rep"), 2 * p + h + 1)
                    tt(RGS[:, h, :], RGS[:, h, :], flat(psa), MUL)
                    v.drain()
                    tt(yret[:, 2 * p + h, :], flat(psb) if h == 0 else psg[1][:, :], RGS[:, h, :], MUL
                       ).then_inc(sem("yret_done"), 1)
                if p + 1 < PAIRS:
                    decay_queries(p + 1)
            split_low("yret", yret, xhi, xlo, KT)
            v.sem_inc(sem("mg_done"), 2)
            with v.Fori(0, KT // 2) as i:
                for u in range(2):
                    v.wait_ge(sem("mg_sig"), 2 * i + u + 1)
                    tt(mgr[:, u, :], mgr[:, u, :], mbr[:, u, :], MUL)
                    v.wait_ge(g_full, T_MRG + 2 * i + u + 1)
                    tt(mgt[:, u, :], mgt[:, u, :], psg[u][:, :], MUL).then_inc(g_free[u], 1)
                    v.drain()
                    tt(merged[:, bass.ds(2 * i + u, 1), :].rearrange("p a t -> p (a t)"), mgr[:, u, :], mgt[:, u, :],
                       ADD).then_inc(sem("mg_done"), 1)
            split_low("merged", merged, xhi, xlo, KT)

            start_sum("out", oacc)
            with v.Fori(0, KT // 2) as i:
                for u in range(2):
                    v.drain()
                    v.wait_ge(sem("tile_sq"), 2 * i + u + 1)
                    tt(oacc[:, :], oacc[:, :], osq[:, u, :], ADD).then_inc(sem("out_added"), 1)

            def residual(y, gain, x, h, next_gain, nth):
                for j in range(KT + 1):
                    if j < KT:
                        stt(y[:, j, :], y[:, j, :], par_col(gain, j), flat(psa), MUL, MUL)
                        v.drain()
                        tt(h[:, j, :], x[:, j, :], y[:, j, :], ADD).then_inc(sem("res_h"), 1)
                    if j:
                        v.wait_ge(sem("norm_high"), KT * nth + j)
                        stt(xlo[:, j - 1, :], h[:, j - 1, :], par_col(next_gain, j - 1),
                            xhi[:, j - 1, :].bitcast(F32), MUL, SUB).then_inc(sem("norm_split"), 1)

            def late_factor(name, rstd, out):
                root(name, rstd)
                v.tensor_copy(out[:, :], flat(psa))
                v.drain()

            root("out", orstd)
            v.wait_ge(sem("res_in"), 16)
            residual(oy, "g_mix_post", oh, oh, "g_ffn_pre", 1)
            v.wait_ge(sem("h_stored"), 16)
            late_factor("pre", orstd, frs)
            v.sem_inc(sem("f_done"), 1)

            def hidden(i, between=None):
                v.drain()
                v.tensor_copy(cp[:, :], prm[:, bass.ds(COLS["conv"] + 8 * i, 8)]).then_inc(sem("cp_ready"), 1)
                v.drain()
                for u, buf in enumerate((fg, fv)):
                    v.wait_ge(g_full, T_UP + 2 * i + u + 1)
                    tt(buf[:, 1, :], psg[u][:, :], frs[:, :], MUL).then_inc(g_free[u], 1)
                if between:
                    between()
                for u, buf in enumerate((fg, fv)):
                    v.wait_ge(sem("cv_a"), 2 * i + u + 1)
                    stt(buf[:, 0, 1:T], buf[:, 1, 0:T - 1], cp[:, 4 * u + 1:4 * u + 2], buf[:, 0, 1:T], MUL, ADD)
                    v.drain()
                    stt(buf[:, 0, 2:T], buf[:, 1, 0:T - 2], cp[:, 4 * u:4 * u + 1], buf[:, 0, 2:T], MUL, ADD
                        ).then_inc(sem("cv_taps"), 1)
                v.drain()
                v.wait_ge(sem("gelu"), i + 1)
                tt(ff[:, bass.ds(i, 1), :].rearrange("p a t -> p (a t)"), fg[:, 0, :], fv[:, 0, :], MUL
                   ).then_inc(sem("f_done"), 1)

            def hidden_low(half, i, u):
                cols = slice(half * HALF, (half + 1) * HALF)
                v.wait_ge(sem("f_h"), half * FT + 2 * i + u + 1)
                tt(flo[:, u, :], ff[:, bass.ds(2 * i + u, 1), cols].rearrange("p a t -> p (a t)"),
                   fhi[:, u, :].bitcast(F32), SUB).then_inc(sem("f_split"), 1)

            def down_square(half, j):
                v.drain()
                v.wait_ge(sem("down_sq"), half * KT + j + 1)
                cols = slice(half * HALF, (half + 1) * HALF)
                tt(dacc[:, cols], dacc[:, cols], dsq[:, j % 2, :], ADD).then_inc(sem("down_added"), 1)

            with v.Fori(0, FT - 1) as i:
                hidden(i)
            hidden(FT - 1, between=lambda: (v.drain(), hidden_low(0, 0, 0), hidden_low(0, 0, 1)))
            start_sum("down", dacc)
            with v.Fori(1, FT // 2) as i:
                for u in range(2):
                    hidden_low(0, i, u)
            for n in range(2 + KT):
                hidden_low(1, n // 2, n % 2)
                if n >= 2:
                    down_square(0, n - 2)
            with v.Fori(1 + KT // 2, FT // 2) as i:
                for u in range(2):
                    hidden_low(1, i, u)
            for j in range(KT):
                down_square(1, j)
            root("down", drstd)
            v.wait_ge(sem("res_in"), 32)
            residual(dy, "g_ffn_post", dh, h2, "g2_pre", 2)
            late_factor("h2", drstd, rs2)

            for g in range(4):
                win = 2 ** (g + 1)
                v.wait_ge(g_full, T_P2 + 2 * g + 1)
                tt(pu[:, :], psg[0][:, :], rs2[:, :], MUL).then_inc(g_free[0], 1)
                v.drain()
                src, dst = pu, ps2
                for k in range(g + 1):
                    s = 2 ** k
                    v.tensor_copy(dst[:, 0:s], src[:, 0:s])
                    tt(dst[:, s:T], src[:, s:T], src[:, 0:T - s], ADD)
                    v.drain()
                    src, dst = dst, (ps4 if dst is ps2 else ps2)
                c = COLS["counts"] + 15 * g
                tt(src[:, 0:win - 1], src[:, 0:win - 1], prm[:, c:c + win - 1], MUL)
                v.drain()
                stt(pu[:, :], src[:, :], 1.0 / win, pu[:, :], MUL, SUB).then_inc(sem("pooled"), 1)
                v.wait_ge(g_full, T_P2 + 2 * g + 2)
                tt(pgt[:, :], psg[1][:, :], rs2[:, :], MUL).then_inc(g_free[1], 1)
                v.drain()
                v.wait_ge(sem("pg_sig"), g + 1)
                tt(pgt[:, :], pgt[:, :], pgs[:, :], MUL)
                v.drain()
                v.wait_ge(sem("mixed"), g + 1)
                stt(cat[:, g, :], flat(psa), par_col("pscale", g), pgt[:, :], MUL, MUL
                    ).then_inc(sem("pool_done"), 1)
            v.drain()
            v.memset(kd[:, :, 0:P], 0.0)
            v.memset(vt2[:, 0, :], 0.0).then_inc(sem("kv_zero"), 1)
            for u, buf in enumerate((kk_f, kv_f)):
                v.wait_ge(g_full, T_P2 + 9 + u)
                tt(buf[:, :], psg[u][:, :], rs2[:, :], MUL).then_inc(g_free[u], 1)

            v.sem_inc(sem("ao_out"), 1)

            def gated(n):
                v.wait_ge(sem("ao_full"), n + 1)
                o = cat[:, 4 + n // 4, (n % 4) * 256:(n % 4) * 256 + 256]
                tt(o, psb[:, 0, 0:256], o, MUL).then_inc(sem("ao_out"), 1)

            def queries(p):
                v.wait_ge(g_full, T_P2 + 10 + 2 * p + 1)
                tt(aq[:, p % 2, :], psg[0][:, :], rs2[:, :], MUL).then_inc(g_free[0], 1)

            queries(0)
            for n in range(4 * PAIRS):
                p, st = n // 4, n % 4
                if st == 0:
                    v.drain()
                    v.tensor_copy(sm[:, 0:2], prm[:, COLS["sinks"] + 2 * p:COLS["sinks"] + 2 * p + 2])
                    v.wait_ge(sem("ab_in"), 16 * p + 16)
                snk = sm[:, 0:2].unsqueeze(2).broadcast_to([P, 2, 2])
                pr = ap_[:, n % 2]
                v.wait_ge(sem("as_full"), n + 1)
                for h in range(2):
                    if st == 0:
                        for b in range(2):
                            mm = stt(pr[:, 2 * h + b, :], psa[:, h, b * 256:b * 256 + 256], 0.125,
                                     ab[p % 2][:, 1 - b, h, :], MUL, ADD)
                    else:
                        mm = stt(pr[:, 2 * h:2 * h + 2, :], psa[:, h, :].rearrange("p (b c) -> p b c", b=2), 0.125,
                                 ab[p % 2][:, 0, h, :].unsqueeze(1).broadcast_to([P, 2, 256]), MUL, ADD)
                mm.then_inc(sem("as_out"), 1)
                v.drain()
                v.tensor_reduce(sm[:, 4:8], pr[:, :, :], AX_X, ALU.max)
                v.drain()
                tt(sm[:, 8:12].rearrange("p (h b) -> p h b", h=2),
                   sm[:, 4:8].rearrange("p (h b) -> p h b", h=2), snk, ALU.max)
                v.drain()
                ts(sm[:, 8:12], sm[:, 8:12], -1.0, None, MUL)
                v.drain()
                tt(sm[:, 12:16].rearrange("p (h b) -> p h b", h=2),
                   sm[:, 8:12].rearrange("p (h b) -> p h b", h=2), snk, ADD).then_inc(sem("am_ready"), 1)
                if st == 1:
                    v.wait_ge(sem("ag_sig"), p + 1)
                    tt(cat[:, 4 + p, :], cat[:, 4 + p, :], gsig[:, :], MUL)
                    v.drain()
                if n:
                    gated(n - 1)
                if st == 0:
                    v.wait_ge(g_full, T_P2 + 10 + 2 * p + 2)
                    tt(cat[:, 4 + p, :], psg[1][:, :], rs2[:, :], MUL).then_inc(g_free[1], 1)
                if st == 2 and p + 1 < PAIRS:
                    queries(p + 1)
                v.wait_ge(sem("ae_ready"), n + 1)
                tt(sm[:, 20:24], sm[:, 16:20], sm[:, 12:16], ADD)
                v.drain()
                v.reciprocal(sm[:, 20:24], sm[:, 20:24])
                v.drain()
                tt(pr[:, :, :], pr[:, :, :], sm[:, 20:24].unsqueeze(2).broadcast_to([P, 4, 256]), MUL
                   ).then_inc(sem("ap_ready"), 1)
            gated(4 * PAIRS - 1)
            split_low("cat", cat, xhi, xlo, KT)
            start_sum("fin", q2acc)
            with v.Fori(0, KT // 2) as i:
                for u in range(2):
                    v.drain()
                    v.wait_ge(sem("tile_sq"), KT + 2 * i + u + 1)
                    tt(q2acc[:, :], q2acc[:, :], q2sq[:, u, :], ADD).then_inc(sem("fin_added"), 1)
            root("fin", q2rstd)
            for j in range(KT):
                stt(y2[:, j, :], y2[:, j, :], par_col("g2_post", j), flat(psa), MUL, MUL).then_inc(sem("y_scaled"), 1)
                if j not in BY_POOL:
                    v.drain()
                    tt(y2[:, j, :], y2[:, j, :], h2[:, j, :], ADD).then_inc(sem("y_done"), 1)

        @block.scalar
        def _(s):
            act = s.activation
            SIG, SQ, CP, IDN, SQRT, EXP = ACT.Sigmoid, ACT.Square, ACT.Copy, ACT.Identity, ACT.Sqrt, ACT.Exp

            def root(name):
                s.wait_ge(sem("norm_ms"), NORM[name] + 1)
                act(sm[:, 0:NB], sm[:, 0:NB], SQRT).then_inc(sem("norm_sd"), 1)

            def split_squares(name, before, src, gain, sq):
                for j in range(KT):
                    s.wait_ge(sem("res_h"), before + j + 1)
                    act(xhi[:, j, :], src[:, j, :], IDN, scale=par_col(gain, j)).then_inc(sem("norm_high"), 1)
                    act(sq[:, j, :], src[:, j, :], SQ).then_inc(sem(name + "_sq"), 1)

            def split_high(name, tmp):
                for j in range(KT):
                    s.wait_ge(sem("normed"), j + 1)
                    act(xhi[:, j, :], tmp[:, j % 2, :], CP).then_inc(sem("norm_high"), 1)

            def high(name, src, hi, n):
                for j in range(n):
                    act(hi[:, j, :], src[:, j, :], CP).then_inc(sem("op_high"), 1)

            for j in range(0, KT, 2):
                s.dma_start(xres[:, j:j + 2, :], xt[:, j:j + 2, :]).then_inc(sem(f"x_in{j // 2}"), 16)
                if j == 0:
                    s.dma_start(posi[:, :], pos).then_inc(sem("pos_in"), 16)
                    s.dma_start(prm[:, :], par).then_inc(sem("pos_in"), 16)
            s.dma_start(mat[:, :, :], mats[:, 0:NMAT, :]).then_inc(consts_in, 16)
            for j in range(KT):
                s.wait_ge(sem(f"x_in{j // 2}"), 16)
                s.wait_ge(sem("a_added"), j + 1)
                act(pa_sq[:, j % 2, :], xres[:, j, :], SQ).then_inc(sem("a_sq"), 1)
            root("a")
            split_high("x", pa_tmp)

            s.wait_ge(sem("pp_ready"), 1)
            for u, buf in enumerate((R, K)):
                s.wait_ge(g_full, u + 1)
                act(buf[:, :], psg[u][:, :], IDN, scale=pp[:, 10 + u:11 + u]).then_inc(sem("low_a"), 1)
            s.wait_ge(g_free[0], 2)
            act(R[0:CH, :], R[0:CH, :], ACT.Tanh)
            s.wait_ge(g_free[1], 2)
            act(K[:, :], K[:, :], SIG)
            s.drain()
            act(ta_hi[:, :], R[:, :], CP).then_inc(sem("low_hi"), 1)
            act(sg_hi[:, :], K[:, :], CP).then_inc(sem("low_hi"), 1)

            s.wait_ge(sem("angle"), 2)
            act(rot[:, 0, :], rot[:, 0, :], ACT.Sin, scale=par_col("sgn"))
            act(rot[:, 1, :], rot[:, 1, :], ACT.Sin).then_inc(sem("sincos"), 1)
            s.wait_ge(sem("sincos"), 1)
            s.dma_start(rot_d, rot[:, :, :]).then_inc(sem("rot_stored"), 16)

            for b in range(2):
                s.sem_inc(sem(f"stored{b}"), 16)
            s.sem_inc(sem("yrw_stored"), 16)

            s.wait_ge(sem("rot_stored"), 16)
            with s.Fori(0, PAIRS) as i:
                def put_later(f):
                    j = 6 + f
                    b = j % 2
                    s.wait_ge(sem(f"stored{b}"), 80 * i + 16 * (f // 2) + 16)
                    s.wait_ge(g_full, T_RW + RW_T * i + j + 1)
                    act(stage[:, b, :], psg[b][:, :], CP).then_inc(g_free[b], 1)
                    s.wait_ge(g_free[b], 8 * i + j // 2 + 3)
                    s.dma_start(later_d[bass.ds(LATER * i + f, 1)].rearrange("a p t -> (a p) t"), stage[:, b, :]
                                ).then_inc(sem(f"stored{b}"), 16)

                s.wait_ge(sem("pp_ready"), i + 2)
                for j, buf in enumerate((R, K, V)):
                    s.wait_ge(g_full, RW_T * i + T_RW + j + 1)
                    act(buf[:, :], psg[j % 2][:, :], IDN, scale=pp[:, 10 + j:11 + j]).then_inc(sem("sh_a"), 1)
                s.wait_ge(g_full, RW_T * i + T_RW + 4)
                act(SG[:, :], psg[1][:, :], SIG, bias=pp[:, 3:4]).then_inc(g_free[1], 1)
                s.wait_ge(g_full, RW_T * i + T_RW + 5)
                act(A[:, :], psg[0][:, :], SIG, bias=pp[:, 4:5]).then_inc(g_free[0], 1)
                s.wait_ge(g_full, RW_T * i + T_RW + 6)
                act(G[:, :], psg[1][:, :], CP).then_inc(g_free[1], 1)
                s.wait_ge(sem("kk_ready"), i + 1)
                act(TM[:, :], KK[:, :], SQ).then_inc(sem("hd_sq"), 1)
                s.wait_ge(sem("hd_ms"), 2 * i + 1)
                act(sm[:, 0:16], sm[:, 0:16], SQRT).then_inc(sem("hd_sd"), 1)
                act(E1[:, :], CS[:, :], EXP, scale=-C0)
                s.wait_ge(sem("yrw_stored"), 16 * i + 16)
                act(EN[:, :], CS[:, :], EXP, scale=C0)
                act(SG[:, :], SG[:, :], EXP, scale=-C0).then_inc(sem("exp_ready"), 1)
                put_later(0)
                for g in range(GROUPS):
                    s.wait_ge(sem("sc_out"), 16 * i + 4 * g + 4)
                    act(ATH[:, :, :], SC[:, :, 0:P], CP).then_inc(sem("at_hi"), 1)
                    for t2 in range(2):
                        s.wait_ge(sem("tr_dve"), 8 * i + 2 * g + t2 + 1)
                        act(VT[:, 2 * t2:2 * t2 + 2, :], bank[t2][:, 256:384].rearrange("p (h d) -> p h d", h=2), CP)
                        act(Z[:, 2 * t2:2 * t2 + 2, 0:CH], bank[t2][:, 384:512].rearrange("p (h d) -> p h d", h=2), CP
                            ).then_inc(sem("tr_act"), 1)
                    s.wait_ge(sem("dv_full"), 4 * i + g + 1)
                    act(Z[:, :, CH:P], bank[1][:, 0:256].rearrange("p (q d) -> p q d", q=4), CP
                        ).then_inc(sem("z_ready"), 1)
                    for lv in range(1, LEVELS):
                        s.wait_ge(sem("m_full"), 20 * i + 5 * g + lv)
                        act(M[:, :, :], bank[3].rearrange("p (q c) -> p q c", q=4), CP).then_inc(sem("m_act"), 1)
                        if lv == 4:
                            put_later(2 * g + 1)
                    s.wait_ge(sem("mt0_full"), 4 * i + g + 1)
                    act(MT[:, :, :], bank[0].rearrange("p (q c) -> p q c", q=4), CP).then_inc(sem("mt0_ready"), 1)
                    s.wait_ge(sem("gh_full"), 4 * i + g + 1)
                    act(GH[:, :, :], bank[2].rearrange("p (q c) -> p q c", q=4), CP, scale=-1.0
                        ).then_inc(sem("gh_ready"), 1)
                    for t2 in range(2):
                        tl = 2 * g + t2
                        for c in range(2):
                            step = 4 * g + 2 * t2 + c
                            s.wait_ge(sem("s_full"), 16 * i + step + 1)
                            act(ST[:, (step + 1) % 2, :], bank[1 + c][:, 0:CH], CP).then_inc(sem("s_new"), 1)
                        s.wait_ge(sem("y_full"), 8 * i + tl + 1)
                        act(YB[:, tl * P:tl * P + P], (bank[0] if t2 == 0 else bank[3])[:, 0:P], CP
                            ).then_inc(sem("y_out"), 1)
                    put_later(2 * g + 2)
                s.drain()
                act(TM[:, :], YB[:, :], SQ).then_inc(sem("hd_sq"), 1)
                s.wait_ge(sem("hd_ms"), 2 * i + 2)
                act(sm[:, 0:16], sm[:, 0:16], SQRT).then_inc(sem("hd_sd"), 1)
                s.wait_ge(sem("gn_nrm"), i + 1)
                act(YB[:, :], YB[:, :], IDN, scale=pp[:, 8:9], bias=pp[:, 9:10]).then_inc(sem("gn_aff"), 1)
                put_later(9)
                s.wait_ge(sem("yrw_done"), i + 1)
                s.dma_start(yrw_d[:, bass.ds(i, 1), :].rearrange("p a t -> p (a t)"), YB[:, :]
                            ).then_inc(sem("yrw_stored"), 16)

            def load_queries_keys(p):
                s.dma_start(RTAB[:, p % 2, :, :], ret_tab[p]).then_inc(sem("ret_in"), 16)
                for parts in ((slice(1, 2), slice(0, 1)) if p == 0 else (slice(0, 2),)):
                    landed = sem("rq_in") if parts == slice(0, 1) else sem("ret_in")
                    rows = later_d[6 * p:6 * p + 2][parts]
                    s.dma_start(rraw[p % 2][:, parts, :], rows.rearrange("a p t -> p a t")).then_inc(landed, 16)
                    for q in range(4):
                        dst, src = q * 32, (q ^ 1) * 32
                        s.dma_start(rswp[dst:dst + 32, parts, :], rows[:, src:src + 32, :].rearrange("a p t -> p a t")
                                    ).then_inc(landed, 16)

            def load_values(p):
                s.dma_start(RV[:, :, :], later_d[6 * p + 2:6 * p + 4].rearrange("a p t -> p a t")
                            ).then_inc(sem("rv_in"), 16)

            def load_gates(p):
                s.dma_start(RG[:, :, :], later_d[6 * p + 4:6 * p + 6].rearrange("a p t -> p a t")
                            ).then_inc(sem("rg_in"), 16)

            def values(p, h):
                s.wait_ge(sem("rv_tr"), 2 * p + h + 1)
                act(RVT[:, h, :, :], psb[:].rearrange("p a (b c) -> p (a b) c", c=P), CP).then_inc(sem("rv_tm"), 1)

            def keys(p):
                s.wait_ge(sem("rk_tr"), p + 1)
                act(RKT[:, :, :], psb[:].rearrange("p a (b c) -> p (a b) c", c=P), CP).then_inc(sem("rk_tm"), 1)

            def gate_sigmoid(p):
                if p:
                    s.wait_ge(sem("yret_done"), 2 * p)
                s.wait_ge(sem("rg_in"), 16 * p + 16)
                act(RGS[:, :, :], RG[:, :, :], SIG).then_inc(sem("rg_sig"), 1)

            def put_branch(j):
                if j > 1:
                    s.wait_ge(sem(f"stored{j % 2}"), 80 * PAIRS + 16 + 16 * (j // 2))
                s.wait_ge(g_full, T_BRW + j + 1)
                act(rstage[:, j % 2, :], psg[0][:, :], CP).then_inc(sem("br_free"), 1)
                s.wait_ge(sem("br_free"), j + 1)
                s.dma_start(later_d[S_BRW + j], rstage[:, j % 2, :]).then_inc(sem(f"stored{j % 2}"), 16)

            s.dma_start(RC[:, :], mats[:, M_CENT_RET, :]).then_inc(sem("rv_in"), 16)
            load_values(0)
            s.dma_start(rott[:, :, :], rot_d).then_inc(sem("rot_in"), 16)
            load_queries_keys(0)
            s.wait_ge(sem("yrw_stored"), 16 * PAIRS + 16)
            s.dma_start(yrw[:, :, :], yrw_d).then_inc(sem("yrw_in"), 16)
            for b in range(2):
                s.wait_ge(sem(f"stored{b}"), 80 * PAIRS + 16)
            load_gates(0)
            for h in range(2):
                values(0, h)
            keys(0)
            s.wait_ge(sem("yrw_in"), 16)
            high("yrw", yrw, xhi, PAIRS)
            gate_sigmoid(0)
            for p in range(PAIRS):
                if p + 1 < PAIRS:
                    s.wait_ge(sem("rkd") if p else sem("rqd"), p + 1)
                    load_queries_keys(p + 1)
                    load_values(p + 1)
                s.wait_ge(sem("ro_full"), 2 * p + 1)
                act(RE[0][:, :], flat(psb), SQ).then_inc(sem("rgn_sq"), 1)
                put_branch(2 * p)
                s.wait_ge(sem("ro_full"), 2 * p + 2)
                act(RE[1][:, :], psg[1][:, :], SQ).then_inc(sem("rgn_sq"), 1)
                s.wait_ge(sem("rgn_ms"), 2 * p + 1)
                act(sm[:, 0:NB], sm[:, 0:NB], SQRT).then_inc(sem("rgn_sd"), 1)
                if p + 1 < PAIRS:
                    s.wait_ge(sem("rg_done"), p + 1)
                    load_gates(p + 1)
                put_branch(2 * p + 1)
                if p + 1 < PAIRS:
                    values(p + 1, 0)
                s.wait_ge(sem("rgn_ms"), 2 * p + 2)
                act(sm[:, NB:2 * NB], sm[:, NB:2 * NB], SQRT).then_inc(sem("rgn_sd"), 1)
                if p + 1 < PAIRS:
                    values(p + 1, 1)
                    keys(p + 1)
                    gate_sigmoid(p + 1)
            for b in range(2):
                s.sem_inc(g_free[b], PAIRS)
            s.wait_ge(sem("yret_done"), KT)
            high("yret", yret, xhi, KT)
            for b in range(2):
                s.wait_ge(sem(f"stored{b}"), 80 * PAIRS + 16 + 16 * PAIRS)
            with s.Fori(0, KT // 2) as i:
                for u in range(2):
                    s.wait_ge(sem("mg_done"), 2 * i + u + 1)
                    for buf, row in ((mgr, S_GRW), (mgt, S_GRET), (mbr, S_BRW)):
                        s.dma_start(buf[:, u, :], later_d[bass.ds(row + 2 * i + u, 1)].rearrange("a p t -> (a p) t")
                                    ).then_inc(sem(f"mg_in{u}"), 16)
                    s.wait_ge(sem(f"mg_in{u}"), 48 * i + 48)
                    act(mgr[:, u, :], mgr[:, u, :], SIG)
                    act(mgt[:, u, :], mgt[:, u, :], SIG).then_inc(sem("mg_sig"), 1)
            s.wait_ge(sem("mg_done"), KT + 2)
            s.dma_start(oh[:, :, :], xt).then_inc(sem("res_in"), 16)
            high("merged", merged, xhi, KT)

            def evacuate(t0, name, y, sq):
                with s.Fori(0, KT // 2) as i:
                    for u in range(2):
                        s.wait_ge(sem(name + "_added"), 2 * i + u + 1)
                        s.wait_ge(g_full, t0 + 2 * i + u + 1)
                        s.sem_inc(go, 1)
                        act(sq[:, u, :], psg[u][:, :], SQ).then_inc(sem("tile_sq"), 1)
                        act(y[:, bass.ds(2 * i + u, 1), :].rearrange("p a t -> p (a t)"), psg[u][:, :], CP
                            ).then_inc(g_free[u], 1)

            evacuate(T_OUT, "out", oy, osq)
            root("out")
            split_squares("pre", 0, oh, "g_ffn_pre", oy)
            s.dma_start(h_d, oh[:, :, :]).then_inc(sem("h_stored"), 16)
            root("pre")

            def gate(i):
                s.wait_ge(sem("f_done"), i + 1)
                s.wait_ge(sem("cp_ready"), i + 1)
                s.wait_ge(g_free[0], T_UP // 2 + 2 + i)
                act(fg[:, 0, :], fg[:, 1, :], IDN, scale=cp[:, 2:3], bias=cp[:, 3:4]).then_inc(sem("cv_a"), 1)

            def value(i):
                s.wait_ge(g_free[1], T_UP // 2 + 2 + i)
                act(fv[:, 0, :], fv[:, 1, :], IDN, scale=cp[:, 6:7], bias=cp[:, 7:8]).then_inc(sem("cv_a"), 1)
                s.wait_ge(sem("cv_taps"), 2 * i + 1)
                act(fg[:, 0, :], fg[:, 0, :], ACT.Gelu_apprx_tanh).then_inc(sem("gelu"), 1)

            def hidden_high(half, i, u):
                s.wait_ge(sem("f_used"), half * FT + 2 * i + u + 1)
                s.sem_inc(go, 1)
                cols = slice(half * HALF, (half + 1) * HALF)
                act(fhi[:, u, :], ff[:, bass.ds(2 * i + u, 1), cols].rearrange("p a t -> p (a t)"), CP
                    ).then_inc(sem("f_h"), 1)

            def weights_high(half, i, u):
                s.wait_ge(w_landed[u], 16 * (B_DOWN // 2) + half * 8 * FT + 16 * i + 16)
                s.wait_ge(w_used, B_DOWN + half * FT + 2 * i + u + 1)
                s.sem_inc(go, 1)
                act(whi[:, u, :], wraw[:, u, :], CP).then_inc(sem("w_high"), 1)

            def copy_out(j):
                act(dy[:, j, 0:HALF], banks[j], CP).then_inc(sem("down_out"), 1)

            banks = [psg[0][:, 0:HALF], psg[0][:, HALF:T], psg[1][:, 0:HALF], psg[1][:, HALF:T]] + bank
            with s.Fori(0, FT - 1) as i:
                gate(i)
                value(i)
            s.sem_inc(sem("f_used"), 2)
            gate(FT - 1)
            hidden_high(0, 0, 0)
            weights_high(0, 0, 0)
            hidden_high(0, 0, 1)
            value(FT - 1)
            weights_high(0, 0, 1)
            for u in range(2):
                hidden_high(0, 1, u)
                weights_high(0, 1, u)
            s.wait_ge(sem("f_done"), FT + 1)
            s.dma_start(dh[:, :, :], h_d).then_inc(sem("res_in"), 16)
            with s.Fori(2, FT // 2) as i:
                for u in range(2):
                    hidden_high(0, i, u)
                    weights_high(0, i, u)
            hidden_high(1, 0, 0)
            weights_high(1, 0, 0)
            s.wait_ge(sem("f_used"), FT + 2)
            for j in range(KT // 2):
                copy_out(j)
            hidden_high(1, 0, 1)
            weights_high(1, 0, 1)
            for j in range(KT // 2, KT):
                copy_out(j)
            s.drain()
            for n in range(2, 2 + KT):
                hidden_high(1, n // 2, n % 2)
                weights_high(1, n // 2, n % 2)
                s.wait_ge(sem("down_added"), n - 1)
                act(dsq[:, n % 2, :], dy[:, n - 2, 0:HALF], SQ).then_inc(sem("down_sq"), 1)
            with s.Fori(1 + KT // 2, FT // 2) as i:
                for u in range(2):
                    hidden_high(1, i, u)
                    weights_high(1, i, u)
            s.wait_ge(sem("f_used"), 2 * FT + 2)
            for j in range(KT):
                s.wait_ge(sem("down_added"), KT + j + 1)
                act(dy[:, j, HALF:T], banks[j], CP)
                act(dsq[:, j % 2, :], banks[j], SQ).then_inc(sem("down_sq"), 1)
            root("down")
            s.dma_start(pw[:, :], pool_w[0]).then_inc(sem("pw_in"), 16)
            split_squares("h2", KT, h2, "g2_pre", dsq8)
            root("h2")

            for g in range(4):
                if g:
                    s.wait_ge(sem("pool_done"), g)
                    s.dma_start(pw[:, :], pool_w[g]).then_inc(sem("pw_in"), 16)
                s.wait_ge(g_free[1], T_P2 // 2 + g + 2)
                act(pgs[:, :], pgt[:, :], SIG).then_inc(sem("pg_sig"), 1)
            s.wait_ge(sem("kv_zero"), 1)
            s.wait_ge(g_free[0], T_P2 // 2 + 6)
            for kv in range(2):
                for h in range(2):
                    act(kd[h * CH:h * CH + CH, kv, P:], kk_f[kv * CH:kv * CH + CH, :], CP)
            s.wait_ge(sem("v2_tr"), 1)
            act(vt2[:, 1:, :], psb[:].rearrange("p a (b c) -> p (a b) c", c=P), CP).then_inc(sem("v2_ready"), 1)

            def load_bias(p):
                s.dma_start(ab[p % 2][:, :, :, :], att_bias[p]).then_inc(sem("ab_in"), 16)

            load_bias(0)

            for n in range(4 * PAIRS):
                p, st = n // 4, n % 4
                s.wait_ge(sem("am_ready"), n + 1)
                for q in range(4):
                    act(ap_[:, n % 2, q, :], ap_[:, n % 2, q, :], EXP, bias=sm[:, 8 + q:9 + q],
                        accum_out=sm[:, 16 + q:17 + q])
                act(sm[:, 12:16], sm[:, 12:16], EXP).then_inc(sem("ae_ready"), 1)
                if st == 0 and p + 1 < PAIRS:
                    if p:
                        s.wait_ge(sem("as_out"), 4 * p)
                    s.wait_ge(sem("ab_in"), 16 * p + 16)
                    load_bias(p + 1)
                if st == 0:
                    s.wait_ge(g_free[1], T_P2 // 2 + 7 + p)
                    act(gsig[:, :], cat[:, 4 + p, :], SIG).then_inc(sem("ag_sig"), 1)
                s.wait_ge(sem("apt_full"), n + 1)
                act(apt[:].rearrange("p a b c -> p (a b c)"), flat(psb), CP).then_inc(sem("apt_ready"), 1)
            s.wait_ge(sem("ao_out"), 17)
            high("cat", cat, xhi, KT)
            evacuate(T_O2, "fin", y2, q2sq)
            root("fin")
            for n, j in enumerate((1, 0, 3, 2, 5, 4, 6, 7)):
                if j in BY_POOL:
                    s.wait_ge(sem("y_pool"), BY_POOL.index(j) + 1)
                else:
                    s.wait_ge(sem("y_done"), n + 1 - sum(b in BY_POOL for b in (1, 0, 3, 2, 5, 4, 6, 7)[:n]))
                s.dma_start(out[:, j, :], y2[:, j, :]).then_inc(sem("stored"), 16)
            s.wait_ge(sem("stored"), 16 * KT)


def constants():
    i = np.arange(P)
    t, s = i[:, None], i[None, :]
    mats = np.zeros((NMAT + 1, P, P), np.float32)
    mats[M_ID] = np.eye(P)
    same = (t // CH) == (s // CH)
    mats[M_CENT] = np.eye(P) - same / CH
    mats[M_CENT_RET] = np.eye(P) - 1 / P
    mats[M_BLK] = same
    mats[M_STRICT] = same & (t < s)
    mats[M_INCL] = same & (t <= s)
    for lv in range(LEVELS):
        low = ((t >> (lv + 1)) == (s >> (lv + 1))) & ((t >> lv) % 2 == 1) & ((s >> lv) % 2 == 0)
        mats[M_LVL + lv] = -1.0 * low
        if lv == 0:
            mats[M_LOW0T] = -1.0 * low.T
    lg = np.log1p(-np.exp2(-5.0 - np.arange(8)))
    ret = np.zeros((PAIRS, P, 4, P), np.float32)
    cdec = np.zeros((P, PAIRS), np.float32)
    for p in range(PAIRS):
        for h in range(2):
            g = lg[2 * p + h]
            rel = s - t
            ret[p, :, h, :] = np.where(rel >= 0, np.exp(np.maximum(rel, 0) * g), 0) * 0.125
            rows = slice(h * CH, h * CH + CH)
            ret[p, rows, 2, :] = np.exp((i + 1.0) * g)[None, :]
            ret[p, rows, 3, :] = np.exp((P - 1.0 - i) * g)[None, :] * 0.125
            cdec[rows, p] = np.exp(P * g)
    slopes = np.exp2(-8.0 * np.arange(1, 9) / 8)
    q, k = np.arange(P)[:, None], np.arange(2 * P)[None, :]
    dist = q + P - k
    win = (dist >= 0) & (dist < P)
    bias = np.zeros((PAIRS, P, 2, 2, 2 * P), np.float32)
    for p in range(PAIRS):
        for h in range(2):
            b = -slopes[2 * p + h] * dist
            bias[p, :, 0, h, :] = np.where(win, b, NEG)
            bias[p, :, 1, h, :] = np.where(win & (k >= P), b, NEG)
    invf = (10000.0 ** (-np.arange(32, dtype=np.float64) / 32)).astype(np.float32)
    counts = np.ones((4, 15), np.float32)
    for g in range(4):
        w = 2 ** (g + 1)
        counts[g, :w - 1] = w / np.arange(1.0, w)
    tab = {"cdecay": cdec, "invf": invf[i % 32][:, None], "sgn": np.where(i % 64 < 32, -1.0, 1.0)[:, None],
           "counts": np.broadcast_to(counts.reshape(1, 60), (P, 60))}
    return mats.transpose(1, 0, 2), ret, bias, {k: v.astype(np.float32) for k, v in tab.items()}


def columns(vec):
    return vec.reshape(-1, P).T


def kernel(**inputs):
    import concourse.bacc as bacc
    from concourse.bass_utils import run_bass_kernel_spmd

    f = {k: np.asarray(v) for k, v in inputs.items()}
    mats, ret, bias, tab = constants()

    def blocks(wm):
        k, n = wm.shape
        b = wm.reshape(k // P, P, n // P, P).transpose(2, 1, 0, 3).reshape(n // P, P, k)
        if k < D:
            b = np.concatenate([b, np.zeros((n // P, P, D - k), wm.dtype)], axis=2)
        return b

    w_in = blocks(f["w_in"][0])
    rw, ret_w, gates = w_in[:14], w_in[14:38], w_in[38:]
    brw, bret, wout = blocks(f["w_branch_rw"][0]), blocks(f["w_branch_ret"][0]), blocks(f["w_out"][0])
    up = blocks(f["ffn_w_up"][0])
    down = f["ffn_w_down"][0].reshape(FT, P, D)
    in2, out2 = blocks(f["w_in_2"][0]), blocks(f["w_out_2"][0])
    low = np.zeros((PAIRS, P, D), np.float32)
    for p in range(PAIRS):
        c = slice(p * P, (p + 1) * P)
        low[p, 0:CH, 0:P] = f["rw_w2"][0][:, c]
        low[p, CH:P, P:2 * P] = f["rw_a2"][0][:, c]
        low[p, :, 2 * P:3 * P] = f["rw_g2"][0][:, c]
    order = [rw[12], rw[13]]
    later = []
    for p in range(PAIRS):
        later += [ret_w[p], ret_w[4 + p], ret_w[8 + 2 * p], ret_w[9 + 2 * p], ret_w[16 + 2 * p], ret_w[17 + 2 * p]]
    later += list(gates)
    for p in range(PAIRS):
        order += [rw[p], rw[4 + p], rw[8 + p], low[p]] + later[LATER * p:LATER * (p + 1)]
    order += list(brw) + list(bret)
    order += list(wout)
    for j in range(FT):
        order += [up[j], up[FT + j]]
    order += list(down)
    for g in range(4):
        order += [in2[g], in2[4 + g]]
    order += [in2[12], in2[13]]
    for p in range(PAIRS):
        order += [in2[8 + p], in2[14 + p]]
    order += list(out2)
    w = np.stack(order)
    assert w.shape[0] == NSTORED

    mu = columns(f["rw_mu"][0])
    vecs = [columns(f[n][0]) for n in ("rw_w0", "rw_a0", "rw_k_k", "rw_k_a", "rw_r_k", "rw_lnx_w", "rw_lnx_b")]
    cw, cb = f["ffn_conv_w"][0], f["ffn_conv_b"][0]
    cw = [columns(cw[n]) for n in range(3)] + [columns(cb)]
    table = {"g_mix_pre": columns(f["norm_mix_pre"][0]), "g_mix_post": columns(f["norm_mix_post"][0]),
             "g_ffn_pre": columns(f["norm_ffn_pre"][0]), "g_ffn_post": columns(f["norm_ffn_post"][0]),
             "g2_pre": columns(f["norm_pre_2"][0]), "g2_post": columns(f["norm_post_2"][0]),
             "mu_low": mu[:, 12:14],
             "rw": np.concatenate([np.stack([mu[:, p], mu[:, 4 + p], mu[:, 8 + p]] + [v[:, p] for v in vecs], axis=1)
                                   for p in range(PAIRS)], axis=1),
             "conv": np.concatenate([np.stack([c[:, j + o] for o in (0, FT) for c in cw], axis=1)
                                     for j in range(FT)], axis=1),
             "pscale": columns(f["pool_scale_2"][0]),
             "sinks": np.broadcast_to(f["attn_sinks_2"][0][None, :], (P, 8))}
    table.update(tab)
    par = np.concatenate([table[n] for n in COLS], axis=1)

    def feature_major(x):
        return x.T.reshape(KT, P, T).transpose(1, 0, 2)

    given = {"xt": feature_major(f["x"][0]), "pos": np.broadcast_to(f["positions"], (P, T)), "w": w, "par": par,
             "mats": mats, "ret_tab": ret, "att_bias": bias, "pool_w": f["pool_w_2"][0]}
    nc = bacc.Bacc("TRN2", target_bir_lowering=False, num_devices=1)
    arrays, args = {}, []
    for name, a in given.items():
        a = np.ascontiguousarray(a)
        arrays[name] = a
        args.append(nc.dram_tensor(name, a.shape, mybir.dt.from_np(a.dtype), kind="ExternalInput").ap())
    args.append(nc.dram_tensor("out", (P, KT, T), F32, kind="ExternalOutput").ap())
    build(nc, *args)
    r = run_bass_kernel_spmd(nc, [arrays], core_ids=[0])
    return r.results[0]["out"].transpose(1, 0, 2).reshape(D, T).T.reshape(1, T, D)
```
